# Optimizing a Trainium2 kernel written in Bass

```python
import math
import jax
import jax.numpy as jnp
from jax import lax
import numpy as np

D_MODEL = 1024
BATCH = 1
SEQ = 512
DEPTH = 1
DEC_BATCH = 8
DEC_SEQ = 16
PAST_LEN = 256

CHUNK = 64
GDN_HEADS = 4
GDN_DK = 128
GDN_DV = 128
CONV_W = 4
SWA_HEADS = 8
SWA_KV_HEADS = 2
SWA_GROUP = SWA_HEADS // SWA_KV_HEADS
SWA_HD = 64
WINDOW = 128
WIN_CHUNKS = WINDOW // CHUNK
N_MEM = 256
XA_HEADS = 4
XA_HD = 128
D_FF = 4 * D_MODEL
N_BRANCH = 3
BRANCH_W = 512
DN_ALPHA = (2.0 * DEPTH) ** 0.25
DN_BETA = (8.0 * DEPTH) ** -0.25
LN_EPS = 1e-5
NORM_EPS = 1e-6

GDN_QK = GDN_HEADS * GDN_DK
GDN_V = GDN_HEADS * GDN_DV
GDN_CONV_CH = 2 * GDN_QK + GDN_V
SWA_Q = SWA_HEADS * SWA_HD
SWA_KV = SWA_KV_HEADS * SWA_HD
XA_Q = XA_HEADS * XA_HD
IN_SPLITS = (GDN_CONV_CH, GDN_HEADS, GDN_HEADS, GDN_V, SWA_Q, SWA_KV, SWA_KV, XA_Q, N_BRANCH * D_MODEL)
D_IN = sum(IN_SPLITS)

kernel_name = 'hybrid_gdn_swa_memxattn_stream_step'

def layer_norm(x, g, b):
    xf = x.astype(jnp.float32)
    mu = jnp.mean(xf, axis=-1, keepdims=True)
    var = jnp.mean(jnp.square(xf - mu), axis=-1, keepdims=True)
    y = (xf - mu) * lax.rsqrt(var + LN_EPS) * g.astype(jnp.float32) + b.astype(jnp.float32)
    return y.astype(x.dtype)

def l2_normalize(x):
    return x * lax.rsqrt(jnp.sum(jnp.square(x), axis=-1, keepdims=True) + NORM_EPS)

def split_in(h):
    offsets = np.cumsum(IN_SPLITS)[:-1].tolist()
    return jnp.split(h, offsets, axis=-1)

def gated_delta_chunked(q, k, v, g, beta, s0):
    B, T, H, DK = q.shape
    DV = v.shape[-1]
    C = min(CHUNK, T)
    N = T // C

    def chunks(t):
        return jnp.transpose(t.reshape(B, N, C, H, t.shape[-1]), (1, 0, 3, 2, 4))

    qc, kc, vc = chunks(q), chunks(k), chunks(v)
    gc = jnp.cumsum(chunks(g[..., None])[..., 0], axis=-1)
    bc = chunks(beta[..., None])
    causal = jnp.tril(jnp.ones((C, C), dtype=bool))
    strict = jnp.tril(jnp.ones((C, C), dtype=bool), -1)
    decay = jnp.exp(jnp.where(causal, gc[..., :, None] - gc[..., None, :], -jnp.inf))
    kb = kc * bc
    a_mat = jnp.where(strict, jnp.einsum('nbhid,nbhjd->nbhij', kb, kc) * decay, 0.0) + jnp.eye(C, dtype=jnp.float32)
    u = lax.linalg.triangular_solve(a_mat, vc * bc, left_side=True, lower=True, unit_diagonal=True)
    w = lax.linalg.triangular_solve(a_mat, kb * jnp.exp(gc)[..., None], left_side=True, lower=True, unit_diagonal=True)
    qk = jnp.einsum('nbhid,nbhjd->nbhij', qc, kc) * decay

    def step(s, inp):
        q_i, k_i, u_i, w_i, qk_i, g_i = inp
        v_new = u_i - jnp.einsum('bhcd,bhde->bhce', w_i, s)
        o_i = (jnp.einsum('bhcd,bhde->bhce', q_i * jnp.exp(g_i)[..., None], s)
               + jnp.einsum('bhij,bhje->bhie', qk_i, v_new))
        g_last = g_i[..., -1:]
        s = (s * jnp.exp(g_last)[..., None]
             + jnp.einsum('bhcd,bhce->bhde', k_i * jnp.exp(g_last - g_i)[..., None], v_new))
        return s, o_i

    s_final, o = lax.scan(step, s0, (qc, kc, u, w, qk, gc))
    o = jnp.transpose(o, (1, 0, 3, 2, 4)).reshape(B, T, H, DV)
    return o, s_final

def gdn_branch(qkv, a, b, z, conv_buf, s0, conv_w, a_log, dt_bias, norm_w):
    B, T, _ = qkv.shape
    xin = jnp.concatenate([conv_buf.astype(qkv.dtype), qkv], axis=1)
    conv = lax.conv_general_dilated(xin, conv_w.astype(xin.dtype)[:, None, :], window_strides=(1,), padding='VALID',
                                    dimension_numbers=('NWC', 'WIO', 'NWC'), feature_group_count=GDN_CONV_CH)
    conv = jax.nn.silu(conv.astype(jnp.float32))
    q, k, v = jnp.split(conv, [GDN_QK, 2 * GDN_QK], axis=-1)
    q = l2_normalize(q.reshape(B, T, GDN_HEADS, GDN_DK)) * (GDN_DK ** -0.5)
    k = l2_normalize(k.reshape(B, T, GDN_HEADS, GDN_DK))
    v = v.reshape(B, T, GDN_HEADS, GDN_DV)
    g = -jnp.exp(a_log.astype(jnp.float32)) * jax.nn.softplus(a.astype(jnp.float32) + dt_bias.astype(jnp.float32))
    beta = jax.nn.sigmoid(b.astype(jnp.float32))
    o, s_final = gated_delta_chunked(q, k, v, g, beta, s0.astype(jnp.float32))
    o = o * lax.rsqrt(jnp.mean(jnp.square(o), axis=-1, keepdims=True) + NORM_EPS) * norm_w.astype(jnp.float32)
    o = o * jax.nn.silu(z.reshape(B, T, GDN_HEADS, GDN_DV).astype(jnp.float32))
    return o.reshape(B, T, GDN_V).astype(qkv.dtype), xin[:, -(CONV_W - 1):], s_final.astype(qkv.dtype)

def sink_attention(q, k, v, valid, sinks):
    s = jnp.einsum('...qkgd,...skd->...kgqs', q, k, preferred_element_type=jnp.float32) * (SWA_HD ** -0.5)
    s = jnp.where(valid, s, -jnp.inf)
    sink = jnp.broadcast_to(sinks.astype(jnp.float32).reshape(SWA_KV_HEADS, SWA_GROUP, 1, 1), s.shape[:-1] + (1,))
    p = jax.nn.softmax(jnp.concatenate([s, sink], axis=-1), axis=-1)[..., :-1]
    return jnp.einsum('...kgqs,...skd->...qkgd', p.astype(v.dtype), v)

def swa_prompt(q, k, v, sinks):
    B, T = q.shape[0], q.shape[1]
    nc = T // CHUNK
    pad = ((0, 0), (WIN_CHUNKS * CHUNK, 0), (0, 0), (0, 0))

    def band(t):
        tp = jnp.pad(t, pad).reshape(B, nc + WIN_CHUNKS, CHUNK, SWA_KV_HEADS, SWA_HD)
        return jnp.concatenate([tp[:, j:j + nc] for j in range(WIN_CHUNKS + 1)], axis=2)

    kb, vb = band(k), band(v)
    qb = q.reshape(B, nc, CHUNK, SWA_KV_HEADS, SWA_GROUP, SWA_HD)
    key_chunk = jnp.arange(nc)[:, None] - WIN_CHUNKS + jnp.arange((WIN_CHUNKS + 1) * CHUNK)[None, :] // CHUNK
    valid = (key_chunk >= 0)[:, None, None, None, :]
    o = sink_attention(qb, kb, vb, valid, sinks)
    return o.reshape(B, T, SWA_Q)

def swa_sample(q, k, v, ck, cv, sinks):
    B, T = q.shape[0], q.shape[1]
    n_keep = ck.shape[1]
    kk = jnp.concatenate([ck.astype(k.dtype), k], axis=1)
    vv = jnp.concatenate([cv.astype(v.dtype), v], axis=1)
    q_pos = PAST_LEN + jnp.arange(T)
    k_pos = jnp.concatenate([PAST_LEN - n_keep + jnp.arange(n_keep), q_pos])
    qc = (q_pos // CHUNK)[:, None]
    kc = (k_pos // CHUNK)[None, :]
    valid = (kc <= qc) & (kc >= qc - WIN_CHUNKS)
    o = sink_attention(q, kk, vv, valid, sinks)
    return o.reshape(B, T, SWA_Q), kk[:, -n_keep:], vv[:, -n_keep:]

def mem_kv(mem, w):
    B, M, _ = mem.shape
    mk, mv = jnp.split(mem @ w, 2, axis=-1)
    return mk.reshape(B, M, XA_HEADS, XA_HD), mv.reshape(B, M, XA_HEADS, XA_HD)

def mem_attention(q, mk, mv):
    B, T = q.shape[0], q.shape[1]
    s = jnp.einsum('bthd,bshd->bhts', q, mk.astype(q.dtype), preferred_element_type=jnp.float32) * (XA_HD ** -0.5)
    p = jax.nn.softmax(s, axis=-1)
    o = jnp.einsum('bhts,bshd->bthd', p.astype(q.dtype), mv.astype(q.dtype))
    return o.reshape(B, T, XA_Q)

def merge_and_channel_mix(x, branches, gate_pre, w_branch, w_o, ln1_g, ln1_b, w_up, w_down, ln2_g, ln2_b):
    gates = jnp.split(jax.nn.sigmoid(gate_pre.astype(jnp.float32)).astype(x.dtype), N_BRANCH, axis=-1)
    merged = gates[0] * (branches[0] @ w_branch[0])
    for i in range(1, N_BRANCH):
        merged = merged + gates[i] * (branches[i] @ w_branch[i])
    x = layer_norm(DN_ALPHA * x + merged @ w_o, ln1_g, ln1_b)
    hidden = jnp.square(jax.nn.relu(x @ w_up))
    return layer_norm(DN_ALPHA * x + hidden @ w_down, ln2_g, ln2_b)

def setup_inputs(seed: int = 0) -> dict:
    key = jax.random.key(seed)
    ks = jax.random.split(key, 24)
    f32 = jnp.float32
    n_keep = min(WINDOW, PAST_LEN)

    def nrm(k, shape, scale=1.0):
        return jax.random.normal(k, shape, f32) * scale

    dt = jnp.exp(jax.random.uniform(ks[10], (DEPTH, GDN_HEADS), f32, minval=math.log(1e-3), maxval=math.log(1e-1)))
    return {
        'x_prompt': nrm(ks[0], (BATCH, SEQ, D_MODEL)),
        'x_sample': nrm(ks[1], (DEC_BATCH, DEC_SEQ, D_MODEL)),
        'state_gdn_s': nrm(ks[2], (DEPTH, DEC_BATCH, GDN_HEADS, GDN_DK, GDN_DV), 0.5),
        'state_gdn_conv': nrm(ks[3], (DEPTH, DEC_BATCH, CONV_W - 1, GDN_CONV_CH)),
        'cache_swa_k': nrm(ks[4], (DEPTH, DEC_BATCH, n_keep, SWA_KV_HEADS, SWA_HD)),
        'cache_swa_v': nrm(ks[5], (DEPTH, DEC_BATCH, n_keep, SWA_KV_HEADS, SWA_HD)),
        'cache_mem_k': nrm(ks[6], (DEPTH, DEC_BATCH, N_MEM, XA_HEADS, XA_HD)),
        'cache_mem_v': nrm(ks[7], (DEPTH, DEC_BATCH, N_MEM, XA_HEADS, XA_HD)),
        'mem_prompt': nrm(ks[8], (BATCH, N_MEM, D_MODEL)),
        'w_in': nrm(ks[9], (DEPTH, D_MODEL, D_IN), D_MODEL ** -0.5),
        'conv_w': nrm(ks[11], (DEPTH, CONV_W, GDN_CONV_CH), CONV_W ** -0.5),
        'a_log': jnp.log(jax.random.uniform(ks[12], (DEPTH, GDN_HEADS), f32, minval=1.0, maxval=16.0)),
        'dt_bias': dt + jnp.log(-jnp.expm1(-dt)),
        'gdn_norm_w': 1.0 + nrm(ks[13], (DEPTH, GDN_DV), 0.02),
        'attn_sinks': nrm(ks[14], (DEPTH, SWA_HEADS), 0.5),
        'w_mem_kv': nrm(ks[15], (DEPTH, D_MODEL, 2 * XA_Q), D_MODEL ** -0.5),
        'w_branch': nrm(ks[16], (DEPTH, N_BRANCH, BRANCH_W, D_MODEL), BRANCH_W ** -0.5),
        'w_o': nrm(ks[17], (DEPTH, D_MODEL, D_MODEL), DN_BETA * D_MODEL ** -0.5),
        'ln1_g': 1.0 + nrm(ks[18], (DEPTH, D_MODEL), 0.02),
        'ln1_b': nrm(ks[19], (DEPTH, D_MODEL), 0.02),
        'w_up': nrm(ks[20], (DEPTH, D_MODEL, D_FF), D_MODEL ** -0.5),
        'w_down': nrm(ks[21], (DEPTH, D_FF, D_MODEL), DN_BETA * D_FF ** -0.5),
        'ln2_g': 1.0 + nrm(ks[22], (DEPTH, D_MODEL), 0.02),
        'ln2_b': nrm(ks[23], (DEPTH, D_MODEL), 0.02),
    }

def reference(x_prompt, x_sample, state_gdn_s, state_gdn_conv, cache_swa_k, cache_swa_v, cache_mem_k, cache_mem_v,
              mem_prompt, w_in, conv_w, a_log, dt_bias, gdn_norm_w, attn_sinks, w_mem_kv, w_branch, w_o,
              ln1_g, ln1_b, w_up, w_down, ln2_g, ln2_b):
    n_keep = cache_swa_k.shape[2]

    x = x_prompt
    B, T, _ = x.shape
    p_s, p_conv, p_k, p_v, p_mk, p_mv = [], [], [], [], [], []
    for l in range(DEPTH):
        qkv, a, b, z, q_s, k_s, v_s, q_x, gate_pre = split_in(x @ w_in[l])
        conv0 = jnp.zeros((B, CONV_W - 1, GDN_CONV_CH), x.dtype)
        s0 = jnp.zeros((B, GDN_HEADS, GDN_DK, GDN_DV), jnp.float32)
        o_g, conv_new, s_new = gdn_branch(qkv, a, b, z, conv0, s0, conv_w[l], a_log[l], dt_bias[l], gdn_norm_w[l])
        k_s = k_s.reshape(B, T, SWA_KV_HEADS, SWA_HD)
        v_s = v_s.reshape(B, T, SWA_KV_HEADS, SWA_HD)
        o_s = swa_prompt(q_s.reshape(B, T, SWA_KV_HEADS, SWA_GROUP, SWA_HD), k_s, v_s, attn_sinks[l])
        mk, mv = mem_kv(mem_prompt, w_mem_kv[l])
        o_x = mem_attention(q_x.reshape(B, T, XA_HEADS, XA_HD), mk, mv)
        x = merge_and_channel_mix(x, (o_g, o_s, o_x), gate_pre, w_branch[l], w_o[l], ln1_g[l], ln1_b[l],
                                  w_up[l], w_down[l], ln2_g[l], ln2_b[l])
        p_s.append(s_new)
        p_conv.append(conv_new)
        p_k.append(k_s[:, T - n_keep:])
        p_v.append(v_s[:, T - n_keep:])
        p_mk.append(mk)
        p_mv.append(mv)
    y_prompt = x

    x = x_sample
    B, T, _ = x.shape
    s_s, s_conv, s_k, s_v = [], [], [], []
    for l in range(DEPTH):
        qkv, a, b, z, q_s, k_s, v_s, q_x, gate_pre = split_in(x @ w_in[l])
        o_g, conv_new, s_new = gdn_branch(qkv, a, b, z, state_gdn_conv[l], state_gdn_s[l], conv_w[l], a_log[l],
                                          dt_bias[l], gdn_norm_w[l])
        o_s, k_buf, v_buf = swa_sample(q_s.reshape(B, T, SWA_KV_HEADS, SWA_GROUP, SWA_HD),
                                       k_s.reshape(B, T, SWA_KV_HEADS, SWA_HD), v_s.reshape(B, T, SWA_KV_HEADS, SWA_HD),
                                       cache_swa_k[l], cache_swa_v[l], attn_sinks[l])
        o_x = mem_attention(q_x.reshape(B, T, XA_HEADS, XA_HD), cache_mem_k[l], cache_mem_v[l])
        x = merge_and_channel_mix(x, (o_g, o_s, o_x), gate_pre, w_branch[l], w_o[l], ln1_g[l], ln1_b[l],
                                  w_up[l], w_down[l], ln2_g[l], ln2_b[l])
        s_s.append(s_new)
        s_conv.append(conv_new)
        s_k.append(k_buf)
        s_v.append(v_buf)
    y_sample = x

    return (y_prompt, y_sample,
            jnp.stack(p_s), jnp.stack(p_conv), jnp.stack(p_k), jnp.stack(p_v), jnp.stack(p_mk), jnp.stack(p_mv),
            jnp.stack(s_s), jnp.stack(s_conv), jnp.stack(s_k), jnp.stack(s_v))


_drawn_inputs = setup_inputs


def setup_inputs(seed=0):
    import zlib

    import numpy as np

    out = dict(_drawn_inputs(seed))
    spreads = {}
    factors = {'gdn_norm_w': 25.838,
     'attn_sinks': 49.072,
     'ln1_g': 2.764,
     'ln1_b': 2.701,
     'ln2_g': 7.909,
     'ln2_b': 8.19,
     'cache_mem_k': 3.628,
     'cache_mem_v': 2.849}
    for name, (base, spread) in spreads.items():
        noise = np.random.default_rng([zlib.crc32(name.encode()), seed]).standard_normal(out[name].shape)
        drawn = base * np.exp(spread * noise) if base else spread * noise
        out[name] = jnp.asarray(drawn.astype(out[name].dtype))
    for name, factor in factors.items():
        out[name] = (out[name] * factor).astype(out[name].dtype)
    return out
```

```python
from contextlib import ExitStack

import numpy as np
import concourse.bass as bass
from concourse import mybir

F32 = mybir.dt.float32
ALU = mybir.AluOpType
ACT = mybir.ActivationFunctionType
AX = mybir.AxisListType

P = 128
DM = 1024
KT = DM // P
NP = 512
NB = 8
ST = 16
TOK = NP + NB * ST
TT = TOK // P
H = 4
PAD = 3
SPAN = ST + PAD
QW = NP + PAD + NB * SPAN
CW = QW - PAD
HT = 14
DFF = 4096
FT = DFF // P
ALPHA = float(2.0 ** 0.25)
NEG = -1.0e30
BLK = 16

CONST_COLS = {}
_at = 0
for _name, _n in (("ident", P), ("ones", P), ("mean", P), ("cum_p", P), ("cum_s", P), ("neg_p", P), ("neg_s", P),
                  ("nstrict_p", P), ("nstrict_s", P), ("blk_s", P), ("bd16", P), ("off16", P), ("off32", P),
                  ("off64", P), ("win0", 256), ("win", 256), ("snew", 240), ("tokblk", NB)):
    CONST_COLS[_name] = (_at, _n)
    _at += _n
NCONST = _at


def shape_constants():
    c = np.zeros((P, NCONST), np.float32)
    j, i = np.arange(P)[:, None], np.arange(P)[None, :]
    same = (j // ST) == (i // ST)

    def put(name, v):
        a, n = CONST_COLS[name]
        c[:, a:a + n] = v

    put("ident", j == i)
    put("ones", 1.0)
    put("mean", 1.0 / P)
    put("cum_p", j <= i)
    put("cum_s", (j <= i) & same)
    put("neg_p", np.where(j <= i, 0.0, NEG))
    put("neg_s", np.where((j <= i) & same, 0.0, NEG))
    put("nstrict_p", np.where(j < i, -1.0, 0.0))
    put("nstrict_s", np.where((j < i) & same, -1.0, 0.0))
    put("blk_s", same)
    put("bd16", (j // BLK) == (i // BLK))
    for s in (16, 32, 64):
        put(f"off{s}", (j // (2 * s) == i // (2 * s)) & (j // s % 2 == 0) & (i // s % 2 == 1))
    row, key = np.arange(P)[:, None] // 64, np.arange(256)[None, :] // 64
    put("win0", np.where(key <= row, 0.0, NEG))
    put("win", np.where((key <= row + 2) & (key >= row), 0.0, NEG))
    x = np.arange(240)[None, :]
    put("snew", np.where((x >= 112) & (x < 128), 0.0, NEG))
    put("tokblk", np.arange(P)[:, None] // ST == np.arange(NB)[None, :])
    return c



def level_count(stage, level, t):
    if stage in ("y", "off"):
        return (TT - 1) * (level - 4) + t
    return TT * (level - 1) + t if level < 4 else 3 * TT + (TT - 1) * (level - 4) + t


ROUNDS = [("norm", _n) for _n in range(16)] + [("gcol", 0)]
for _t in range(TT):
    ROUNDS += [(_x, _t) for _x in ("qk", "grow", "brow", "ktr", "vtr")] + ([("kk", _t - 1)] if _t else [])
ROUNDS += [("kk", TT - 1)] + [("ntr", _t) for _t in range(TT)]
for _l in range(1, 7):
    for _x in ("p", "pt", "x", "xt") if _l < 4 else ("y", "x", "xt"):
        ROUNDS += [(_x, level_count(_x, _l, _t)) for _t in range(TT if _l < 4 else TT - 1)
                   if (_x, _l) not in (("pt", 3), ("x", 6))]
for _t in range(4):
    ROUNDS += [("ks", _t), ("vn", _t), ("go", _t), ("ds", _t)]
ROUNDS += [("kst", 0), ("ks", 4), ("vn", 4), ("go", 4)] + [("ss", _n) for _n in range(8)]
ROUNDS += [("on", _n) for _n in range(8)]
ROUND = {r: _n for _n, r in enumerate(ROUNDS)}


def build(nc, xT, memT, w_h, w_ab, w_mem, w_mix, w_o, w_up, w_down, conv_w, conv_s, dt_b, a_log, norm_w,
          sinks, sinks_row, ln1, ln2, s0, ckT, cvT, cv, cmkT, cmv, consts,
          o_y, o_ps, o_pconv, o_pk, o_pv, o_pm, o_ss, o_sconv, o_skT, o_svT):
    with ExitStack() as ctx:
        def sb(name, cols):
            return ctx.enter_context(nc.sbuf_tensor(name, [P, cols], F32))

        semaphores = {}

        def sem(name):
            if name not in semaphores:
                semaphores[name] = ctx.enter_context(nc.semaphore(name))
            return semaphores[name]

        cst = sb("cst", NCONST)

        def const(name):
            a, n = CONST_COLS[name]
            return cst[:, a:a + n]

        ident = const("ident")
        x_sb = sb("x_sb", KT * TOK)
        x3 = x_sb[:, :].rearrange("p (k t) -> p k t", k=KT)
        arena = sb("arena", HT * TOK + 12 * TOK + 12 * QW)
        h_sb = arena[:, 0:HT * TOK]
        h3 = h_sb.rearrange("p (k t) -> p k t", k=HT)
        Q0 = HT * TOK
        qkv3 = arena[:, Q0:Q0 + 12 * TOK].rearrange("p (k t) -> p k t", k=12)
        P0 = Q0 + 12 * TOK
        pad3 = arena[:, P0:P0 + 12 * QW].rearrange("p (k t) -> p k t", k=12)
        work = sb("work", 4 * 2560 + 4096)
        ring = sb("ring", 4 * 1024)
        small = sb("small", 1120)

        def tiles(ap):
            return ap.rearrange("p (t h x) -> p t h x", h=H, x=P)

        NT = tiles(arena[:, P0:P0 + 2560])
        X = tiles(arena[:, P0 + 2560:P0 + 5120])
        XT = tiles(arena[:, P0 + 5120:P0 + 7680])
        PW = tiles(arena[:, Q0 + 8 * TOK:Q0 + 12 * TOK])
        PWT = tiles(work[:, 0:2560])
        KD = tiles(work[:, 2560:5120])
        VB = tiles(work[:, 5120:7680])
        QKD = tiles(work[:, 7680:10240])
        S0 = work[:, 10240:14336].rearrange("p (h b v) -> p h b v", h=H, b=NB)

        def heads(ap):
            return ap.rearrange("p (h x) -> p h x", h=H)

        conv_acc = [ring[:, 2048:2048 + CW], ring[:, 3072:3072 + CW]]
        conv_acc_streams = [a[:, NP + PAD:NP + PAD + NB * SPAN].rearrange("p (b s) -> p b s", b=NB)[:, :, 0:ST]
                            for a in (ring[:, 2048:3072], ring[:, 3072:4096])]
        rn_o = [work[:, 2560 + TOK * i:2560 + TOK * (i + 1)] for i in range(2)]
        sq = [ring[:, 0:TOK], ring[:, 1024:1024 + TOK]]
        rn = [ring[:, 2048:2048 + TOK], ring[:, 3072:3072 + TOK]]
        d_sb = [heads(ring[:, 0:512]), heads(ring[:, 512:1024])]
        eg_sb = [heads(ring[:, 1024:1536]), heads(ring[:, 1536:2048])]
        KB, DEC = X, XT
        S = heads(ring[:, 3072:3584])
        r_sb = heads(ring[:, 3584:4096])
        vn_sb = d_sb[0]
        kst_sb = d_sb[1]
        vm_sb = [ring[:, 1024:2048].rearrange("p (b x) -> p b x", b=NB),
                 ring[:, 2048:3072].rearrange("p (b x) -> p b x", b=NB)]

        taken = [0]

        def sm(n, **shape):
            a = taken[0]
            taken[0] += n
            assert taken[0] <= 1120
            ap = small[:, a:a + n]
            return ap.rearrange(f"p ({' '.join(shape)} x) -> p {' '.join(shape)} x", **shape) if shape else ap

        dtb, alog, nea = sm(4), sm(4), sm(4)
        nrm = sm(1)
        sinkb, sinkc, nsinkb, nsinkc = sm(8), sm(1), sm(8), sm(1)
        cw_sb = sm(48)
        ln1c = sm(16)
        cs_in, cs_out = sm(288), sm(288)
        ab = sm(40, t=TT)
        t_a, t_b, t_c, g_tok = (sm(20, t=TT) for _ in range(4))
        beta, e_b, glc, kdec, nbeg = (sm(20, t=TT) for _ in range(5))
        gcl = sm(40, t=TT)
        egl = sm(16, t=4)
        egs = sm(32, h=H)
        wab = sm(64, k=KT)
        eps = sm(1)
        nm, den, es, rden = ([sm(2) for _ in range(2)] for _ in range(4))
        stats, mv, rstd, nmr = (list(x) for x in zip(*[(sm(12), sm(2), sm(1), sm(1)) for _ in range(2)]))

        psum = ctx.enter_context(nc.psum_tensor("psum", [P, 4096], F32))
        ps = [psum[:, 512 * i:512 * i + 512] for i in range(8)]
        sc_ps = [psum[:, 1024 * i:1024 * i + 1024].rearrange("p (u s) -> p u s", u=2)[:, :, 0:256] for i in range(2)]

        W_Q, W_K, W_V, M_Q = 4, 8, 9, 10
        oG = qkv3[:, 0:4, :]
        oS = arena[:, P0:P0 + 2560].rearrange("p (m t) -> p m t", m=H)
        oX = arena[:, P0 + 2560:P0 + 5120].rearrange("p (m t) -> p m t", m=H)
        vtok = arena[:, P0 + 5120:P0 + 5760].rearrange("p (t x) -> p t x", t=TT)
        mkv = arena[:, P0 + 5760:P0 + 7808].rearrange("p (s x) -> p s x", s=2)
        mkT = work[:, 0:1024].rearrange("p (h s) -> p h s", h=H)
        ck_sb = work[:, 1024:2048].rearrange("p (b s) -> p b s", b=NB)
        cv_sb = work[:, 2048:3072].rearrange("p (b s) -> p b s", b=NB)
        sm_sb = [work[:, 3072 + 512 * i:3584 + 512 * i].rearrange("p (u s) -> p u s", u=2) for i in range(2)]
        pT_sb = [work[:, 4096 + 512 * i:4608 + 512 * i].rearrange("p (u s q) -> p u s q", u=2, s=2)
                 for i in range(2)]
        qs_sb = work[:, 5120:5632].rearrange("p (b m t) -> p b m t", b=NB, m=4)
        mem_sb = work[:, 6144:8192].rearrange("p (k t) -> p k t", k=KT)
        cm = [work[:, 6144 + 4096 * i:10240 + 4096 * i].rearrange("p (e w x) -> p e w x", e=2, w=2)
              for i in range(2)]

        MIXN = 36 * P
        mixw = [work[:, i * MIXN:(i + 1) * MIXN] for i in range(2)]
        merged = arena[:, 0:KT * TOK].rearrange("p (k t) -> p k t", k=KT)
        sg = [arena[:, P0 + 5120 + TOK * i:P0 + 5120 + TOK * (i + 1)] for i in range(2)]
        gated = [arena[:, P0 + 6400 + TOK * i:P0 + 6400 + TOK * (i + 1)] for i in range(2)]
        colw = [ring[:, 2048:3072], ring[:, 3072:4096]]
        hid = arena[:, 0:FT * TOK].rearrange("p (k t) -> p k t", k=FT)
        relu = [arena[:, FT * TOK + TOK * i:FT * TOK + TOK * (i + 1)] for i in range(2)]
        downw = [work[:, 4096 * i:4096 * (i + 1)] for i in range(2)]
        xn = [work[:, 8192 + 1024 * i:9216 + 1024 * i] for i in range(2)]
        ln2gb = work[:, 10240:12288]

        block = ctx.enter_context(nc.Block())

        UNITS = ([("wp", t, m) for t in range(4) for m in range(4)] + [("ws", 0, p) for p in range(4)]
                 + [u for t in range(4) for u in (("mp", t, 0), ("mp", t, 1), ("ms", 0, t))])
        NU = len(UNITS)
        W_SCALE, M_SCALE = 64 ** -0.5, P ** -0.5

        def cols(ap3, c, n=TOK):
            return ap3[:, bass.ds(c * n, n)]

        def stream(ap):
            return ap[:, NP:TOK].rearrange("p (b s) -> p b s", b=NB)

        def padded(row):
            return row[:, PAD:PAD + NP], row[:, PAD + NP:QW].rearrange("p (b s) -> p b s", b=NB)[:, :, PAD:]

        def wtile(w, n):
            return w[bass.ds(n, 1), :, :].rearrange("a p x -> (a p) x")

        @block.sync
        def _(sp):
            def load(dst, src, name):
                sp.dma_start(dst, src).then_inc(sem(name), 16)

            load(x_sb[:, :], xT, "x_in")
            load(wab.rearrange("p k x -> p (k x)"), w_ab, "ab_in")
            for s in range(2):
                load(ring[:, s * 1024:(s + 1) * 1024], w_h[s], f"w{s}_in")
            load(cst[:, :], consts, "cst_in")
            for dst, src in ((dtb, dt_b.to_broadcast([P, 4])), (alog, a_log.to_broadcast([P, 4])), (nrm, norm_w),
                             (cw_sb, conv_w), (ln1c, ln1), (sinkb, sinks_row.to_broadcast([P, 8])),
                             (sinkc, sinks), (cs_in, conv_s)):
                load(dst, src, "par_in")
            load(S0.rearrange("p h b v -> p (h b v)"), s0, "s0_in")
            with sp.Fori(1, 13) as i:
                for s in range(2):
                    sp.wait_ge(sem("h_mm"), 2 * i - 1 + s)
                    load(ring[:, s * 1024:(s + 1) * 1024], wtile(w_h, 2 * i + s), f"w{s}_in")
            sp.wait_ge(sem("cs_out"), 1)
            sp.dma_start(o_pconv, pad3[:, :, NP:NP + PAD]).then_inc(sem("conv_st"), 16)
            sp.dma_start(o_sconv, cs_out).then_inc(sem("conv_st"), 16)
            sp.wait_ge(sem("h_out_v"), 13)
            sp.wait_ge(sem("h_out_a"), 13)
            for out, c in ((o_pk, W_K), (o_pv, W_V)):
                sp.dma_start(out, h3[:, c, NP - P:NP]).then_inc(sem("out_st"), 16)
            for out, old, c in ((o_skT, ckT, W_K), (o_svT, cvT, W_V)):
                sp.dma_start(out[:, :, P - ST:], stream(h3[:, c, :])).then_inc(sem("out_st"), 16)
                sp.dma_start(out[:, :, 0:P - ST], old[:, :, ST:]).then_inc(sem("out_st"), 16)
            sp.wait_ge(sem("ds_out"), 4)
            sp.dma_start(o_ps, S.rearrange("p h x -> p (h x)")).then_inc(sem("ps_st"), 16)
            for n in range(8):
                sp.wait_ge(sem("ss_out"), n + 1)
                h, b = n // 2, n % 2 * 4
                sp.dma_start(o_ss[:, (h * NB + b) * P:(h * NB + b + 4) * P],
                             S0[:, h, b:b + 4, :].rearrange("p b v -> p (b v)")).then_inc(sem("ss_st"), 16)
            sp.wait_ge(sem("gdn_end"), 1)
            sp.wait_ge(sem("ss_st"), 16 * 8)
            sp.wait_ge(sem("ps_st"), 16)
            load(mem_sb.rearrange("p k t -> p (k t)"), memT, "mem_in")
            load(ck_sb, ckT, "ck_in")
            load(cv_sb, cv, "ck_in")
            for k in range(KT):
                if k >= 4:
                    sp.wait_ge(sem("mem_mm"), k - 3)
                load(ring[:, (k % 4) * 1024:(k % 4 + 1) * 1024], w_mem[k], f"wm{k % 4}_in")
            sp.wait_ge(sem("mkv_out_v"), 2)
            sp.wait_ge(sem("mkv_out_a"), 2)
            sp.dma_start(o_pm, mkv).then_inc(sem("pm_st"), 16)
            for p in range(4):
                if p == 0:
                    sp.wait_ge(sem("mem_mm"), KT)
                if p >= 2:
                    sp.wait_ge(sem("pv_mm"), UNITS.index(("ms", 0, p - 2)) + 1)
                for e in range(2):
                    load(cm[p % 2][:, e, 0, :], cmkT[2 * p + e], f"cm{p % 2}_in")
                    load(cm[p % 2][:, e, 1, :], cmv[2 * p + e], f"cm{p % 2}_in")
            for s in range(2):
                load(colw[s], w_o[s], f"o{s}_in")
            sp.wait_ge(sem("pv_mm"), NU)
            for s in range(2):
                load(mixw[s], w_mix[s], f"x{s}_in")
            with sp.Fori(1, 4) as i:
                for s in range(2):
                    sp.wait_ge(sem("gate_mm"), 6 * i - 3 + 3 * s)
                    load(mixw[s], wtile(w_mix, 2 * i + s), f"x{s}_in")
            with sp.Fori(1, 4) as i:
                for s in range(2):
                    sp.wait_ge(sem("o_mm"), 2 * i - 1 + s)
                    load(colw[s], wtile(w_o, 2 * i + s), f"o{s}_in")
            for s in range(2):
                sp.wait_ge(sem("o_mm"), 7 + s)
                load(colw[s], w_up[s], f"u{s}_in")
            for s in range(2):
                load(downw[s], w_down[s], f"d{s}_in")
            for j in range(2):
                load(ln2gb[:, j * DM:(j + 1) * DM], ln2[j:j + 1, :].to_broadcast([P, DM]), "ln2_in")
            with sp.Fori(1, 16) as i:
                for s in range(2):
                    sp.wait_ge(sem("up_mm"), 2 * i - 1 + s)
                    load(colw[s], wtile(w_up, 2 * i + s), f"u{s}_in")
            with sp.Fori(1, 4) as i:
                for s in range(2):
                    sp.wait_ge(sem("down_mm"), 2 * i - 1 + s)
                    load(downw[s], wtile(w_down, 2 * i + s), f"d{s}_in")
            for t in range(TT):
                sp.wait_ge(sem("final_out"), t + 1)
                sp.dma_start(o_y[t], xn[t % 2]).then_inc(sem(f"y{t % 2}_st"), 16)
            sp.wait_ge(sem("y0_st"), 48)
            sp.wait_ge(sem("y1_st"), 32)
            sp.wait_ge(sem("out_st"), 16 * 6)
            sp.wait_ge(sem("conv_st"), 32)

        @block.tensor
        def _(pe):
            def product(s, ksteps, weight, act, done, b0=0):
                for k in range(ksteps):
                    w = weight[:, k * P:(k + 1) * P]
                    pe.matmul(ps[b0 + 2 * s][:, :], w, act[:, k, 0:NP], start=k == 0, stop=k == ksteps - 1)
                    mm = pe.matmul(ps[b0 + 2 * s + 1][:, 0:P], w, act[:, k, NP:TOK], start=k == 0,
                                   stop=k == ksteps - 1)
                if done:
                    mm.then_inc(sem(done), 1)

            pe.wait_ge(sem("x_in"), 16)
            pe.wait_ge(sem("ab_in"), 16)
            for t in range(TT):
                for k in range(KT):
                    mm = pe.matmul(ps[7][:, t * 8:t * 8 + 8], x3[:, k, t * P:(t + 1) * P], wab[:, k, :],
                                   start=k == 0, stop=k == KT - 1)
            mm.then_inc(sem("ab_mm"), 1)

            def h_tiles(i, first):
                for s in range(2):
                    pe.wait_ge(sem(f"w{s}_in"), 16 * (i + 1))
                    if not first:
                        pe.wait_ge(sem("h_out_v" if s == 0 else "h_out_a"), i)
                    product(s, KT, ring[:, s * 1024:(s + 1) * 1024], x3, "h_mm")

            h_tiles(0, True)
            with pe.Fori(1, 13) as i:
                h_tiles(i, False)

            def bank(stage, n):
                r = ROUND[stage, n]
                if r >= 8:
                    old, m = ROUNDS[r - 8]
                    pe.wait_ge(sem(f"{old}_out"), m + 1)
                return ps[r % 8]

            def per_head(stage, t, lhsT, rhs):
                b = heads(bank(stage, t)[:, :])
                for h in range(H):
                    mm = pe.matmul(b[:, h, :], lhsT(h), rhs(h), start=True, stop=True)
                mm.then_inc(sem(f"{stage}_mm"), 1)

            def per_head_transpose(stage, t, src):
                b = heads(bank(stage, t)[:, :])
                for h in range(H):
                    mm = pe.transpose(b[:, h, :], src(h), ident)
                mm.then_inc(sem(f"{stage}_mm"), 1)

            def tok(t):
                return slice(t * P, (t + 1) * P)

            pe.wait_ge(sem("cst_in"), 16)
            pe.wait_ge(sem("h_out_v"), 13)
            pe.wait_ge(sem("h_out_a"), 13)
            for n in range(8):
                pe.wait_ge(sem("sq_out"), n + 1)
                for j, c in enumerate((slice(0, NP), slice(NP, TOK))):
                    b = bank("norm", 2 * n + j)
                    pe.matmul(b[:, 0:c.stop - c.start], const("ones"), sq[n % 2][:, c], start=True,
                              stop=True).then_inc(sem("norm_mm"), 1)
            pe.wait_ge(sem("g_out"), 1)
            b = bank("gcol", 0)
            for t in range(TT):
                kind = "p" if t < 4 else "s"
                pe.matmul(b[:, t * 8:t * 8 + 4], const(f"cum_{kind}"), g_tok[:, t, :], start=True, stop=True)
                mm = pe.matmul(b[:, t * 8 + 4:t * 8 + 8], const("ones" if t < 4 else "blk_s"), g_tok[:, t, :],
                               start=True, stop=True)
            mm.then_inc(sem("gcol_mm"), 1)
            pe.wait_ge(sem("beta_out"), 1)
            pe.wait_ge(sem("qk_norm"), 8)
            pe.wait_ge(sem("silu_out"), 12)

            def key_products(t):
                pe.wait_ge(sem("brow_out"), t + 1)
                per_head("kk", t, lambda h: qkv3[:, 4 + h, tok(t)], lambda h: KB[:, t, h, :])

            for t in range(TT):
                cum = const("cum_p" if t < 4 else "cum_s")
                per_head("qk", t, lambda h: qkv3[:, 4 + h, tok(t)], lambda h: qkv3[:, h, tok(t)])
                per_head("grow", t, lambda h: g_tok[:, t, h:h + 1].to_broadcast([P, P]), lambda h: cum)
                per_head("brow", t, lambda h: beta[:, t, h:h + 1].to_broadcast([P, P]), lambda h: ident)
                per_head_transpose("ktr", t, lambda h: qkv3[:, 4 + h, tok(t)])
                per_head_transpose("vtr", t, lambda h: qkv3[:, 8 + h, tok(t)])
                if t:
                    key_products(t - 1)
            key_products(TT - 1)
            for t in range(TT):
                pe.wait_ge(sem("nd_out"), t + 1)
                per_head_transpose("ntr", t, lambda h: PWT[:, t, h, :])

            def update(level, t):
                power = "p" if level < 4 else "y"
                pe.wait_ge(sem(f"{power}_out"), level_count(power, level, t) + 1)
                if level == 1:
                    pe.wait_ge(sem("x0_out"), t + 1)
                else:
                    pe.wait_ge(sem("xt_out"), level_count("xt", level - 1, t) + 1)
                if level < 6:
                    per_head("x", level_count("x", level, t), lambda h: XT[:, t, h, :], lambda h: PW[:, t, h, :])

            def update_t(level, t):
                per_head("xt", level_count("xt", level, t), lambda h: PW[:, t, h, :], lambda h: XT[:, t, h, :])

            for level in (1, 2, 3):
                for t in range(TT):
                    if level == 1:
                        pe.wait_ge(sem("ntr_out"), t + 1)
                    else:
                        pe.wait_ge(sem("p_out"), level_count("p", level - 1, t) + 1)
                        pe.wait_ge(sem("pt_out"), level_count("pt", level - 1, t) + 1)
                    per_head("p", level_count("p", level, t), lambda h: PWT[:, t, h, :], lambda h: PW[:, t, h, :])
                if level < 3:
                    for t in range(TT):
                        per_head("pt", level_count("pt", level, t), lambda h: PW[:, t, h, :], lambda h: PWT[:, t, h, :])
                for t in range(TT):
                    update(level, t)
                for t in range(TT):
                    update_t(level, t)
            for level in (4, 5, 6):
                for t in range(TT - 1):
                    pe.wait_ge(sem("off_out"), level_count("off", level, t) + 1)
                    pe.wait_ge(sem("x_out"), level_count("x", level - 1, t) + 1)
                    per_head("y", level_count("y", level, t), lambda h: PWT[:, t, h, :], lambda h: X[:, t, h, :])
                for t in range(TT - 1):
                    update(level, t)
                for t in range(TT - 1):
                    update_t(level, t)

            def new_values(t):
                pe.wait_ge(sem("r_out"), t + 1)
                per_head("vn", t, lambda h: XT[:, t, h, :], lambda h: r_sb[:, h, :])

            for t in range(TT - 1):
                pe.wait_ge(sem("xt_out"), level_count("xt", 6, t) + 1)
                pe.wait_ge(sem("s_zero"), 1)
                if t >= 1:
                    pe.wait_ge(sem("ds_out"), t)
                per_head("ks", t, lambda h: qkv3[:, 4 + h, tok(t)], lambda h: S[:, h, :])
                new_values(t)
                pe.wait_ge(sem("qe_out"), t + 1)
                pe.wait_ge(sem("qk_out"), t + 1)
                b = heads(bank("go", t)[:, :])
                pe.wait_ge(sem("vn_out"), t + 1)
                for h in range(H):
                    pe.matmul(b[:, h, :], S[:, h, :], qkv3[:, h, tok(t)], start=True, stop=False)
                    mm = pe.matmul(b[:, h, :], vn_sb[:, h, :], QKD[:, t, h, :], start=False, stop=True)
                mm.then_inc(sem("go_mm"), 1)
                pe.wait_ge(sem("ktr_out"), t + 1)
                per_head("ds", t, lambda h: KD[:, t, h, :], lambda h: vn_sb[:, h, :])
            pe.wait_ge(sem("s0_in"), 16)
            b = heads(bank("kst", 0)[:, :])
            for h in range(H):
                for j in range(NB):
                    c = slice(NP + j * ST, NP + (j + 1) * ST)
                    mm = pe.matmul(b[:, h, j * ST:(j + 1) * ST], S0[:, h, j, :], qkv3[:, 4 + h, c],
                                   start=True, stop=True)
            mm.then_inc(sem("kst_mm"), 1)
            pe.wait_ge(sem("kst_out"), 1)
            per_head_transpose("ks", 4, lambda h: kst_sb[:, h, :])
            pe.wait_ge(sem("xt_out"), level_count("xt", 3, 4) + 1)
            new_values(4)
            pe.wait_ge(sem("qe_out"), 5)
            pe.wait_ge(sem("qk_out"), 5)
            b = heads(bank("go", 4)[:, :])
            pe.wait_ge(sem("vn_out"), 5)
            for h in range(H):
                pe.matmul(b[:, h, :], vn_sb[:, h, :], QKD[:, 4, h, :], start=True, stop=False,
                          skip_group_check=True)
                for j in range(NB):
                    c = slice(NP + j * ST, NP + (j + 1) * ST)
                    mm = pe.matmul(b[:, h, j * ST:(j + 1) * ST], S0[:, h, j, :], qkv3[:, h, c], start=False,
                                   stop=j == NB - 1, skip_group_check=True)
            mm.then_inc(sem("go_mm"), 1)
            for n in range(8):
                h, j = n // 2, n % 2 * 4
                b = bank("ss", n)
                pe.wait_ge(sem("vm_out"), h + 1)
                pe.matmul(b[:, :], KD[:, 4, h, :], vm_sb[h % 2][:, j:j + 4, :].rearrange("p b x -> p (b x)"),
                          start=True, stop=True).then_inc(sem("ss_mm"), 1)
            for n in range(4):
                pe.wait_ge(sem("osq_out"), n + 1)
                for j, c in enumerate((slice(0, NP), slice(NP, TOK))):
                    b = bank("on", 2 * n + j)
                    pe.matmul(b[:, 0:c.stop - c.start], const("mean"), sq[n % 2][:, c], start=True,
                              stop=True).then_inc(sem("on_mm"), 1)

            pe.wait_ge(sem("gdn_end"), 1)
            pe.wait_ge(sem("mem_in"), 16)
            for k in range(KT):
                pe.wait_ge(sem(f"wm{k % 4}_in"), 16 * (k // 4 + 1))
                for st in range(2):
                    for half in range(2):
                        mm = pe.matmul(ps[2 * st + half][:, :], mem_sb[:, k, st * P:(st + 1) * P],
                                       ring[:, (k % 4) * 1024 + half * 512:(k % 4) * 1024 + half * 512 + 512],
                                       start=k == 0, stop=k == KT - 1)
                mm.then_inc(sem("mem_mm"), 1)
            for t in range(TT):
                b = ps[6 + t // 4][:, (t % 4) * P:(t % 4 + 1) * P]
                mm = pe.transpose(b, h3[:, W_V, tok(t)], ident)
            mm.then_inc(sem("vtok_mm"), 1)
            pe.wait_ge(sem("mkv_out_v"), 2)
            pe.wait_ge(sem("mkv_out_a"), 2)
            for h in range(H):
                for st in range(2):
                    b = ps[4 + h // 2][:, (h % 2) * 256 + st * P:(h % 2) * 256 + st * P + P]
                    mm = pe.transpose(b, mkv[:, st, h * P:(h + 1) * P], ident)
            mm.then_inc(sem("mkT_mm"), 1)

            def scores(n):
                kind, t, m = UNITS[n]
                if n >= 2:
                    pe.wait_ge(sem("exp_out"), n - 1)
                b = sc_ps[n % 2]
                if kind == "wp":
                    k0 = max(t - 1, 0) * P
                    for g in range(2):
                        r = slice(64 * g, 64 * g + 64)
                        mm = pe.matmul(b[:, g, :], h3[r, W_Q + m, tok(t)],
                                       h3[r, W_K, k0:k0 + 256], start=True, stop=True)
                if kind == "ws":
                    for e in range(2):
                        j = 2 * m + e
                        for g in range(2):
                            r = slice(64 * g, 64 * g + 64)
                            q = qs_sb[r, j, :, :].rearrange("p m t -> p (m t)")
                            pe.matmul(b[r, e, 0:P], q, ck_sb[r, j, :], start=True, stop=True)
                            mm = pe.matmul(b[r, e, P:], q, h3[r, W_K, NP:TOK],
                                           start=True, stop=True)
                if kind == "mp":
                    for u in range(2):
                        mm = pe.matmul(b[:, u, :], h3[:, M_Q + 2 * m + u, tok(t)],
                                       mkT[:, 2 * m + u, :], start=True, stop=True)
                if kind == "ms":
                    pe.wait_ge(sem(f"cm{m % 2}_in"), 64 * (m // 2 + 1))
                    for e in range(2):
                        for h in range(H):
                            mm = pe.matmul(b[32 * h:32 * h + 32, e, :],
                                           h3[:, M_Q + h, NP + 32 * m:NP + 32 * m + 32],
                                           cm[m % 2][:, e, 0, h * 256:h * 256 + 256], start=True, stop=True,
                                           tile_position=(0, 32 * h))
                mm.then_inc(sem("sc_mm"), 1)

            def probs_turned(n):
                pe.wait_ge(sem("prob_out"), n + 1)
                if n >= 2:
                    pe.wait_ge(sem("pT_out"), n - 1)
                b = ps[4 + n % 2]
                for u in range(2):
                    for st in range(2):
                        mm = pe.transpose(b[:, (2 * u + st) * P:(2 * u + st + 1) * P],
                                          sm_sb[n % 2][:, u, st * P:(st + 1) * P], ident)
                mm.then_inc(sem("pT_mm"), 1)

            def values(n):
                kind, t, m = UNITS[n]
                pe.wait_ge(sem("pT_out"), n + 1)
                if n >= 2:
                    pe.wait_ge(sem("at_out"), n - 1)
                b, pT = ps[6 + n % 2], pT_sb[n % 2]
                for u in range(2):
                    for st in range(2):
                        go = dict(start=st == 0, stop=st == 1)
                        if kind == "wp":
                            mm = pe.matmul(b[64 * u:64 * u + 64, 0:P], vtok[:, max(t - 1, 0) + st, 64 * u:64 * u + 64],
                                           pT[:, u, st, :], **go)
                        if kind == "mp":
                            c = 512 + (2 * m + u) * P
                            mm = pe.matmul(b[:, u * P:(u + 1) * P], mkv[:, st, c:c + P], pT[:, u, st, :], **go)
                    if kind == "ws":
                        for g in range(2):
                            r = slice(64 * g, 64 * g + 64)
                            pe.matmul(b[r, u * 64:u * 64 + 64], cv_sb[:, 2 * m + u, r], pT[:, u, 0, r],
                                      start=True, stop=False)
                            mm = pe.matmul(b[r, u * 64:u * 64 + 64], vtok[:, 4, r], pT[:, u, 1, r],
                                           start=False, stop=True)
                    if kind == "ms":
                        for h in range(H):
                            for st in range(2):
                                c = 512 * st + h * P
                                mm = pe.matmul(b[:, h * 32 + 16 * u:h * 32 + 16 * u + 16],
                                               cm[m % 2][:, u, 1, c:c + P],
                                               pT[:, u, st, 32 * h + 16 * u:32 * h + 16 * u + 16],
                                               start=st == 0, stop=st == 1)
                mm.then_inc(sem("pv_mm"), 1)

            pe.wait_ge(sem("ck_in"), 32)
            pe.wait_ge(sem("qs_out"), 1)
            pe.wait_ge(sem("vtok_out"), 2)
            pe.wait_ge(sem("mkT_out"), 2)
            for n in range(NU + 2):
                if n < NU:
                    scores(n)
                if 1 <= n <= NU:
                    probs_turned(n - 1)
                if n >= 2:
                    values(n - 2)

            pe.wait_ge(sem("at_out"), NU)

            def mix_tiles(i, first):
                for s in range(2):
                    pe.wait_ge(sem(f"x{s}_in"), 16 * (i + 1))
                    for br, act in enumerate((oG, oS, oX)):
                        j = 3 * s + br
                        if not first or j >= 2:
                            pe.wait_ge(sem("gated_out"), 6 * i + j - 1)
                        product(0, 4, mixw[s][:, br * 512:br * 512 + 512], act, None, b0=4 * (j % 2))
                        product(1, KT, mixw[s][:, 1536 + br * DM:1536 + (br + 1) * DM], x3, "gate_mm",
                                b0=4 * (j % 2))

            mix_tiles(0, True)
            with pe.Fori(1, 4) as i:
                mix_tiles(i, False)

            def column_tiles(i, first, name, out, weights, ksteps, act):
                for s in range(2):
                    pe.wait_ge(sem(f"{name}{s}_in"), 16 * (i + 1))
                    if not first:
                        pe.wait_ge(sem(out + "_out"), 2 * i + s - 1)
                    product(s, ksteps, weights[s], act, out + "_mm")

            pe.wait_ge(sem("merged_out"), 8)
            column_tiles(0, True, "o", "o", colw, KT, merged)
            with pe.Fori(1, 4) as i:
                column_tiles(i, False, "o", "o", colw, KT, merged)

            def to_tokens(t, done):
                if t >= 2:
                    pe.wait_ge(sem(f"{done}_norm"), t - 1)
                for k in range(KT):
                    mm = pe.transpose(ps[2 * (t % 2) + k // 4][:, (k % 4) * P:(k % 4 + 1) * P], x3[:, k, tok(t)],
                                      ident)
                mm.then_inc(sem(f"{done}_turn"), 1)

            def to_channels(t):
                pe.wait_ge(sem("ln1_norm"), t + 1)
                if t >= 2:
                    pe.wait_ge(sem("ln1_out"), t - 1)
                for k in range(KT):
                    mm = pe.transpose(ps[4 + 2 * (t % 2) + k // 4][:, (k % 4) * P:(k % 4 + 1) * P],
                                      xn[t % 2][:, k * P:(k + 1) * P], ident)
                mm.then_inc(sem("ln1_back"), 1)

            pe.wait_ge(sem("o_out"), 8)
            for t in range(TT + 1):
                if t < TT:
                    to_tokens(t, "ln1")
                if t >= 1:
                    to_channels(t - 1)

            pe.wait_ge(sem("ln1_out"), TT)
            column_tiles(0, True, "u", "up", colw, KT, x3)
            with pe.Fori(1, 16) as i:
                column_tiles(i, False, "u", "up", colw, KT, x3)
            pe.wait_ge(sem("hid_out"), FT)
            column_tiles(0, True, "d", "down", downw, FT, hid)
            with pe.Fori(1, 4) as i:
                column_tiles(i, False, "d", "down", downw, FT, hid)
            pe.wait_ge(sem("down_out"), 8)
            for t in range(TT):
                to_tokens(t, "ln2")

        @block.vector
        def _(dve):
            steps = [0]

            def then_wait(ins):
                steps[0] += 1
                ins.then_inc(sem("dve_step"), 1)
                dve.wait_ge(sem("dve_step"), steps[0])

            def bc(ap, n):
                return ap.unsqueeze(2).to_broadcast([P, ap.shape[1], n])

            def flat(ap):
                return ap.rearrange("p h x -> p (h x)")

            dve.memset(pad3[:, :, 0:PAD], 0.0)
            dve.memset(eps, 1e-6)
            dve.wait_ge(sem("par_in"), 16 * 8)
            dve.tensor_copy(pad3[:, :, NP + PAD:].rearrange("p k (b s) -> p k b s", b=NB)[:, :, :, 0:PAD],
                            cs_in.rearrange("p (k b s) -> p k b s", k=12, b=NB))
            dve.tensor_scalar(nsinkb, sinkb, -1.0, None, ALU.mult)
            dve.tensor_scalar(nsinkc, sinkc, -1.0, None, ALU.mult)
            dve.wait_ge(sem("ab_mm"), 1)
            then_wait(dve.tensor_copy(ab.rearrange("p t x -> p (t x)"), ps[7][:, 0:40]))
            then_wait(dve.tensor_tensor(t_a, ab[:, :, 0:4], dtb.unsqueeze(1).to_broadcast([P, TT, 4]), ALU.add))
            dve.scalar_tensor_tensor(t_b, t_a, -1.0, t_a, ALU.mult, ALU.max).then_inc(sem("ab_out"), 1)
            then_wait(dve.tensor_scalar(t_a, t_a, 0.0, None, ALU.max))
            dve.wait_ge(sem("ln_out"), 1)
            then_wait(dve.tensor_tensor(t_a, t_a, t_c, ALU.add))
            dve.scalar_tensor_tensor(g_tok, t_a, -1.0, nea.unsqueeze(1).to_broadcast([P, TT, 4]), ALU.mult,
                                     ALU.mult).then_inc(sem("g_out"), 1)
            then_wait(dve.tensor_scalar(e_b, e_b, 1.0, None, ALU.add))
            dve.reciprocal(beta, e_b).then_inc(sem("beta_out"), 1)

            def read_tile(i, dst, split):
                dve.wait_ge(sem("h_mm"), 2 * i + 1)
                if split:
                    a, b = padded(dst)
                    dve.tensor_copy(a, ps[0][:, :])
                    last = dve.tensor_copy(b, ps[1][:, 0:P].rearrange("p (b s) -> p b s", b=NB))
                else:
                    dve.tensor_copy(dst[:, 0:NP], ps[0][:, :])
                    last = dve.tensor_copy(dst[:, NP:TOK], ps[1][:, 0:P])
                last.then_inc(sem("h_out_v"), 1)

            pad_flat = arena[:, P0:P0 + 12 * QW]
            with dve.Fori(0, 6) as i:
                read_tile(i, cols(pad_flat, 2 * i, QW), True)

            def convolve(i, s, first):
                n = 2 * i + s
                if s == 0 or first:
                    dve.wait_ge(sem("h_out_v"), 6)
                    dve.wait_ge(sem("h_out_a"), 6)
                if not first:
                    dve.wait_ge(sem("silu_out"), n - 1)
                acc = conv_acc[s]

                def tap(w):
                    return arena[:, bass.ds(n * QW + (P0 + w), CW)], cw_sb[:, bass.ds(4 * n + w, 1)]

                x0, w0 = tap(0)
                dve.tensor_scalar(acc, x0, w0, None, ALU.mult).then_inc(sem("conv_step"), 1)
                for w in range(1, 4):
                    dve.wait_ge(sem("conv_step"), 3 * n + w)
                    xw, ww = tap(w)
                    ins = dve.scalar_tensor_tensor(acc, xw, ww, acc, ALU.mult, ALU.add)
                    ins.then_inc(sem("conv_step" if w < 3 else "conv_out"), 1)

            def tile_and_conv(i, first):
                read_tile(i + 6, cols(h_sb, 2 * i), False)
                for s in range(2):
                    convolve(i, s, first)

            tile_and_conv(0, True)
            with dve.Fori(1, 6) as i:
                tile_and_conv(i, False)
            read_tile(12, h3[:, 12, :], False)
            dve.tensor_copy(cs_out.rearrange("p (k b s) -> p k b s", k=12, b=NB),
                            pad3[:, :, NP + PAD:].rearrange("p k (b s) -> p k b s", b=NB)[:, :, :, ST:]
                            ).then_inc(sem("cs_out"), 1)

            for n in range(8):
                dve.wait_ge(sem("norm_out"), 2 * n + 2)
                then_wait(dve.reciprocal(rn[n % 2], rn[n % 2]))
                dve.scalar_tensor_tensor(qkv3[:, n, :], qkv3[:, n, :], P ** -0.5 if n < H else 1.0, rn[n % 2],
                                         ALU.mult, ALU.mult).then_inc(sem("qk_norm"), 1)

            def result(stage, n):
                dve.wait_ge(sem(f"{stage}_mm"), n + 1)
                return ps[ROUND[stage, n] % 8]

            then_wait(dve.tensor_copy(gcl.rearrange("p t x -> p (t x)"), result("gcol", 0)[:, 0:40]))
            dve.tensor_tensor(glc, gcl[:, :, 4:8], gcl[:, :, 0:4], ALU.subtract).then_inc(sem("gcol_out"), 1)
            dve.wait_ge(sem("ecol_out"), 2)
            then_wait(dve.scalar_tensor_tensor(nbeg, beta, -1.0, nbeg, ALU.mult, ALU.mult))

            dve.wait_ge(sem("conv_st"), 32)

            def lower_part(t):
                dve.tensor_tensor(NT[:, t], heads(result("kk", t)[:, :]), DEC[:, t], ALU.mult
                                  ).then_inc(sem("kk_out"), 1)

            for t in range(TT):
                b = heads(result("grow", t)[:, :])
                mask = const("neg_p" if t < 4 else "neg_s")
                if t >= 2:
                    dve.wait_ge(sem("dec_out"), t - 1)
                then_wait(dve.tensor_tensor(d_sb[t % 2], b, bc(gcl[:, t, 0:4], P), ALU.subtract))
                dve.tensor_tensor(d_sb[t % 2], d_sb[t % 2], mask.unsqueeze(1).to_broadcast([P, H, P]),
                                  ALU.min).then_inc(sem("dmin_out"), 1)
                dve.tensor_tensor(KB[:, t], qkv3[:, 4:8, t * P:(t + 1) * P], heads(result("brow", t)[:, :]),
                                  ALU.mult).then_inc(sem("brow_out"), 1)
                dve.tensor_tensor(KD[:, t], heads(result("ktr", t)[:, :]), bc(kdec[:, t, :], P),
                                  ALU.mult).then_inc(sem("ktr_out"), 1)
                dve.tensor_tensor(VB[:, t], heads(result("vtr", t)[:, :]), bc(beta[:, t, :], P),
                                  ALU.mult).then_inc(sem("vtr_out"), 1)
                e = eg_sb[t % 2]
                dve.wait_ge(sem("grow_out"), t + 1)
                if t < 4:
                    dve.tensor_copy(egl[:, t, :].unsqueeze(2), e[:, :, P - 1:P])
                else:
                    dve.tensor_copy(egs, e[:, :, ST - 1::ST])
                q = qkv3[:, 0:4, t * P:(t + 1) * P]
                b = heads(result("qk", t)[:, :])
                dve.tensor_tensor(q, q, e, ALU.mult).then_inc(sem("qe_out"), 1)
                dve.wait_ge(sem("dec_out"), t + 1)
                dve.tensor_tensor(QKD[:, t], b, DEC[:, t], ALU.mult).then_inc(sem("qk_out"), 1)
                if t:
                    lower_part(t - 1)
            lower_part(TT - 1)

            for level in range(1, 7):
                tt = TT if level < 4 else TT - 1
                if level < 6:
                    for t in range(tt):
                        if level == 1:
                            dve.wait_ge(sem("x0_out"), t + 1)
                        b = result("x", level_count("x", level, t))
                        dve.tensor_tensor(X[:, t], X[:, t], heads(b[:, :]), ALU.add).then_inc(sem("x_out"), 1)
                for t in range(tt):
                    b = result("xt", level_count("xt", level, t))
                    dve.tensor_tensor(XT[:, t], XT[:, t], heads(b[:, :]), ALU.add).then_inc(sem("xt_out"), 1)
                if level == 1:
                    then_wait(dve.memset(S, 0.0))
                    dve.sem_inc(sem("s_zero"), 1)

            def residual(t):
                b = heads(result("ks", t)[:, :])
                dve.tensor_tensor(r_sb, b, bc(nbeg[:, t, :], P), ALU.mult).then_inc(sem("ks_out"), 1)
                dve.wait_ge(sem("ks_out"), t + 1)
                dve.tensor_tensor(r_sb, r_sb, VB[:, t], ALU.add).then_inc(sem("r_out"), 1)

            for t in range(TT - 1):
                residual(t)
                b = heads(result("ds", t)[:, :])
                then_wait(dve.tensor_tensor(S, S, bc(egl[:, t, :], P), ALU.mult))
                dve.tensor_tensor(S, S, b, ALU.add).then_inc(sem("ds_out"), 1)

            def stream_states(h):
                for n in (2 * h, 2 * h + 1):
                    j = n % 2 * 4
                    state = S0[:, h, j:j + 4, :]
                    b = result("ss", n)[:, :].rearrange("p (b v) -> p b v", b=4)
                    then_wait(dve.tensor_tensor(state, state, bc(egs[:, h, j:j + 4], P), ALU.mult))
                    dve.tensor_tensor(state, state, b, ALU.add).then_inc(sem("ss_out"), 1)

            residual(4)
            dve.wait_ge(sem("vn_out"), 5)
            for h in range(H):
                if h >= 2:
                    dve.wait_ge(sem("ss_mm"), 2 * h - 2)
                dve.tensor_tensor(vm_sb[h % 2], vn_sb[:, h, :].unsqueeze(1).to_broadcast([P, NB, P]),
                                  const("tokblk").unsqueeze(2).to_broadcast([P, NB, P]), ALU.mult
                                  ).then_inc(sem("vm_out"), 1)
                if h >= 1:
                    stream_states(h - 1)
            stream_states(H - 1)
            for n in range(4):
                dve.wait_ge(sem("on_out"), 2 * n + 2)
                then_wait(dve.reciprocal(rn_o[n % 2], rn_o[n % 2]))
                then_wait(dve.scalar_tensor_tensor(oG[:, n, :], oG[:, n, :], nrm[:, 0:1], rn_o[n % 2],
                                                   ALU.mult, ALU.mult))
                if n == 0:
                    dve.wait_ge(sem("z_out"), 1)
                dve.tensor_tensor(oG[:, n, :], oG[:, n, :], h3[:, n, :], ALU.mult).then_inc(sem("og_out"), 1)
            dve.wait_ge(sem("og_out"), 4)
            dve.sem_inc(sem("gdn_end"), 1)

            dve.wait_ge(sem("mem_mm"), KT)
            for st in range(2):
                dve.tensor_copy(mkv[:, st, 0:512], ps[2 * st][:, :]).then_inc(sem("mkv_out_v"), 1)
            dve.wait_ge(sem("vtok_mm"), 1)
            dve.tensor_copy(vtok[:, 0:4, :].rearrange("p t x -> p (t x)"), ps[6][:, :]).then_inc(sem("vtok_out"), 1)
            dve.tensor_copy(vtok[:, 4, :], ps[7][:, 0:P]).then_inc(sem("vtok_out"), 1)
            dve.wait_ge(sem("mkT_mm"), 1)
            for j in range(2):
                dve.tensor_copy(mkT[:, 2 * j:2 * j + 2, :].rearrange("p h s -> p (h s)"), ps[4 + j][:, :]
                                ).then_inc(sem("mkT_out"), 1)

            def front(n):
                kind, t, m = UNITS[n]
                dve.wait_ge(sem("sc_mm"), n + 1)
                b = sc_ps[n % 2]
                s, neg = sm_sb[n % 2], nm[n % 2]
                if kind in ("mp", "ms"):
                    then_wait(dve.tensor_reduce(neg, b, AX.X, ALU.max, negate=True))
                    dve.tensor_scalar(neg, neg, M_SCALE, None, ALU.mult).then_inc(sem("nm_out"), 1)
                    return
                if n >= 2:
                    dve.wait_ge(sem("pT_mm"), n - 1)
                if kind == "wp":
                    mask = const("win0" if t == 0 else "win")
                    then_wait(dve.scalar_tensor_tensor(s, b, W_SCALE, mask.unsqueeze(1).to_broadcast([P, 2, 256]),
                                                       ALU.mult, ALU.add))
                    sink, nsink = sinkb[:, m::4], nsinkb[:, m::4]
                else:
                    dve.tensor_scalar(s[:, :, 0:P], b[:, :, 0:P], W_SCALE, None, ALU.mult)
                    for e in range(2):
                        x = 112 - ST * (2 * m + e)
                        last = dve.scalar_tensor_tensor(s[:, e, P:], b[:, e, P:], W_SCALE,
                                                        const("snew")[:, x:x + P], ALU.mult, ALU.add)
                    then_wait(last)
                    sink, nsink = sinkc.to_broadcast([P, 2]), nsinkc.to_broadcast([P, 2])
                then_wait(dve.tensor_reduce(neg, s, AX.X, ALU.max, negate=True))
                then_wait(dve.tensor_tensor(neg, neg, nsink, ALU.min))
                dve.tensor_tensor(es[n % 2], neg, sink, ALU.add).then_inc(sem("nm_out"), 1)

            def back(n):
                i = n % 2
                dve.wait_ge(sem("exp_out"), n + 1)
                if UNITS[n][0] in ("wp", "ws"):
                    then_wait(dve.tensor_tensor(den[i], den[i], es[i], ALU.add))
                then_wait(dve.reciprocal(rden[i], den[i]))
                dve.tensor_tensor(sm_sb[i], sm_sb[i], rden[i].unsqueeze(2).to_broadcast([P, 2, 256]), ALU.mult
                                  ).then_inc(sem("prob_out"), 1)

            for n in range(NU + 1):
                if n < NU:
                    front(n)
                if n >= 1:
                    back(n - 1)

            merged_flat = arena[:, 0:KT * TOK]

            def merge(i, first):
                for s in range(2):
                    dst = cols(merged_flat, 2 * i + s)
                    for br in range(3):
                        j = 3 * s + br
                        g, b0 = sg[j % 2], 4 * (j % 2)
                        dve.wait_ge(sem("sg_out"), 6 * i + j + 1)
                        to = dst if br == 0 else gated[j % 2]
                        if br == 1 and not (first and s == 0):
                            dve.wait_ge(sem("merged_out"), 2 * i + s)
                        if br == 2:
                            dve.wait_ge(sem("merged_two"), 2 * i + s + 1)
                        dve.tensor_tensor(to[:, 0:NP], ps[b0][:, :], g[:, 0:NP], ALU.mult)
                        dve.tensor_tensor(to[:, NP:TOK], ps[b0 + 1][:, 0:P], g[:, NP:TOK], ALU.mult
                                          ).then_inc(sem("gated_out"), 1)
                        if br:
                            dve.wait_ge(sem("gated_out"), 6 * i + j + 1)
                            dve.tensor_tensor(dst, dst, gated[j % 2], ALU.add
                                              ).then_inc(sem("merged_two" if br == 1 else "merged_out"), 1)

            merge(0, True)
            with dve.Fori(1, 4) as i:
                merge(i, False)

            def residuals(i, name):
                for s in range(2):
                    dve.wait_ge(sem(name + "_mm"), 2 * i + s + 1)
                    x = cols(x_sb[:, :], 2 * i + s)
                    dve.scalar_tensor_tensor(x[:, 0:NP], x[:, 0:NP], ALPHA, ps[2 * s][:, :], ALU.mult, ALU.add)
                    dve.scalar_tensor_tensor(x[:, NP:TOK], x[:, NP:TOK], ALPHA, ps[2 * s + 1][:, 0:P], ALU.mult,
                                             ALU.add).then_inc(sem(name + "_out"), 1)

            with dve.Fori(0, 4) as i:
                residuals(i, "o")

            def token_stats(t, name):
                i = t % 2
                dve.wait_ge(sem(f"{name}_turn"), t + 1)
                for j in range(2):
                    last = dve.bn_stats(stats[i][:, 6 * j:6 * j + 6], ps[2 * i + j][:, :])
                then_wait(last)
                then_wait(dve.bn_aggr(mv[i], stats[i]))
                then_wait(dve.tensor_scalar(rstd[i], mv[i][:, 1:2], 1e-5, None, ALU.add))
                dve.sem_inc(sem("var_out"), 1)
                dve.wait_ge(sem("dev_out"), t + 1 + (TT if name == "ln2" else 0))
                then_wait(dve.reciprocal(rstd[i], rstd[i]))

            for t in range(TT):
                i = t % 2
                token_stats(t, "ln1")
                if t >= 2:
                    dve.wait_ge(sem("ln1_back"), t - 1)
                for j in range(2):
                    last = dve.tensor_scalar(xn[i][:, 512 * j:512 * j + 512], ps[2 * i + j][:, :], mv[i][:, 0:1],
                                             rstd[i], ALU.subtract, ALU.mult)
                last.then_inc(sem("ln1_norm"), 1)

            dve.wait_ge(sem("out_st"), 16 * 6)
            hid_flat = arena[:, 0:FT * TOK]
            with dve.Fori(0, 16) as i:
                for s in range(2):
                    dve.wait_ge(sem("up_out"), 2 * i + s + 1)
                    dve.tensor_tensor(cols(hid_flat, 2 * i + s), relu[s], relu[s], ALU.mult
                                      ).then_inc(sem("hid_out"), 1)
            with dve.Fori(0, 4) as i:
                residuals(i, "down")
            dve.wait_ge(sem("ln2_in"), 32)
            for t in range(TT):
                i = t % 2
                token_stats(t, "ln2")
                if t >= 2:
                    dve.wait_ge(sem(f"y{i}_st"), 16 * (t // 2))
                for j in range(2):
                    last = dve.tensor_scalar(xn[i][:, 512 * j:512 * j + 512], ps[2 * i + j][:, :], mv[i][:, 0:1],
                                             rstd[i], ALU.subtract, ALU.mult)
                last.then_inc(sem("ln2_norm"), 1)
                dve.wait_ge(sem("ln2_norm"), t + 1)
                then_wait(dve.tensor_tensor(xn[i], xn[i], ln2gb[:, 0:DM], ALU.mult))
                dve.tensor_tensor(xn[i], xn[i], ln2gb[:, DM:], ALU.add).then_inc(sem("final_out"), 1)

        @block.scalar
        def _(act):
            steps = [0]

            def then_wait(ins):
                steps[0] += 1
                ins.then_inc(sem("act_step"), 1)
                act.wait_ge(sem("act_step"), steps[0])

            act.wait_ge(sem("par_in"), 16 * 8)
            act.activation(nea, alog, ACT.Exp)
            act.wait_ge(sem("ab_out"), 1)
            act.activation(e_b, ab[:, :, 4:8], ACT.Exp, scale=-1.0)
            then_wait(act.activation(t_b, t_b, ACT.Exp, scale=-1.0))
            act.activation(t_c, t_b, ACT.Ln, bias=1.0).then_inc(sem("ln_out"), 1)

            def read_tile(i, dst, split):
                act.wait_ge(sem("h_mm"), 2 * i + 2)
                if split:
                    a, b = padded(dst)
                    act.copy(a, ps[2][:, :])
                    last = act.copy(b, ps[3][:, 0:P].rearrange("p (b s) -> p b s", b=NB))
                else:
                    act.copy(dst[:, 0:NP], ps[2][:, :])
                    last = act.copy(dst[:, NP:TOK], ps[3][:, 0:P])
                last.then_inc(sem("h_out_a"), 1)

            pad_flat = arena[:, P0:P0 + 12 * QW]
            with act.Fori(0, 6) as i:
                read_tile(i, cols(pad_flat, 2 * i + 1, QW), True)
            with act.Fori(0, 6) as i:
                read_tile(i + 6, cols(h_sb, 2 * i + 1), False)
                for s in range(2):
                    act.wait_ge(sem("conv_out"), 2 * i + s + 1)
                    row = cols(arena[:, Q0:Q0 + 12 * TOK], 2 * i + s)
                    act.activation(row[:, 0:NP], conv_acc[s][:, 0:NP], ACT.Silu)
                    own = conv_acc_streams[s]
                    act.activation(stream(row), own, ACT.Silu).then_inc(sem("silu_out"), 1)
            read_tile(12, h3[:, 13, :], False)
            act.wait_ge(sem("h_out_v"), 13)
            act.wait_ge(sem("h_out_a"), 13)
            act.activation(h3[:, 0:4, :], h3[:, 0:4, :], ACT.Silu).then_inc(sem("z_out"), 1)

            def lengths(stage, n, to, used):
                if n >= 2:
                    act.wait_ge(sem(used), n - 1)
                for j, c in enumerate((slice(0, NP), slice(NP, TOK))):
                    act.wait_ge(sem(f"{stage}_mm"), 2 * n + j + 1)
                    b = ps[ROUND[stage, 2 * n + j] % 8][:, 0:c.stop - c.start]
                    act.activation(to[n % 2][:, c], b, ACT.Sqrt, bias=eps[:, 0:1]).then_inc(sem(f"{stage}_out"), 1)

            act.wait_ge(sem("silu_out"), 8)
            for n in range(8):
                if n >= 2:
                    act.wait_ge(sem("norm_mm"), 2 * n - 2)
                act.activation(sq[n % 2], qkv3[:, n, :], ACT.Square).then_inc(sem("sq_out"), 1)
                if n >= 1:
                    lengths("norm", n - 1, rn, "qk_norm")
            lengths("norm", 7, rn, "qk_norm")
            act.wait_ge(sem("gcol_out"), 1)
            act.activation(kdec, glc, ACT.Exp).then_inc(sem("ecol_out"), 1)
            act.activation(nbeg, gcl[:, :, 0:4], ACT.Exp).then_inc(sem("ecol_out"), 1)
            act.wait_ge(sem("norm_mm"), 16)
            for t in range(TT):
                act.wait_ge(sem("dmin_out"), t + 1)
                if t >= 2:
                    act.wait_ge(sem("qe_out"), t - 1)
                act.activation(eg_sb[t % 2], heads(ps[ROUND["grow", t] % 8][:, :]), ACT.Exp
                               ).then_inc(sem("grow_out"), 1)
                act.activation(DEC[:, t], d_sb[t % 2], ACT.Exp).then_inc(sem("dec_out"), 1)

            def keep(stage, t, dst, after=None):
                act.wait_ge(sem(f"{after or stage}_mm"), t + 1)
                act.copy(dst, heads(ps[ROUND[stage, t] % 8][:, :])).then_inc(sem(f"{stage}_out"), 1)

            for t in range(TT):
                keep("ntr", t, PW[:, t])
            for level in (1, 2, 3):
                for t in range(TT):
                    if level == 1:
                        act.wait_ge(sem("x0_out"), t + 1)
                    keep("p", level_count("p", level, t), PW[:, t], after="pt" if level < 3 else None)
                if level < 3:
                    for t in range(TT):
                        keep("pt", level_count("pt", level, t), PWT[:, t])
            for level in (4, 5, 6):
                for t in range(TT - 1):
                    keep("y", level_count("y", level, t), PW[:, t])
            for t in range(TT):
                if t == 4:
                    keep("kst", 0, kst_sb)
                keep("vn", t, vn_sb)
                keep("go", t, oG[:, :, t * P:(t + 1) * P])
            act.wait_ge(sem("ss_mm"), 8)
            for n in range(4):
                if n >= 2:
                    act.wait_ge(sem("on_mm"), 2 * n - 2)
                act.activation(sq[n % 2], oG[:, n, :], ACT.Square).then_inc(sem("osq_out"), 1)
                if n >= 1:
                    lengths("on", n - 1, rn_o, "og_out")
            lengths("on", 3, rn_o, "og_out")

            act.wait_ge(sem("mem_mm"), KT)
            for st in range(2):
                act.copy(mkv[:, st, 512:1024], ps[2 * st + 1][:, :]).then_inc(sem("mkv_out_a"), 1)

            def exponentials(n):
                kind, t, m = UNITS[n]
                i = n % 2
                act.wait_ge(sem("nm_out"), n + 1)
                window = kind in ("wp", "ws")
                if not window and n >= 2:
                    act.wait_ge(sem("pT_mm"), n - 1)
                b = sc_ps[i]
                for u in range(2):
                    ins = act.activation(sm_sb[i][:, u, :], sm_sb[i][:, u, :] if window else b[:, u, :], ACT.Exp,
                                         bias=nm[i][:, u:u + 1], scale=1.0 if window else M_SCALE,
                                         accum_out=den[i][:, u:u + 1])
                if window:
                    ins = act.activation(es[i], es[i], ACT.Exp)
                ins.then_inc(sem("exp_out"), 1)

            def turned(n):
                act.wait_ge(sem("pT_mm"), n + 1)
                if n >= 2:
                    act.wait_ge(sem("pv_mm"), n - 1)
                act.copy(pT_sb[n % 2].rearrange("p u s q -> p (u s q)"), ps[4 + n % 2][:, :]
                         ).then_inc(sem("pT_out"), 1)

            def outputs(n):
                kind, t, m = UNITS[n]
                act.wait_ge(sem("pv_mm"), n + 1)
                b = ps[6 + n % 2]
                c = NP + 32 * m
                if kind == "wp":
                    ins = act.copy(oS[:, m, t * P:(t + 1) * P], b[:, 0:P])
                if kind == "mp":
                    ins = act.copy(oX[:, 2 * m:2 * m + 2, t * P:(t + 1) * P],
                                   b[:, 0:256].rearrange("p (u q) -> p u q", u=2))
                if kind == "ws":
                    ins = act.copy(oS[:, :, c:c + 32].rearrange("p m (e t) -> p m e t", e=2),
                                   b[:, 0:P].rearrange("p (e m t) -> p m e t", e=2, m=4))
                if kind == "ms":
                    ins = act.copy(oX[:, :, c:c + 32], b[:, 0:P].rearrange("p (h x) -> p h x", h=H))
                ins.then_inc(sem("at_out"), 1)

            for n in range(NU + 2):
                if n < NU:
                    exponentials(n)
                if 1 <= n <= NU:
                    turned(n - 1)
                if n >= 2:
                    outputs(n - 2)

            act.wait_ge(sem("pm_st"), 16)
            act.wait_ge(sem("pv_mm"), NU)

            def gates(i, first):
                for j in range(6):
                    b0 = 4 * (j % 2) + 2
                    act.wait_ge(sem("gate_mm"), 6 * i + j + 1)
                    if not first or j >= 2:
                        act.wait_ge(sem("gated_out"), 6 * i + j - 1)
                    act.activation(sg[j % 2][:, 0:NP], ps[b0][:, :], ACT.Sigmoid)
                    act.activation(sg[j % 2][:, NP:TOK], ps[b0 + 1][:, 0:P], ACT.Sigmoid
                                   ).then_inc(sem("sg_out"), 1)

            gates(0, True)
            with act.Fori(1, 4) as i:
                gates(i, False)

            def deviation(t, n):
                act.wait_ge(sem("var_out"), n + 1)
                act.activation(rstd[t % 2], rstd[t % 2], ACT.Sqrt).then_inc(sem("dev_out"), 1)

            for t in range(TT + 1):
                if t < TT:
                    deviation(t, t)
                if t == 0:
                    continue
                t -= 1
                act.wait_ge(sem("ln1_back"), t + 1)
                for k in range(KT):
                    ins = act.activation(x3[:, k, t * P:(t + 1) * P],
                                         ps[4 + 2 * (t % 2) + k // 4][:, (k % 4) * P:(k % 4 + 1) * P], ACT.Identity,
                                         bias=ln1c[:, 8 + k:9 + k], scale=ln1c[:, k:k + 1])
                ins.then_inc(sem("ln1_out"), 1)

            def relus(i, first):
                for s in range(2):
                    act.wait_ge(sem("up_mm"), 2 * i + s + 1)
                    if not first:
                        act.wait_ge(sem("hid_out"), 2 * i + s - 1)
                    act.activation(relu[s][:, 0:NP], ps[2 * s][:, :], ACT.Relu)
                    act.activation(relu[s][:, NP:TOK], ps[2 * s + 1][:, 0:P], ACT.Relu).then_inc(sem("up_out"), 1)

            relus(0, True)
            with act.Fori(1, 16) as i:
                relus(i, False)
            for t in range(TT):
                deviation(t, TT + t)

        @block.gpsimd
        def _(pool):
            pool.wait_ge(sem("cst_in"), 16)

            def masked(out, src, mask):
                return pool.tensor_tensor(out, src, const(mask).unsqueeze(1).to_broadcast([P, H, P]), ALU.mult)

            for t in range(TT):
                pool.wait_ge(sem("kk_out"), t + 1)
                masked(NT[:, t], NT[:, t], "nstrict_p" if t < 4 else "nstrict_s").then_inc(sem("nt_out"), 1)
                pool.wait_ge(sem("nt_out"), t + 1)
                masked(PWT[:, t], NT[:, t], "bd16").then_inc(sem("nd_out"), 1)
            for t in range(TT):
                pool.wait_ge(sem("ntr_out"), t + 1)
                one = ident.unsqueeze(1).to_broadcast([P, H, P])
                pool.tensor_tensor(X[:, t], PW[:, t], one, ALU.add)
                pool.tensor_tensor(XT[:, t], PWT[:, t], one, ALU.add).then_inc(sem("x0_out"), 1)
            for level, size in ((4, 16), (5, 32), (6, 64)):
                for t in range(TT - 1):
                    if level == 4:
                        pool.wait_ge(sem("p_mm"), level_count("p", 3, t) + 1)
                    else:
                        pool.wait_ge(sem("y_mm"), level_count("y", level - 1, t) + 1)
                    masked(PWT[:, t], NT[:, t], f"off{size}").then_inc(sem("off_out"), 1)
            pool.wait_ge(sem("gdn_end"), 1)
            for m in range(4):
                last = pool.tensor_copy(qs_sb[:, :, m, :], stream(h3[:, W_Q + m, :]))
            last.then_inc(sem("qs_out"), 1)


def kernel(x_prompt, x_sample, state_gdn_s, state_gdn_conv, cache_swa_k, cache_swa_v, cache_mem_k, cache_mem_v,
           mem_prompt, w_in, conv_w, a_log, dt_bias, gdn_norm_w, attn_sinks, w_mem_kv, w_branch, w_o,
           ln1_g, ln1_b, w_up, w_down, ln2_g, ln2_b):
    import concourse.bacc as bacc
    from concourse.bass_utils import run_bass_kernel_spmd

    def ktiles(a):
        return a.reshape(a.shape[0] // P, P, -1).transpose(1, 0, 2)

    def coltiles(a):
        k = a.shape[0] // P
        return a.reshape(k, P, -1, P).transpose(2, 1, 0, 3).reshape(-1, P, k * P)

    w_in, w_branch = np.asarray(w_in)[0], np.asarray(w_branch)[0]
    x = np.concatenate([np.asarray(x_prompt)[0], np.asarray(x_sample).reshape(NB * ST, DM)])
    order = [h * 64 + d for m in range(4) for h in (m, 4 + m) for d in range(64)]
    o = 1536
    w_a, w_z = w_in[:, o:o + 8], w_in[:, o + 8:o + 520]
    o += 520
    w_qs, w_ks, w_vs, w_qx, w_g = (w_in[:, o + a:o + b] for a, b in (
        (0, 512), (512, 640), (640, 768), (768, 1280), (1280, 1280 + 3 * DM)))
    gate = [coltiles(w_g[:, b * DM:(b + 1) * DM]) for b in range(3)]
    branch = [coltiles(w) for w in (w_branch[0], w_branch[1][order], w_branch[2])]
    ck, cv = (np.asarray(c)[0].reshape(NB, P, P) for c in (cache_swa_k, cache_swa_v))
    cmk, cmv = (np.asarray(c)[0].reshape(NB, 256, H, P) for c in (cache_mem_k, cache_mem_v))
    conv_s = np.asarray(state_gdn_conv)[0].reshape(NB, PAD, 12, P)
    arrays = {
        "xT": ktiles(x.T).reshape(P, -1),
        "memT": ktiles(np.asarray(mem_prompt)[0].T).reshape(P, -1),
        "w_h": coltiles(np.concatenate([w_in[:, :1536], w_z, w_qs[:, order], w_ks, w_vs, w_qx], axis=1)),
        "w_ab": ktiles(w_a).reshape(P, -1),
        "w_mem": np.asarray(w_mem_kv)[0].reshape(KT, P, 2 * 512),
        "w_mix": np.concatenate(branch + gate, axis=2),
        "w_o": coltiles(np.asarray(w_o)[0]),
        "w_up": coltiles(np.asarray(w_up)[0]),
        "w_down": coltiles(np.asarray(w_down)[0]),
        "conv_w": np.asarray(conv_w)[0].reshape(4, 12, P).transpose(2, 1, 0).reshape(P, -1),
        "conv_s": conv_s.transpose(3, 2, 0, 1).reshape(P, -1),
        "dt_b": np.asarray(dt_bias), "a_log": np.asarray(a_log),
        "norm_w": np.asarray(gdn_norm_w).reshape(P, 1),
        "sinks": np.repeat(np.asarray(attn_sinks).reshape(8), ST).reshape(P, 1),
        "sinks_row": np.asarray(attn_sinks),
        "ln1": np.concatenate([np.asarray(a).reshape(KT, P).T for a in (ln1_g, ln1_b)], axis=1),
        "ln2": np.concatenate([np.asarray(ln2_g), np.asarray(ln2_b)]),
        "s0": np.asarray(state_gdn_s)[0].transpose(2, 1, 0, 3).reshape(P, -1),
        "ckT": ck.transpose(2, 0, 1), "cvT": cv.transpose(2, 0, 1), "cv": cv.transpose(1, 0, 2),
        "cmkT": cmk.transpose(0, 3, 2, 1).reshape(NB, P, -1),
        "cmv": cmv.reshape(NB, 2, P, 512).transpose(0, 2, 1, 3).reshape(NB, P, -1),
        "consts": shape_constants(),
    }
    outs = {"o_y": (TT, P, DM), "o_ps": (P, 512), "o_pconv": (P, 12, PAD), "o_pk": (P, P), "o_pv": (P, P),
            "o_pm": (P, 2, 1024), "o_ss": (P, H * NB * P), "o_sconv": (P, 12 * NB * PAD),
            "o_skT": (P, NB, P), "o_svT": (P, NB, P)}

    nc = bacc.Bacc("TRN2", target_bir_lowering=False, num_devices=1)
    arrays = {k: np.ascontiguousarray(v) for k, v in arrays.items()}
    args = {k: nc.dram_tensor(k, v.shape, F32, kind="ExternalInput").ap() for k, v in arrays.items()}
    args |= {k: nc.dram_tensor(k, v, F32, kind="ExternalOutput").ap() for k, v in outs.items()}
    build(nc, **args)
    r = run_bass_kernel_spmd(nc, [arrays], core_ids=[0]).results[0]

    y = r["o_y"].reshape(TOK, DM)
    pm = r["o_pm"].transpose(1, 0, 2).reshape(1, 1, 256, 2, H, P)
    s_kv = [r[k].transpose(1, 2, 0).reshape(1, NB, P, 2, 64) for k in ("o_skT", "o_svT")]
    return (y[:NP].reshape(1, NP, DM), y[NP:].reshape(NB, ST, DM),
            r["o_ps"].reshape(P, H, P).transpose(1, 0, 2).reshape(1, 1, H, P, P),
            r["o_pconv"].transpose(2, 1, 0).reshape(1, 1, PAD, 1536),
            r["o_pk"].T.reshape(1, 1, P, 2, 64), r["o_pv"].T.reshape(1, 1, P, 2, 64),
            pm[..., 0, :, :], pm[..., 1, :, :],
            r["o_ss"].reshape(P, H, NB, P).transpose(2, 1, 0, 3).reshape(1, NB, H, P, P),
            r["o_sconv"].reshape(P, 12, NB, PAD).transpose(2, 3, 1, 0).reshape(1, NB, PAD, 1536),
            s_kv[0], s_kv[1])
```

```python
from contextlib import ExitStack

import numpy as np
import concourse.bass as bass
from concourse import mybir

F32 = mybir.dt.float32
F32R = mybir.dt.float32r
ALU = mybir.AluOpType
ACT = mybir.ActivationFunctionType
AX = mybir.AxisListType

P = 128
DM = 1024
KT = DM // P
NP = 512
NB = 8
ST = 16
TOK = NP + NB * ST
HALF = TOK // 2
TT = TOK // P
H = 4
PAD = 3
SPAN = ST + PAD
QW = NP + PAD + NB * SPAN
CW = QW - PAD
HT = 14
DFF = 4096
FT = DFF // P
ALPHA = float(2.0 ** 0.25)
NEG = -1.0e30
BLK = 16

FFN_ORDER = (("up", 0), ("up", 1), ("down", 0), ("up", 2), ("down", 1), ("up", 3), ("down", 2), ("down", 3))

CONST_COLS = {}
_at = 0
for _name, _n in (("ident", P), ("ones", P), ("mean", P), ("cum_p", P), ("cum_s", P), ("neg_p", P), ("neg_s", P),
                  ("nstrict_p", P), ("nstrict_s", P), ("blk_s", P), ("bd16", P), ("off16", P), ("off32", P),
                  ("off64", P), ("win0", 256), ("win", 256), ("snew", 240), ("tokblk", NB)):
    CONST_COLS[_name] = (_at, _n)
    _at += _n
NCONST = _at


def shape_constants():
    c = np.zeros((P, NCONST), np.float32)
    j, i = np.arange(P)[:, None], np.arange(P)[None, :]
    same = (j // ST) == (i // ST)

    def put(name, v):
        a, n = CONST_COLS[name]
        c[:, a:a + n] = v

    put("ident", j == i)
    put("ones", 1.0)
    put("mean", 1.0 / P)
    put("cum_p", j <= i)
    put("cum_s", (j <= i) & same)
    put("neg_p", np.where(j <= i, 0.0, NEG))
    put("neg_s", np.where((j <= i) & same, 0.0, NEG))
    put("nstrict_p", np.where(j < i, -1.0, 0.0))
    put("nstrict_s", np.where((j < i) & same, -1.0, 0.0))
    put("blk_s", same)
    put("bd16", (j // BLK) == (i // BLK))
    for s in (16, 32, 64):
        put(f"off{s}", (j // (2 * s) == i // (2 * s)) & (j // s % 2 == 0) & (i // s % 2 == 1))
    row, key = np.arange(P)[:, None] // 64, np.arange(256)[None, :] // 64
    put("win0", np.where(key <= row, 0.0, NEG))
    put("win", np.where((key <= row + 2) & (key >= row), 0.0, NEG))
    x = np.arange(240)[None, :]
    put("snew", np.where((x >= 112) & (x < 128), 0.0, NEG))
    put("tokblk", np.arange(P)[:, None] // ST == np.arange(NB)[None, :])
    return c



def level_count(stage, level, t):
    if stage in ("y", "off"):
        return (TT - 1) * (level - 4) + t
    return TT * (level - 1) + t if level < 4 else 3 * TT + (TT - 1) * (level - 4) + t


ROUNDS = [("norm", _n) for _n in range(16)] + [("gcol", 0)]
for _t in range(TT):
    ROUNDS += [(_x, _t) for _x in ("qk", "grow", "brow", "ktr", "vtr")] + ([("kk", _t - 1)] if _t else [])
ROUNDS += [("kk", TT - 1)] + [("ntr", _t) for _t in range(TT)]
for _l in range(1, 7):
    for _x in ("p", "pt", "x", "xt") if _l < 4 else ("y", "x", "xt"):
        ROUNDS += [(_x, level_count(_x, _l, _t)) for _t in range(TT if _l < 4 else TT - 1)
                   if (_x, _l) not in (("pt", 3), ("x", 6))]
for _t in range(4):
    ROUNDS += [("ks", _t), ("vn", _t), ("go", _t), ("ds", _t)]
ROUNDS += [("kst", 0), ("ks", 4), ("vn", 4), ("go", 4)] + [("ss", _n) for _n in range(8)]
ROUNDS += [("on", _n) for _n in range(8)]
ROUND = {r: _n for _n, r in enumerate(ROUNDS)}
DN_BANKS = 6

NPRE = 14
NFILL = 26 - NPRE


def fill_plan():
    steps, ends, done = {}, [], 0
    for r, (stage, n) in enumerate(ROUNDS):
        if stage == "norm":
            k = FILL_NORM
        elif stage in FILL_FIRST and n in FILL_FIRST[stage]:
            k = FILL_FIRST[stage][n]
        else:
            k = FILL_EACH.get(stage, 0)
        steps[r] = min(k, NFILL * KT - done)
        done += steps[r]
        while len(ends) < done // KT:
            ends.append(r)
    assert done == NFILL * KT, done
    return steps, ends


FILL_NORM = 2
FILL_EACH = {"grow": 2, "brow": 1, "ks": 2, "vn": 3, "go": 2, "ds": 1}
FILL_FIRST = {"gcol": {0: 4}, "qk": {0: 4}, "ntr": {0: 2}, "p": {0: 2, 5: 1, 10: 1}, "x": {0: 1, 5: 1, 10: 1},
              "y": {0: 3, 4: 3, 8: 3}}
FILL_STEPS, FILL_END = fill_plan()


def build(nc, xT, memT, w_h, w_ab, w_mem, w_mix, w_tiles, conv_w, conv_s, dt_b, a_log, norm_w,
          sinks, sinks_row, ln1, ln2, s0, ckT, cvT, cv, cmkT, cmv, consts,
          o_y, o_ps, o_pconv, o_pk, o_pv, o_pm, o_ss, o_sconv, o_skT, o_svT):
    with ExitStack() as ctx:
        base = -(-nc.sbuf_base // 32) * 32

        def place(name, at, cols, dtype=F32):
            return nc.alloc_sbuf_tensor_at(name, [P, cols], dtype, offset=base + 4 * at)

        CST, SMALL, XSB, ARENA, WORK, RING = 0, 2560, 3680, 8800, 33448, 47784

        semaphores = {}

        def sem(name):
            if name not in semaphores:
                semaphores[name] = ctx.enter_context(nc.semaphore(name))
            return semaphores[name]

        cst = place("cst", CST, NCONST)

        def const(name):
            a, n = CONST_COLS[name]
            return cst[:, a:a + n]

        ident = const("ident")
        x_sb = place("x_sb", XSB, KT * TOK)
        x3 = x_sb[:, :].rearrange("p (k t) -> p k t", k=KT)
        arena = place("arena", ARENA, HT * TOK + 12 * TOK + 12 * QW)
        h_sb = arena[:, 0:HT * TOK]
        h3 = h_sb.rearrange("p (k t) -> p k t", k=HT)
        Q0 = HT * TOK
        qkv3 = arena[:, Q0:Q0 + 12 * TOK].rearrange("p (k t) -> p k t", k=12)
        P0 = Q0 + 12 * TOK
        pad3 = arena[:, P0:P0 + 12 * QW].rearrange("p (k t) -> p k t", k=12)
        work = place("work", WORK, 4 * 2560 + 4096)
        ring = place("ring", RING, 4 * 1024)
        small = place("small", SMALL, 1120)

        def word_parts(name, high, low, words):
            return tuple(place(f"{name}_{x}", at, words, F32R)[:, :] for x, at in (("high", high), ("low", low)))

        xa_flat = word_parts("xa", WORK, WORK + KT * TOK, KT * TOK)
        xa = tuple(x.rearrange("p (k t) -> p k t", k=KT) for x in xa_flat)
        wa = [word_parts(f"wa{i}", WORK + 10240 + 2048 * i, WORK + 11264 + 2048 * i, DM) for i in range(2)]
        fill_w = ([place("fill_w", RING + 4096, DM)[:, :]]
                  + [work[:, 10240 + DM * i:10240 + DM * (i + 1)] for i in range(3)])

        def tiles(ap):
            return ap.rearrange("p (t h x) -> p t h x", h=H, x=P)

        NT = tiles(arena[:, P0:P0 + 2560])
        X = tiles(arena[:, P0 + 2560:P0 + 5120])
        XT = tiles(arena[:, P0 + 5120:P0 + 7680])
        PW = tiles(arena[:, Q0 + 8 * TOK:Q0 + 12 * TOK])
        PWT = tiles(work[:, 0:2560])
        KD = tiles(work[:, 2560:5120])
        VB = tiles(work[:, 5120:7680])
        QKD = tiles(work[:, 7680:10240])
        S0 = work[:, 10240:14336].rearrange("p (h b v) -> p h b v", h=H, b=NB)

        def heads(ap):
            return ap.rearrange("p (h x) -> p h x", h=H)

        conv_acc = [ring[:, 2048:2048 + CW], ring[:, 3072:3072 + CW]]
        conv_acc_streams = [a[:, NP + PAD:NP + PAD + NB * SPAN].rearrange("p (b s) -> p b s", b=NB)[:, :, 0:ST]
                            for a in (ring[:, 2048:3072], ring[:, 3072:4096])]
        rn_o = [work[:, 2560 + TOK * i:2560 + TOK * (i + 1)] for i in range(2)]
        sq = [ring[:, 0:TOK], ring[:, 1024:1024 + TOK]]
        rn = [ring[:, 2048:2048 + TOK], ring[:, 3072:3072 + TOK]]
        d_sb = [heads(ring[:, 0:512]), heads(ring[:, 512:1024])]
        eg_sb = [heads(ring[:, 1024:1536]), heads(ring[:, 1536:2048])]
        KB, DEC = X, XT
        S = heads(ring[:, 3072:3584])
        r_sb = heads(ring[:, 3584:4096])
        vn_sb = d_sb[0]
        kst_sb = d_sb[1]
        vm_sb = [ring[:, 1024:2048].rearrange("p (b x) -> p b x", b=NB),
                 ring[:, 2048:3072].rearrange("p (b x) -> p b x", b=NB)]

        taken = [0]

        def sm(n, **shape):
            a = taken[0]
            taken[0] += n
            assert taken[0] <= 1120
            ap = small[:, a:a + n]
            return ap.rearrange(f"p ({' '.join(shape)} x) -> p {' '.join(shape)} x", **shape) if shape else ap

        dtb, alog, nea = sm(4), sm(4), sm(4)
        nrm = sm(1)
        sinkb, sinkc, nsinkb, nsinkc = sm(8), sm(1), sm(8), sm(1)
        cw_sb = sm(48)
        ln1c = sm(16)
        cs_in, cs_out = sm(288), sm(288)
        ab = sm(40, t=TT)
        t_a, t_b, t_c, g_tok = (sm(20, t=TT) for _ in range(4))
        beta, e_b, glc, kdec, nbeg = (sm(20, t=TT) for _ in range(5))
        gcl = sm(40, t=TT)
        egl = sm(16, t=4)
        egs = sm(32, h=H)
        wab = sm(64, k=KT)
        eps = sm(1)
        nm, den, es, rden = ([sm(2) for _ in range(2)] for _ in range(4))
        stats, mv, rstd, nmr = (list(x) for x in zip(*[(sm(12), sm(2), sm(1), sm(1)) for _ in range(2)]))

        psum = ctx.enter_context(nc.psum_tensor("psum", [P, 4096], F32))
        ps = [psum[:, 512 * i:512 * i + 512] for i in range(8)]
        sc_ps = [psum[:, 1024 * i:1024 * i + 1024].rearrange("p (u s) -> p u s", u=2)[:, :, 0:256] for i in range(2)]

        W_Q, W_K, W_V, M_Q = 4, 8, 9, 10
        oG = qkv3[:, 0:4, :]
        oS = arena[:, P0:P0 + 2560].rearrange("p (m t) -> p m t", m=H)
        oX = arena[:, P0 + 2560:P0 + 5120].rearrange("p (m t) -> p m t", m=H)
        vtok = arena[:, P0 + 5120:P0 + 5760].rearrange("p (t x) -> p t x", t=TT)
        mkv = arena[:, P0 + 5760:P0 + 7808].rearrange("p (s x) -> p s x", s=2)
        mkT = work[:, 0:1024].rearrange("p (h s) -> p h s", h=H)
        ck_sb = work[:, 1024:2048].rearrange("p (b s) -> p b s", b=NB)
        cv_sb = work[:, 2048:3072].rearrange("p (b s) -> p b s", b=NB)
        sm_sb = [work[:, 3072 + 512 * i:3584 + 512 * i].rearrange("p (u s) -> p u s", u=2) for i in range(2)]
        pT_sb = [work[:, 4096 + 512 * i:4608 + 512 * i].rearrange("p (u s q) -> p u s q", u=2, s=2)
                 for i in range(2)]
        qs_sb = work[:, 5120:5632].rearrange("p (b m t) -> p b m t", b=NB, m=4)
        mem_sb = work[:, 6144:8192].rearrange("p (k t) -> p k t", k=KT)
        cm = [work[:, 6144 + 4096 * i:10240 + 4096 * i].rearrange("p (e w x) -> p e w x", e=2, w=2)
              for i in range(2)]

        def parts(name, high, low, cols):
            return tuple(place(f"{name}_{x}", at, cols, F32R)[:, :].rearrange("p (k t) -> p k t", t=TOK)
                         for x, at in (("high", high), ("low", low)))

        xp = parts("x", ARENA + Q0 + 2560, XSB, KT * TOK)
        oh = place("o_high", ARENA, 12 * TOK, F32R)[:, :].rearrange("p (b k t) -> p b k t", b=3, t=TOK)
        op = [(oh[:, br], place(f"o{br}_low", at, 4 * TOK, F32R)[:, :].rearrange("p (k t) -> p k t", t=TOK))
              for br, at in enumerate((ARENA + Q0, ARENA + P0, ARENA + P0 + 2560))]
        mp_ = parts("merged", WORK, WORK + 5120, KT * TOK)
        RAWN = 12 * P
        JOBS, TILES = 24, 8 + 2 * FT
        raw = [place(f"raw{i}", 50136 + RAWN * i, RAWN)[:, :] for i in range(2)]
        w_high, w_low = ([place(f"w{i}_{x}", at + d, RAWN, F32R)[:, :] for i, at in enumerate((WORK + 10240, 46760))]
                         for x, d in (("high", 0), ("low", RAWN)))
        w_parts = list(zip(w_high, w_low))
        sg = [arena[:, P0 + 5120 + TOK * i:P0 + 5120 + TOK * (i + 1)] for i in range(2)]
        gated = [arena[:, P0 + 6400 + TOK * i:P0 + 6400 + TOK * (i + 1)] for i in range(2)]
        y_flat = arena[:, 0:KT * TOK]
        y3 = y_flat.rearrange("p (k t) -> p k t", k=KT)
        x1 = parts("x1", XSB, ARENA + Q0 + 2560, KT * TOK)
        hid = [parts("hid0", WORK, WORK + 5120, KT * TOK), parts("hid1", ARENA + 5120, ARENA + P0, KT * TOK)]
        relu = [arena[:, P0 + 5120 + TOK * i:P0 + 5120 + TOK * (i + 1)] for i in range(2)]
        xn = [work[:, 1024 * i:1024 * (i + 1)] for i in range(2)]
        ln2gb = work[:, 2048:4096]
        merged_sum = place("merged_sum", ARENA + 12 * TOK, TOK)[:, :]

        def flat_parts(p):
            return tuple(x.rearrange("p k t -> p (k t)") for x in p)

        xp_flat, mp_flat, hid_flat = flat_parts(xp), flat_parts(mp_), [flat_parts(x) for x in hid]

        block = ctx.enter_context(nc.Block())

        UNITS = ([("wp", t, m) for t in range(4) for m in range(4)] + [("ws", 0, p) for p in range(4)]
                 + [u for t in range(4) for u in (("mp", t, 0), ("mp", t, 1), ("ms", 0, t))])
        NU = len(UNITS)
        W_SCALE, M_SCALE = 64 ** -0.5, P ** -0.5

        def cols(ap3, c, n=TOK):
            return ap3[:, bass.ds(c * n, n)]

        def stream(ap):
            return ap[:, NP:TOK].rearrange("p (b s) -> p b s", b=NB)

        def padded(row):
            return row[:, PAD:PAD + NP], row[:, PAD + NP:QW].rearrange("p (b s) -> p b s", b=NB)[:, :, PAD:]

        def halves_of(dst, b0, split):
            if not split:
                return [(dst[:, 0:HALF], ps[b0][:, 0:HALF]), (dst[:, HALF:TOK], ps[b0 + 1][:, 0:HALF])]
            prompt, streams = padded(dst)
            return [(prompt[:, 0:HALF], ps[b0][:, 0:HALF]), (prompt[:, HALF:NP], ps[b0 + 1][:, 0:NP - HALF]),
                    (streams, ps[b0 + 1][:, NP - HALF:HALF].rearrange("p (b s) -> p b s", b=NB))]

        def wtile(w, n):
            return w[bass.ds(n, 1), :, :].rearrange("a p x -> (a p) x")

        @block.sync
        def _(sp):
            def load(dst, src, name):
                sp.dma_start(dst, src).then_inc(sem(name), 16)

            for j in range(2):
                c = slice(4 * j * TOK, 4 * (j + 1) * TOK)
                load(x_sb[:, c], xT[:, c], f"x{j}_in")
                load(ring[:, j * 1024:(j + 1) * 1024], w_h[j], f"wa{j}_in")
            load(wab.rearrange("p k x -> p (k x)"), w_ab, "ab_in")
            load(cst[:, :], consts, "cst_in")
            for dst, src in ((dtb, dt_b.to_broadcast([P, 4])), (alog, a_log.to_broadcast([P, 4])), (nrm, norm_w),
                             (cw_sb, conv_w), (ln1c, ln1), (sinkb, sinks_row.to_broadcast([P, 8])),
                             (sinkc, sinks), (cs_in, conv_s)):
                load(dst, src, "par_in")
            with sp.Fori(1, NPRE // 2) as i:
                for s in range(2):
                    sp.wait_ge(sem("wa_high"), 2 * i - 1 + s)
                    sp.wait_ge(sem("wa_low"), 2 * i - 1 + s)
                    load(ring[:, s * 1024:(s + 1) * 1024], wtile(w_h, 2 * i + s), f"wa{s}_in")

            def fill_load(f):
                if f == 1:
                    sp.wait_ge(sem("h_mm"), NPRE)
                if f >= 4:
                    sp.wait_ge(sem("fill_mm"), f - 3)
                load(fill_w[f % 4], w_h[NPRE + f], f"fill{f % 4}_in")

            for f in range(4):
                fill_load(f)
            sp.wait_ge(sem("cs_out"), 1)
            sp.dma_start(o_pconv, pad3[:, :, NP:NP + PAD]).then_inc(sem("conv_st"), 16)
            sp.dma_start(o_sconv, cs_out).then_inc(sem("conv_st"), 16)
            for f in range(4, NFILL):
                fill_load(f)
            sp.wait_ge(sem("fill_mm"), NFILL)
            load(S0.rearrange("p h b v -> p (h b v)"), s0, "s0_in")
            sp.wait_ge(sem("fill_out"), NFILL)
            for out, c in ((o_pk, W_K), (o_pv, W_V)):
                sp.dma_start(out, h3[:, c, NP - P:NP]).then_inc(sem("out_st"), 16)
            for out, old, c in ((o_skT, ckT, W_K), (o_svT, cvT, W_V)):
                sp.dma_start(out[:, :, P - ST:], stream(h3[:, c, :])).then_inc(sem("out_st"), 16)
                sp.dma_start(out[:, :, 0:P - ST], old[:, :, ST:]).then_inc(sem("out_st"), 16)
            sp.wait_ge(sem("ds_out"), 4)
            sp.dma_start(o_ps, S.rearrange("p h x -> p (h x)")).then_inc(sem("ps_st"), 16)
            for n in range(8):
                sp.wait_ge(sem("ss_out"), n + 1)
                h, b = n // 2, n % 2 * 4
                sp.dma_start(o_ss[:, (h * NB + b) * P:(h * NB + b + 4) * P],
                             S0[:, h, b:b + 4, :].rearrange("p b v -> p (b v)")).then_inc(sem("ss_st"), 16)
            sp.wait_ge(sem("gdn_end"), 1)
            sp.wait_ge(sem("ss_st"), 16 * 8)
            sp.wait_ge(sem("ps_st"), 16)
            load(mem_sb.rearrange("p k t -> p (k t)"), memT, "mem_in")
            load(ck_sb, ckT, "ck_in")
            load(cv_sb, cv, "ck_in")
            for k in range(KT):
                if k >= 4:
                    sp.wait_ge(sem("mem_mm"), k - 3)
                load(ring[:, (k % 4) * 1024:(k % 4 + 1) * 1024], w_mem[k], f"wm{k % 4}_in")
            sp.wait_ge(sem("mkv_out_v"), 2)
            sp.wait_ge(sem("mkv_out_a"), 2)
            sp.dma_start(o_pm, mkv).then_inc(sem("pm_st"), 16)
            for p in range(4):
                if p == 0:
                    sp.wait_ge(sem("mem_mm"), KT)
                if p >= 2:
                    sp.wait_ge(sem("pv_mm"), UNITS.index(("ms", 0, p - 2)) + 1)
                for e in range(2):
                    load(cm[p % 2][:, e, 0, :], cmkT[2 * p + e], f"cm{p % 2}_in")
                    load(cm[p % 2][:, e, 1, :], cmv[2 * p + e], f"cm{p % 2}_in")
            def stream_in(n, slot, src, first=False):
                if not first:
                    sp.wait_ge(sem("high_out"), n - 1)
                    sp.wait_ge(sem("low_out"), n - 1)
                load(raw[slot][:, 0:src.shape[-1]], src, f"raw{slot}_in")

            sp.wait_ge(sem("mem_mm"), KT)
            sp.wait_ge(sem("qs_out"), 1)
            for s in range(2):
                stream_in(s, s, w_mix[s], first=True)
            with sp.Fori(1, JOBS // 2) as i:
                for s in range(2):
                    stream_in(2 * i + s, s, wtile(w_mix, 2 * i + s))
            with sp.Fori(0, TILES // 2) as i:
                for s in range(2):
                    stream_in(2 * i + (JOBS + s), s, wtile(w_tiles, 2 * i + s))
            sp.wait_ge(sem("tile_mm"), JOBS + TILES - 8)
            for j in range(2):
                load(ln2gb[:, j * DM:(j + 1) * DM], ln2[j:j + 1, :].to_broadcast([P, DM]), "ln2_in")
            for t in range(TT):
                sp.wait_ge(sem("final_out"), t + 1)
                sp.dma_start(o_y[t], xn[t % 2]).then_inc(sem(f"y{t % 2}_st"), 16)
            sp.wait_ge(sem("y0_st"), 48)
            sp.wait_ge(sem("y1_st"), 32)
            sp.wait_ge(sem("out_st"), 16 * 6)
            sp.wait_ge(sem("conv_st"), 32)

        @block.tensor
        def _(pe):
            def product3(b0, ksteps, weights, k0, act, arrived=None):
                halves = [(ps[b0][:, 0:HALF], slice(0, HALF)), (ps[b0 + 1][:, 0:HALF], slice(HALF, TOK))]
                for k in range(ksteps):
                    if arrived:
                        arrived(k)
                    c = slice((k0 + k) * P, (k0 + k + 1) * P)
                    for n, (weight, part) in enumerate(((0, 0), (0, 1), (1, 0))):
                        for out, half in halves:
                            mm = pe.matmul(out, weights[weight][:, c], act[part][:, k, half],
                                           start=k == 0 and n == 0, stop=k == ksteps - 1 and n == 2)
                return mm

            pe.wait_ge(sem("x0_in"), 16)
            pe.wait_ge(sem("x1_in"), 16)
            pe.wait_ge(sem("ab_in"), 16)
            for t in range(TT):
                for k in range(KT):
                    mm = pe.matmul(ps[7][:, t * 8:t * 8 + 8], x3[:, k, t * P:(t + 1) * P], wab[:, k, :],
                                   start=k == 0, stop=k == KT - 1)
            mm.then_inc(sem("ab_mm"), 1)

            def x_parts(k):
                pe.wait_ge(sem("xa_high"), k + 1)
                pe.wait_ge(sem("xa_low"), k + 1)

            def h_tiles(i, first):
                for s in range(2):
                    pe.wait_ge(sem("wa_high"), 2 * i + (s + 1))
                    pe.wait_ge(sem("wa_low"), 2 * i + (s + 1))
                    if not first:
                        pe.wait_ge(sem("h_out_v" if s == 0 else "h_out_a"), i)
                    product3(2 * s, KT, wa[s], 0, xa, x_parts if first and s == 0 else None
                             ).then_inc(sem("h_mm"), 1)

            h_tiles(0, True)
            with pe.Fori(1, NPRE // 2) as i:
                h_tiles(i, False)

            filled = [0, 0]

            def fill_before(stage, n):
                r = ROUND[stage, n]
                while filled[1] <= r:
                    for _ in range(FILL_STEPS[filled[1]]):
                        f, k = divmod(filled[0], KT)
                        if k == 0:
                            pe.wait_ge(sem(f"fill{f % 4}_in"), 16 * (f // 4 + 1))
                            if f:
                                pe.wait_ge(sem("fill_out"), f)
                        w = fill_w[f % 4][:, k * P:(k + 1) * P]
                        pe.matmul(ps[6][:, :], w, x3[:, k, 0:NP], start=k == 0, stop=k == KT - 1)
                        mm = pe.matmul(ps[7][:, 0:P], w, x3[:, k, NP:TOK], start=k == 0, stop=k == KT - 1)
                        if k == KT - 1:
                            mm.then_inc(sem("fill_mm"), 1)
                        filled[0] += 1
                    filled[1] += 1

            def bank(stage, n):
                fill_before(stage, n)
                r = ROUND[stage, n]
                if r >= DN_BANKS:
                    old, m = ROUNDS[r - DN_BANKS]
                    pe.wait_ge(sem(f"{old}_out"), m + 1)
                return ps[r % DN_BANKS]

            def per_head(stage, t, lhsT, rhs):
                b = heads(bank(stage, t)[:, :])
                for h in range(H):
                    mm = pe.matmul(b[:, h, :], lhsT(h), rhs(h), start=True, stop=True)
                mm.then_inc(sem(f"{stage}_mm"), 1)

            def per_head_transpose(stage, t, src):
                b = heads(bank(stage, t)[:, :])
                for h in range(H):
                    mm = pe.transpose(b[:, h, :], src(h), ident)
                mm.then_inc(sem(f"{stage}_mm"), 1)

            def tok(t):
                return slice(t * P, (t + 1) * P)

            pe.wait_ge(sem("cst_in"), 16)
            pe.wait_ge(sem("h_out_v"), NPRE // 2)
            pe.wait_ge(sem("h_out_a"), NPRE // 2)
            pe.wait_ge(sem("ab_out"), 1)
            for n in range(8):
                fill_before("norm", 2 * n)
                pe.wait_ge(sem("sq_out"), n + 1)
                for j, c in enumerate((slice(0, NP), slice(NP, TOK))):
                    b = bank("norm", 2 * n + j)
                    pe.matmul(b[:, 0:c.stop - c.start], const("ones"), sq[n % 2][:, c], start=True,
                              stop=True).then_inc(sem("norm_mm"), 1)
            b = bank("gcol", 0)
            pe.wait_ge(sem("g_out"), 1)
            for t in range(TT):
                kind = "p" if t < 4 else "s"
                pe.matmul(b[:, t * 8:t * 8 + 4], const(f"cum_{kind}"), g_tok[:, t, :], start=True, stop=True)
                mm = pe.matmul(b[:, t * 8 + 4:t * 8 + 8], const("ones" if t < 4 else "blk_s"), g_tok[:, t, :],
                               start=True, stop=True)
            mm.then_inc(sem("gcol_mm"), 1)
            fill_before("qk", 0)
            pe.wait_ge(sem("beta_out"), 1)
            pe.wait_ge(sem("qk_norm"), 8)
            pe.wait_ge(sem("silu_out"), 12)

            def key_products(t):
                fill_before("kk", t)
                pe.wait_ge(sem("brow_out"), t + 1)
                per_head("kk", t, lambda h: qkv3[:, 4 + h, tok(t)], lambda h: KB[:, t, h, :])

            for t in range(TT):
                cum = const("cum_p" if t < 4 else "cum_s")
                per_head("qk", t, lambda h: qkv3[:, 4 + h, tok(t)], lambda h: qkv3[:, h, tok(t)])
                per_head("grow", t, lambda h: g_tok[:, t, h:h + 1].to_broadcast([P, P]), lambda h: cum)
                per_head("brow", t, lambda h: beta[:, t, h:h + 1].to_broadcast([P, P]), lambda h: ident)
                per_head_transpose("ktr", t, lambda h: qkv3[:, 4 + h, tok(t)])
                per_head_transpose("vtr", t, lambda h: qkv3[:, 8 + h, tok(t)])
                if t:
                    key_products(t - 1)
            key_products(TT - 1)
            for t in range(TT):
                fill_before("ntr", t)
                pe.wait_ge(sem("nd_out"), t + 1)
                per_head_transpose("ntr", t, lambda h: PWT[:, t, h, :])

            def update(level, t):
                power = "p" if level < 4 else "y"
                if level < 6:
                    fill_before("x", level_count("x", level, t))
                pe.wait_ge(sem(f"{power}_out"), level_count(power, level, t) + 1)
                if level == 1:
                    pe.wait_ge(sem("x0_out"), t + 1)
                else:
                    pe.wait_ge(sem("xt_out"), level_count("xt", level - 1, t) + 1)
                if level < 6:
                    per_head("x", level_count("x", level, t), lambda h: XT[:, t, h, :], lambda h: PW[:, t, h, :])

            def update_t(level, t):
                per_head("xt", level_count("xt", level, t), lambda h: PW[:, t, h, :], lambda h: XT[:, t, h, :])

            for level in (1, 2, 3):
                for t in range(TT):
                    fill_before("p", level_count("p", level, t))
                    if level == 1:
                        pe.wait_ge(sem("ntr_out"), t + 1)
                    else:
                        pe.wait_ge(sem("p_out"), level_count("p", level - 1, t) + 1)
                        pe.wait_ge(sem("pt_out"), level_count("pt", level - 1, t) + 1)
                    per_head("p", level_count("p", level, t), lambda h: PWT[:, t, h, :], lambda h: PW[:, t, h, :])
                if level < 3:
                    for t in range(TT):
                        per_head("pt", level_count("pt", level, t), lambda h: PW[:, t, h, :], lambda h: PWT[:, t, h, :])
                for t in range(TT):
                    update(level, t)
                for t in range(TT):
                    update_t(level, t)
            for level in (4, 5, 6):
                for t in range(TT - 1):
                    fill_before("y", level_count("y", level, t))
                    pe.wait_ge(sem("off_out"), level_count("off", level, t) + 1)
                    pe.wait_ge(sem("x_out"), level_count("x", level - 1, t) + 1)
                    per_head("y", level_count("y", level, t), lambda h: PWT[:, t, h, :], lambda h: X[:, t, h, :])
                for t in range(TT - 1):
                    update(level, t)
                for t in range(TT - 1):
                    update_t(level, t)

            def new_values(t):
                fill_before("vn", t)
                pe.wait_ge(sem("r_out"), t + 1)
                per_head("vn", t, lambda h: XT[:, t, h, :], lambda h: r_sb[:, h, :])

            for t in range(TT - 1):
                fill_before("ks", t)
                pe.wait_ge(sem("xt_out"), level_count("xt", 6, t) + 1)
                pe.wait_ge(sem("s_zero"), 1)
                if t >= 1:
                    pe.wait_ge(sem("ds_out"), t)
                per_head("ks", t, lambda h: qkv3[:, 4 + h, tok(t)], lambda h: S[:, h, :])
                new_values(t)
                pe.wait_ge(sem("qe_out"), t + 1)
                pe.wait_ge(sem("qk_out"), t + 1)
                b = heads(bank("go", t)[:, :])
                pe.wait_ge(sem("vn_out"), t + 1)
                for h in range(H):
                    pe.matmul(b[:, h, :], S[:, h, :], qkv3[:, h, tok(t)], start=True, stop=False)
                    mm = pe.matmul(b[:, h, :], vn_sb[:, h, :], QKD[:, t, h, :], start=False, stop=True)
                mm.then_inc(sem("go_mm"), 1)
                pe.wait_ge(sem("ktr_out"), t + 1)
                per_head("ds", t, lambda h: KD[:, t, h, :], lambda h: vn_sb[:, h, :])
            pe.wait_ge(sem("s0_in"), 16)
            b = heads(bank("kst", 0)[:, :])
            for h in range(H):
                for j in range(NB):
                    c = slice(NP + j * ST, NP + (j + 1) * ST)
                    mm = pe.matmul(b[:, h, j * ST:(j + 1) * ST], S0[:, h, j, :], qkv3[:, 4 + h, c],
                                   start=True, stop=True)
            mm.then_inc(sem("kst_mm"), 1)
            pe.wait_ge(sem("kst_out"), 1)
            per_head_transpose("ks", 4, lambda h: kst_sb[:, h, :])
            pe.wait_ge(sem("xt_out"), level_count("xt", 3, 4) + 1)
            new_values(4)
            pe.wait_ge(sem("qe_out"), 5)
            pe.wait_ge(sem("qk_out"), 5)
            b = heads(bank("go", 4)[:, :])
            pe.wait_ge(sem("vn_out"), 5)
            for h in range(H):
                pe.matmul(b[:, h, :], vn_sb[:, h, :], QKD[:, 4, h, :], start=True, stop=False,
                          skip_group_check=True)
                for j in range(NB):
                    c = slice(NP + j * ST, NP + (j + 1) * ST)
                    mm = pe.matmul(b[:, h, j * ST:(j + 1) * ST], S0[:, h, j, :], qkv3[:, h, c], start=False,
                                   stop=j == NB - 1, skip_group_check=True)
            mm.then_inc(sem("go_mm"), 1)
            for n in range(8):
                h, j = n // 2, n % 2 * 4
                b = bank("ss", n)
                pe.wait_ge(sem("vm_out"), h + 1)
                pe.matmul(b[:, :], KD[:, 4, h, :], vm_sb[h % 2][:, j:j + 4, :].rearrange("p b x -> p (b x)"),
                          start=True, stop=True).then_inc(sem("ss_mm"), 1)
            for n in range(4):
                pe.wait_ge(sem("osq_out"), n + 1)
                for j, c in enumerate((slice(0, NP), slice(NP, TOK))):
                    b = bank("on", 2 * n + j)
                    pe.matmul(b[:, 0:c.stop - c.start], const("mean"), sq[n % 2][:, c], start=True,
                              stop=True).then_inc(sem("on_mm"), 1)

            pe.wait_ge(sem("gdn_end"), 1)
            pe.wait_ge(sem("mem_in"), 16)
            for k in range(KT):
                pe.wait_ge(sem(f"wm{k % 4}_in"), 16 * (k // 4 + 1))
                for st in range(2):
                    for half in range(2):
                        mm = pe.matmul(ps[2 * st + half][:, :], mem_sb[:, k, st * P:(st + 1) * P],
                                       ring[:, (k % 4) * 1024 + half * 512:(k % 4) * 1024 + half * 512 + 512],
                                       start=k == 0, stop=k == KT - 1)
                mm.then_inc(sem("mem_mm"), 1)
            for t in range(TT):
                b = ps[6 + t // 4][:, (t % 4) * P:(t % 4 + 1) * P]
                mm = pe.transpose(b, h3[:, W_V, tok(t)], ident)
            mm.then_inc(sem("vtok_mm"), 1)
            pe.wait_ge(sem("mkv_out_v"), 2)
            pe.wait_ge(sem("mkv_out_a"), 2)
            for h in range(H):
                for st in range(2):
                    b = ps[4 + h // 2][:, (h % 2) * 256 + st * P:(h % 2) * 256 + st * P + P]
                    mm = pe.transpose(b, mkv[:, st, h * P:(h + 1) * P], ident)
            mm.then_inc(sem("mkT_mm"), 1)

            def scores(n):
                kind, t, m = UNITS[n]
                if n >= 2:
                    pe.wait_ge(sem("exp_out"), n - 1)
                b = sc_ps[n % 2]
                if kind == "wp":
                    k0 = max(t - 1, 0) * P
                    for g in range(2):
                        r = slice(64 * g, 64 * g + 64)
                        mm = pe.matmul(b[:, g, :], h3[r, W_Q + m, tok(t)],
                                       h3[r, W_K, k0:k0 + 256], start=True, stop=True)
                if kind == "ws":
                    for e in range(2):
                        j = 2 * m + e
                        for g in range(2):
                            r = slice(64 * g, 64 * g + 64)
                            q = qs_sb[r, j, :, :].rearrange("p m t -> p (m t)")
                            pe.matmul(b[r, e, 0:P], q, ck_sb[r, j, :], start=True, stop=True)
                            mm = pe.matmul(b[r, e, P:], q, h3[r, W_K, NP:TOK],
                                           start=True, stop=True)
                if kind == "mp":
                    for u in range(2):
                        mm = pe.matmul(b[:, u, :], h3[:, M_Q + 2 * m + u, tok(t)],
                                       mkT[:, 2 * m + u, :], start=True, stop=True)
                if kind == "ms":
                    pe.wait_ge(sem(f"cm{m % 2}_in"), 64 * (m // 2 + 1))
                    for e in range(2):
                        for h in range(H):
                            mm = pe.matmul(b[32 * h:32 * h + 32, e, :],
                                           h3[:, M_Q + h, NP + 32 * m:NP + 32 * m + 32],
                                           cm[m % 2][:, e, 0, h * 256:h * 256 + 256], start=True, stop=True,
                                           tile_position=(0, 32 * h))
                mm.then_inc(sem("sc_mm"), 1)

            def probs_turned(n):
                pe.wait_ge(sem("prob_out"), n + 1)
                if n >= 2:
                    pe.wait_ge(sem("pT_out"), n - 1)
                b = ps[4 + n % 2]
                for u in range(2):
                    for st in range(2):
                        mm = pe.transpose(b[:, (2 * u + st) * P:(2 * u + st + 1) * P],
                                          sm_sb[n % 2][:, u, st * P:(st + 1) * P], ident)
                mm.then_inc(sem("pT_mm"), 1)

            def values(n):
                kind, t, m = UNITS[n]
                pe.wait_ge(sem("pT_out"), n + 1)
                if n >= 2:
                    pe.wait_ge(sem("at_out"), n - 1)
                b, pT = ps[6 + n % 2], pT_sb[n % 2]
                for u in range(2):
                    for st in range(2):
                        go = dict(start=st == 0, stop=st == 1)
                        if kind == "wp":
                            mm = pe.matmul(b[64 * u:64 * u + 64, 0:P], vtok[:, max(t - 1, 0) + st, 64 * u:64 * u + 64],
                                           pT[:, u, st, :], **go)
                        if kind == "mp":
                            c = 512 + (2 * m + u) * P
                            mm = pe.matmul(b[:, u * P:(u + 1) * P], mkv[:, st, c:c + P], pT[:, u, st, :], **go)
                    if kind == "ws":
                        for g in range(2):
                            r = slice(64 * g, 64 * g + 64)
                            pe.matmul(b[r, u * 64:u * 64 + 64], cv_sb[:, 2 * m + u, r], pT[:, u, 0, r],
                                      start=True, stop=False)
                            mm = pe.matmul(b[r, u * 64:u * 64 + 64], vtok[:, 4, r], pT[:, u, 1, r],
                                           start=False, stop=True)
                    if kind == "ms":
                        for h in range(H):
                            for st in range(2):
                                c = 512 * st + h * P
                                mm = pe.matmul(b[:, h * 32 + 16 * u:h * 32 + 16 * u + 16],
                                               cm[m % 2][:, u, 1, c:c + P],
                                               pT[:, u, st, 32 * h + 16 * u:32 * h + 16 * u + 16],
                                               start=st == 0, stop=st == 1)
                mm.then_inc(sem("pv_mm"), 1)

            pe.wait_ge(sem("ck_in"), 32)
            pe.wait_ge(sem("qs_out"), 1)
            pe.wait_ge(sem("vtok_out"), 2)
            pe.wait_ge(sem("mkT_out"), 2)
            for n in range(NU + 2):
                if n < NU:
                    scores(n)
                if 1 <= n <= NU:
                    probs_turned(n - 1)
                if n >= 2:
                    values(n - 2)

            pe.wait_ge(sem("at_out"), NU)

            def mix_jobs(i, first):
                for j in range(6):
                    s, b0, n = j % 2, 4 * (j % 2), 6 * i + j
                    pe.wait_ge(sem("high_out"), n + 1)
                    pe.wait_ge(sem("low_out"), n + 1)
                    if first and j < 3:
                        pe.wait_ge(sem("op_out"), 2 * (j + 1))
                    if first and j == 0:
                        pe.wait_ge(sem("xp_out"), 2)
                    if not first or j >= 2:
                        pe.wait_ge(sem("gated_out"), n - 1)
                    product3(b0, 4, w_parts[s], 0, op[j % 3])
                    product3(b0 + 2, KT, w_parts[s], 4, xp).then_inc(sem("tile_mm"), 1)

            mix_jobs(0, True)
            with pe.Fori(1, JOBS // 6) as i:
                mix_jobs(i, False)

            def column_tiles(i, n0, act, free, freed):
                for s in range(2):
                    n = 2 * i + (n0 + s)
                    pe.wait_ge(sem("high_out"), n + 1)
                    pe.wait_ge(sem("low_out"), n + 1)
                    pe.wait_ge(sem(free), freed + s)
                    product3(2 * s, KT, w_parts[s], 0, act).then_inc(sem("tile_mm"), 1)

            pe.wait_ge(sem("merged_parts"), 16)
            pe.wait_ge(sem("gated_out"), JOBS)
            column_tiles(0, JOBS, mp_, "gated_out", JOBS - 1)
            with pe.Fori(1, 4) as i:
                column_tiles(i, JOBS, mp_, "o_out", 2 * i - 1)

            def to_tokens(t, done):
                if t >= 2:
                    pe.wait_ge(sem(f"{done}_norm"), t - 1)
                for k in range(KT):
                    mm = pe.transpose(ps[2 * (t % 2) + k // 4][:, (k % 4) * P:(k % 4 + 1) * P], y3[:, k, tok(t)],
                                      ident)
                mm.then_inc(sem(f"{done}_turn"), 1)

            def to_channels(t):
                pe.wait_ge(sem("ln1_norm"), t + 1)
                if t >= 2:
                    pe.wait_ge(sem("ln1_out"), t - 1)
                for k in range(KT):
                    mm = pe.transpose(ps[4 + 2 * (t % 2) + k // 4][:, (k % 4) * P:(k % 4 + 1) * P],
                                      xn[t % 2][:, k * P:(k + 1) * P], ident)
                mm.then_inc(sem("ln1_back"), 1)

            pe.wait_ge(sem("y_done"), 1)
            for t in range(TT + 1):
                if t < TT:
                    to_tokens(t, "ln1")
                if t >= 1:
                    to_channels(t - 1)

            pe.wait_ge(sem("ln1_norm"), TT)
            pe.wait_ge(sem("x1_low"), TT)
            before = ("ln1_norm", TT - 1)
            for stage, (kind, chunk) in enumerate(FFN_ORDER):
                n0 = JOBS + 8 + 8 * stage
                act = x1 if kind == "up" else hid[chunk % 2]
                if kind == "down":
                    pe.wait_ge(sem("hid_low"), 8 * (chunk + 1))
                column_tiles(0, n0, act, before[0], before[1])
                with pe.Fori(1, 4) as i:
                    column_tiles(i, n0, act, kind + "_out", 2 * i + (8 * chunk - 1))
                before = (kind + "_out", 8 * chunk + 7)
            pe.wait_ge(sem("down_out"), 32)
            for t in range(TT):
                to_tokens(t, "ln2")

        @block.vector
        def _(dve):
            steps = [0]

            def then_wait(ins):
                steps[0] += 1
                ins.then_inc(sem("dve_step"), 1)
                dve.wait_ge(sem("dve_step"), steps[0])

            def bc(ap, n):
                return ap.unsqueeze(2).to_broadcast([P, ap.shape[1], n])

            def flat(ap):
                return ap.rearrange("p h x -> p (h x)")

            dve.memset(pad3[:, :, 0:PAD], 0.0)
            dve.memset(eps, 1e-6)
            for k in range(KT):
                dve.wait_ge(sem("xa_high"), k + 1)
                dve.tensor_tensor(xa[1][:, k], x3[:, k], xa[0][:, k], ALU.subtract).then_inc(sem("xa_low"), 1)
            dve.wait_ge(sem("par_in"), 16 * 8)
            dve.tensor_copy(pad3[:, :, NP + PAD:].rearrange("p k (b s) -> p k b s", b=NB)[:, :, :, 0:PAD],
                            cs_in.rearrange("p (k b s) -> p k b s", k=12, b=NB))
            dve.tensor_scalar(nsinkb, sinkb, -1.0, None, ALU.mult)
            dve.tensor_scalar(nsinkc, sinkc, -1.0, None, ALU.mult)
            dve.wait_ge(sem("ab_mm"), 1)
            then_wait(dve.tensor_copy(ab.rearrange("p t x -> p (t x)"), ps[7][:, 0:40]))
            then_wait(dve.tensor_tensor(t_a, ab[:, :, 0:4], dtb.unsqueeze(1).to_broadcast([P, TT, 4]), ALU.add))
            dve.scalar_tensor_tensor(t_b, t_a, -1.0, t_a, ALU.mult, ALU.max).then_inc(sem("ab_out"), 1)
            then_wait(dve.tensor_scalar(t_a, t_a, 0.0, None, ALU.max))
            dve.wait_ge(sem("ln_out"), 1)
            then_wait(dve.tensor_tensor(t_a, t_a, t_c, ALU.add))
            dve.scalar_tensor_tensor(g_tok, t_a, -1.0, nea.unsqueeze(1).to_broadcast([P, TT, 4]), ALU.mult,
                                     ALU.mult).then_inc(sem("g_out"), 1)
            then_wait(dve.tensor_scalar(e_b, e_b, 1.0, None, ALU.add))
            dve.reciprocal(beta, e_b).then_inc(sem("beta_out"), 1)

            def read_tile(i, dst, split):
                dve.wait_ge(sem("h_mm"), 2 * i + 1)
                for d, b in halves_of(dst, 0, split):
                    last = dve.tensor_copy(d, b)
                last.then_inc(sem("h_out_v"), 1)

            pad_flat = arena[:, P0:P0 + 12 * QW]

            def convolve(i, s, first):
                n = 2 * i + s
                if s == 0:
                    dve.wait_ge(sem("h_out_v"), i + 1)
                    dve.wait_ge(sem("h_out_a"), i + 1)
                if not first:
                    dve.wait_ge(sem("silu_out"), n - 1)
                acc = conv_acc[s]

                def tap(w):
                    return arena[:, bass.ds(n * QW + (P0 + w), CW)], cw_sb[:, bass.ds(4 * n + w, 1)]

                x0, w0 = tap(0)
                dve.tensor_scalar(acc, x0, w0, None, ALU.mult).then_inc(sem("conv_step"), 1)
                for w in range(1, 4):
                    dve.wait_ge(sem("conv_step"), 3 * n + w)
                    xw, ww = tap(w)
                    ins = dve.scalar_tensor_tensor(acc, xw, ww, acc, ALU.mult, ALU.add)
                    ins.then_inc(sem("conv_step" if w < 3 else "conv_out"), 1)

            def tile_and_conv(i, dst, split, first=False):
                read_tile(i, dst, split)
                for s in range(2):
                    convolve(i - 1, s, first)

            read_tile(0, cols(pad_flat, 0, QW), True)
            tile_and_conv(1, cols(pad_flat, 2, QW), True, first=True)
            with dve.Fori(2, 6) as i:
                tile_and_conv(i, cols(pad_flat, 2 * i, QW), True)
            tile_and_conv(6, h3[:, 0, :], False)
            for i in range(7, NPRE // 2):
                read_tile(i, h3[:, 2 * (i - 6), :], False)
            dve.tensor_copy(cs_out.rearrange("p (k b s) -> p k b s", k=12, b=NB),
                            pad3[:, :, NP + PAD:].rearrange("p k (b s) -> p k b s", b=NB)[:, :, :, ST:]
                            ).then_inc(sem("cs_out"), 1)

            for n in range(8):
                dve.wait_ge(sem("norm_out"), 2 * n + 2)
                then_wait(dve.reciprocal(rn[n % 2], rn[n % 2]))
                dve.scalar_tensor_tensor(qkv3[:, n, :], qkv3[:, n, :], P ** -0.5 if n < H else 1.0, rn[n % 2],
                                         ALU.mult, ALU.mult).then_inc(sem("qk_norm"), 1)

            def result(stage, n):
                dve.wait_ge(sem(f"{stage}_mm"), n + 1)
                return ps[ROUND[stage, n] % DN_BANKS]

            then_wait(dve.tensor_copy(gcl.rearrange("p t x -> p (t x)"), result("gcol", 0)[:, 0:40]))
            dve.tensor_tensor(glc, gcl[:, :, 4:8], gcl[:, :, 0:4], ALU.subtract).then_inc(sem("gcol_out"), 1)
            dve.wait_ge(sem("ecol_out"), 2)
            then_wait(dve.scalar_tensor_tensor(nbeg, beta, -1.0, nbeg, ALU.mult, ALU.mult))

            dve.wait_ge(sem("conv_st"), 32)

            def lower_part(t):
                dve.tensor_tensor(NT[:, t], heads(result("kk", t)[:, :]), DEC[:, t], ALU.mult
                                  ).then_inc(sem("kk_out"), 1)

            for t in range(TT):
                b = heads(result("grow", t)[:, :])
                mask = const("neg_p" if t < 4 else "neg_s")
                if t >= 2:
                    dve.wait_ge(sem("dec_out"), t - 1)
                then_wait(dve.tensor_tensor(d_sb[t % 2], b, bc(gcl[:, t, 0:4], P), ALU.subtract))
                dve.tensor_tensor(d_sb[t % 2], d_sb[t % 2], mask.unsqueeze(1).to_broadcast([P, H, P]),
                                  ALU.min).then_inc(sem("dmin_out"), 1)
                dve.tensor_tensor(KB[:, t], qkv3[:, 4:8, t * P:(t + 1) * P], heads(result("brow", t)[:, :]),
                                  ALU.mult).then_inc(sem("brow_out"), 1)
                dve.tensor_tensor(KD[:, t], heads(result("ktr", t)[:, :]), bc(kdec[:, t, :], P),
                                  ALU.mult).then_inc(sem("ktr_out"), 1)
                dve.tensor_tensor(VB[:, t], heads(result("vtr", t)[:, :]), bc(beta[:, t, :], P),
                                  ALU.mult).then_inc(sem("vtr_out"), 1)
                e = eg_sb[t % 2]
                dve.wait_ge(sem("grow_out"), t + 1)
                if t < 4:
                    dve.tensor_copy(egl[:, t, :].unsqueeze(2), e[:, :, P - 1:P])
                else:
                    dve.tensor_copy(egs, e[:, :, ST - 1::ST])
                q = qkv3[:, 0:4, t * P:(t + 1) * P]
                b = heads(result("qk", t)[:, :])
                dve.tensor_tensor(q, q, e, ALU.mult).then_inc(sem("qe_out"), 1)
                dve.wait_ge(sem("dec_out"), t + 1)
                dve.tensor_tensor(QKD[:, t], b, DEC[:, t], ALU.mult).then_inc(sem("qk_out"), 1)
                if t:
                    lower_part(t - 1)
            lower_part(TT - 1)

            for level in range(1, 7):
                tt = TT if level < 4 else TT - 1
                if level < 6:
                    for t in range(tt):
                        if level == 1:
                            dve.wait_ge(sem("x0_out"), t + 1)
                        b = result("x", level_count("x", level, t))
                        dve.tensor_tensor(X[:, t], X[:, t], heads(b[:, :]), ALU.add).then_inc(sem("x_out"), 1)
                for t in range(tt):
                    b = result("xt", level_count("xt", level, t))
                    dve.tensor_tensor(XT[:, t], XT[:, t], heads(b[:, :]), ALU.add).then_inc(sem("xt_out"), 1)
                if level == 1:
                    then_wait(dve.memset(S, 0.0))
                    dve.sem_inc(sem("s_zero"), 1)

            def residual(t):
                b = heads(result("ks", t)[:, :])
                dve.tensor_tensor(r_sb, b, bc(nbeg[:, t, :], P), ALU.mult).then_inc(sem("ks_out"), 1)
                dve.wait_ge(sem("ks_out"), t + 1)
                dve.tensor_tensor(r_sb, r_sb, VB[:, t], ALU.add).then_inc(sem("r_out"), 1)

            for t in range(TT - 1):
                residual(t)
                b = heads(result("ds", t)[:, :])
                then_wait(dve.tensor_tensor(S, S, bc(egl[:, t, :], P), ALU.mult))
                dve.tensor_tensor(S, S, b, ALU.add).then_inc(sem("ds_out"), 1)

            def stream_states(h):
                for n in (2 * h, 2 * h + 1):
                    j = n % 2 * 4
                    state = S0[:, h, j:j + 4, :]
                    b = result("ss", n)[:, :].rearrange("p (b v) -> p b v", b=4)
                    then_wait(dve.tensor_tensor(state, state, bc(egs[:, h, j:j + 4], P), ALU.mult))
                    dve.tensor_tensor(state, state, b, ALU.add).then_inc(sem("ss_out"), 1)

            residual(4)
            dve.wait_ge(sem("vn_out"), 5)
            for h in range(H):
                if h >= 2:
                    dve.wait_ge(sem("ss_mm"), 2 * h - 2)
                dve.tensor_tensor(vm_sb[h % 2], vn_sb[:, h, :].unsqueeze(1).to_broadcast([P, NB, P]),
                                  const("tokblk").unsqueeze(2).to_broadcast([P, NB, P]), ALU.mult
                                  ).then_inc(sem("vm_out"), 1)
                if h >= 1:
                    stream_states(h - 1)
            stream_states(H - 1)
            for n in range(4):
                dve.wait_ge(sem("on_out"), 2 * n + 2)
                then_wait(dve.reciprocal(rn_o[n % 2], rn_o[n % 2]))
                then_wait(dve.scalar_tensor_tensor(oG[:, n, :], oG[:, n, :], nrm[:, 0:1], rn_o[n % 2],
                                                   ALU.mult, ALU.mult))
                if n == 0:
                    dve.wait_ge(sem("z_out"), 1)
                dve.tensor_tensor(oG[:, n, :], oG[:, n, :], h3[:, n, :], ALU.mult).then_inc(sem("og_out"), 1)
            dve.wait_ge(sem("og_out"), 4)
            dve.sem_inc(sem("gdn_end"), 1)

            dve.wait_ge(sem("mem_mm"), KT)
            for st in range(2):
                dve.tensor_copy(mkv[:, st, 0:512], ps[2 * st][:, :]).then_inc(sem("mkv_out_v"), 1)
            dve.wait_ge(sem("vtok_mm"), 1)
            dve.tensor_copy(vtok[:, 0:4, :].rearrange("p t x -> p (t x)"), ps[6][:, :]).then_inc(sem("vtok_out"), 1)
            dve.tensor_copy(vtok[:, 4, :], ps[7][:, 0:P]).then_inc(sem("vtok_out"), 1)
            dve.wait_ge(sem("mkT_mm"), 1)
            for j in range(2):
                dve.tensor_copy(mkT[:, 2 * j:2 * j + 2, :].rearrange("p h s -> p (h s)"), ps[4 + j][:, :]
                                ).then_inc(sem("mkT_out"), 1)

            def front(n):
                kind, t, m = UNITS[n]
                dve.wait_ge(sem("sc_mm"), n + 1)
                b = sc_ps[n % 2]
                s, neg = sm_sb[n % 2], nm[n % 2]
                if kind in ("mp", "ms"):
                    then_wait(dve.tensor_reduce(neg, b, AX.X, ALU.max, negate=True))
                    dve.tensor_scalar(neg, neg, M_SCALE, None, ALU.mult).then_inc(sem("nm_out"), 1)
                    return
                if n >= 2:
                    dve.wait_ge(sem("pT_mm"), n - 1)
                if kind == "wp":
                    mask = const("win0" if t == 0 else "win")
                    then_wait(dve.scalar_tensor_tensor(s, b, W_SCALE, mask.unsqueeze(1).to_broadcast([P, 2, 256]),
                                                       ALU.mult, ALU.add))
                    sink, nsink = sinkb[:, m::4], nsinkb[:, m::4]
                else:
                    dve.tensor_scalar(s[:, :, 0:P], b[:, :, 0:P], W_SCALE, None, ALU.mult)
                    for e in range(2):
                        x = 112 - ST * (2 * m + e)
                        last = dve.scalar_tensor_tensor(s[:, e, P:], b[:, e, P:], W_SCALE,
                                                        const("snew")[:, x:x + P], ALU.mult, ALU.add)
                    then_wait(last)
                    sink, nsink = sinkc.to_broadcast([P, 2]), nsinkc.to_broadcast([P, 2])
                then_wait(dve.tensor_reduce(neg, s, AX.X, ALU.max, negate=True))
                then_wait(dve.tensor_tensor(neg, neg, nsink, ALU.min))
                dve.tensor_tensor(es[n % 2], neg, sink, ALU.add).then_inc(sem("nm_out"), 1)

            def back(n):
                i = n % 2
                dve.wait_ge(sem("exp_out"), n + 1)
                if UNITS[n][0] in ("wp", "ws"):
                    then_wait(dve.tensor_tensor(den[i], den[i], es[i], ALU.add))
                then_wait(dve.reciprocal(rden[i], den[i]))
                dve.tensor_tensor(sm_sb[i], sm_sb[i], rden[i].unsqueeze(2).to_broadcast([P, 2, 256]), ALU.mult
                                  ).then_inc(sem("prob_out"), 1)

            for n in range(NU + 1):
                if n < NU:
                    front(n)
                if n >= 1:
                    back(n - 1)

            def low_part(n, slot, width=8 * P):
                dve.wait_ge(sem("high_out"), n + 1)
                dve.tensor_tensor(w_low[slot][:, 0:width], raw[slot][:, 0:width], w_high[slot][:, 0:width],
                                  ALU.subtract).then_inc(sem("low_out"), 1)

            def outputs_low(br, raw_o):
                dve.wait_ge(sem("oh_out"), br + 1)
                dve.tensor_tensor(op[br][1], raw_o, op[br][0], ALU.subtract).then_inc(sem("op_out"), 2)

            dve.wait_ge(sem("xh_out"), 1)
            dve.tensor_tensor(xp[1], x3, xp[0], ALU.subtract).then_inc(sem("xp_out"), 2)
            low_part(0, 0, RAWN)
            outputs_low(0, oG)
            outputs_low(1, oS)
            outputs_low(2, oX)

            def merge(i, first, last):
                for j in range(6):
                    s, br, n = j % 2, j % 3, 6 * i + j
                    low_part(n + 1, 1 - s, 8 * P if last and j == 5 else RAWN)
                    c = 2 * i + j // 3
                    g, b0, total = sg[s], 4 * s, merged_sum
                    dve.wait_ge(sem("sg_out"), n + 1)
                    if br == 0 and not (first and j == 0):
                        dve.wait_ge(sem("merged_parts"), 2 * c)
                    if br == 1 and not (first and j == 1):
                        dve.wait_ge(sem("merged_out"), c)
                    if br == 2:
                        dve.wait_ge(sem("merged_two"), c + 1)
                    to = total if br == 0 else gated[s]
                    dve.tensor_tensor(to[:, 0:HALF], ps[b0][:, 0:HALF], g[:, 0:HALF], ALU.mult)
                    dve.tensor_tensor(to[:, HALF:], ps[b0 + 1][:, 0:HALF], g[:, HALF:], ALU.mult
                                      ).then_inc(sem("gated_out"), 1)
                    if br:
                        dve.wait_ge(sem("gated_out"), n + 1)
                        dve.tensor_tensor(total, total, gated[s], ALU.add
                                          ).then_inc(sem("merged_two" if br == 1 else "merged_out"), 1)
                    if br == 2:
                        dve.wait_ge(sem("mh_out"), c + 1)
                        dve.tensor_tensor(cols(mp_flat[1], c), total, cols(mp_flat[0], c), ALU.subtract
                                          ).then_inc(sem("merged_parts"), 2)

            merge(0, True, False)
            with dve.Fori(1, 3) as i:
                merge(i, False, False)
            merge(3, False, True)

            def residuals(i, n0, name, done, skip_last=False):
                for s in range(2):
                    n = 2 * i + (n0 + s)
                    if not (skip_last and s == 1):
                        low_part(n + 1, 1 - s)
                    dve.wait_ge(sem("tile_mm"), n + 1)
                    y = cols(y_flat, 2 * i + s)
                    for h, c in ((0, slice(0, HALF)), (1, slice(HALF, TOK))):
                        b = ps[2 * s + h][:, 0:HALF]
                        if name == "o":
                            src = cols(xp_flat[0], 2 * i + s)
                            last = dve.scalar_tensor_tensor(y[:, c], src[:, c], ALPHA, b, ALU.mult, ALU.add)
                        else:
                            last = dve.scalar_tensor_tensor(y[:, c], y[:, c], ALPHA if name == "first" else 1.0, b,
                                                            ALU.mult, ALU.add)
                    last.then_inc(sem(done), 1)
                    if name == "o":
                        dve.wait_ge(sem(done), 2 * i + s + 1)
                        dve.scalar_tensor_tensor(y, cols(xp_flat[1], 2 * i + s), ALPHA, y, ALU.mult, ALU.add)

            dve.wait_ge(sem("gated_out"), JOBS)
            with dve.Fori(0, 4) as i:
                residuals(i, JOBS, "o", "o_out")
            then_wait(dve.memset(sg[0][:, 0:1], 0.0))
            dve.sem_inc(sem("y_done"), 1)

            def token_stats(t, name):
                i = t % 2
                dve.wait_ge(sem(f"{name}_turn"), t + 1)
                for j in range(2):
                    last = dve.bn_stats(stats[i][:, 6 * j:6 * j + 6], ps[2 * i + j][:, :])
                then_wait(last)
                then_wait(dve.bn_aggr(mv[i], stats[i]))
                then_wait(dve.tensor_scalar(rstd[i], mv[i][:, 1:2], 1e-5, None, ALU.add))
                dve.sem_inc(sem("var_out"), 1)
                dve.wait_ge(sem("dev_out"), t + 1 + (TT if name == "ln2" else 0))
                then_wait(dve.reciprocal(rstd[i], rstd[i]))
                if name == "ln1" and t >= 2:
                    dve.wait_ge(sem("ln1_back"), t - 1)
                if name == "ln2" and t >= 2:
                    dve.wait_ge(sem(f"y{i}_st"), 16 * (t // 2))
                for j in range(2):
                    last = dve.tensor_scalar(xn[i][:, 512 * j:512 * j + 512], ps[2 * i + j][:, :], mv[i][:, 0:1],
                                             rstd[i], ALU.subtract, ALU.mult)
                last.then_inc(sem(f"{name}_norm"), 1)

            for t in range(TT + 1):
                if t < TT:
                    token_stats(t, "ln1")
                if t >= 1:
                    c = slice((t - 1) * P, t * P)
                    dve.wait_ge(sem("x1_high"), t)
                    dve.tensor_tensor(x1[1][:, :, c], y3[:, :, c], x1[0][:, :, c], ALU.subtract
                                      ).then_inc(sem("x1_low"), 1)

            def squares(i, n0, chunk):
                for s in range(2):
                    n, c = 2 * i + (n0 + s), 2 * i + (8 * chunk + s)
                    low_part(n + 1, 1 - s)
                    dve.wait_ge(sem("up_out"), c + 1)
                    dve.tensor_tensor(relu[s], relu[s], relu[s], ALU.mult).then_inc(sem("sqr_out"), 1)
                    dve.wait_ge(sem("hid_high"), c + 1)
                    dve.tensor_tensor(cols(hid_flat[chunk % 2][1], 2 * i + s), relu[s],
                                      cols(hid_flat[chunk % 2][0], 2 * i + s), ALU.subtract
                                      ).then_inc(sem("hid_low"), 1)

            for stage, (kind, chunk) in enumerate(FFN_ORDER):
                n0 = JOBS + 8 + 8 * stage
                if kind == "up":
                    with dve.Fori(0, 4) as i:
                        squares(i, n0, chunk)
                elif chunk < 3:
                    with dve.Fori(0, 4) as i:
                        residuals(i, n0, "first" if chunk == 0 else "more", "down_out")
                else:
                    with dve.Fori(0, 3) as i:
                        residuals(i, n0, "more", "down_out")
                    residuals(3, n0, "more", "down_out", skip_last=True)
            dve.wait_ge(sem("ln2_in"), 32)
            for t in range(TT):
                i = t % 2
                token_stats(t, "ln2")
                dve.wait_ge(sem("ln2_norm"), t + 1)
                then_wait(dve.tensor_tensor(xn[i], xn[i], ln2gb[:, 0:DM], ALU.mult))
                dve.tensor_tensor(xn[i], xn[i], ln2gb[:, DM:], ALU.add).then_inc(sem("final_out"), 1)

        @block.scalar
        def _(act):
            steps = [0]

            def then_wait(ins):
                steps[0] += 1
                ins.then_inc(sem("act_step"), 1)
                act.wait_ge(sem("act_step"), steps[0])

            for k in range(KT):
                act.wait_ge(sem(f"x{k // 4}_in"), 16)
                act.copy(xa[0][:, k], x3[:, k]).then_inc(sem("xa_high"), 1)

            def first_high(i, s, first=False):
                act.wait_ge(sem(f"wa{s}_in"), 16 * (i + 1))
                if not first:
                    act.wait_ge(sem("h_mm"), 2 * i + (s - 1))
                act.copy(wa[s][0], ring[:, s * 1024:(s + 1) * 1024]).then_inc(sem("wa_high"), 1)

            for s in range(2):
                first_high(0, s, first=True)
            act.wait_ge(sem("par_in"), 16 * 8)
            act.activation(nea, alog, ACT.Exp)
            act.wait_ge(sem("ab_out"), 1)
            act.activation(e_b, ab[:, :, 4:8], ACT.Exp, scale=-1.0)
            then_wait(act.activation(t_b, t_b, ACT.Exp, scale=-1.0))
            act.activation(t_c, t_b, ACT.Ln, bias=1.0).then_inc(sem("ln_out"), 1)

            def read_tile(i, dst, split):
                act.wait_ge(sem("h_mm"), 2 * i + 2)
                for d, b in halves_of(dst, 2, split):
                    last = act.copy(d, b)
                last.then_inc(sem("h_out_a"), 1)

            def silu(i, s):
                act.wait_ge(sem("conv_out"), 2 * i + (s + 1))
                row = cols(arena[:, Q0:Q0 + 12 * TOK], 2 * i + s)
                act.activation(row[:, 0:NP], conv_acc[s][:, 0:NP], ACT.Silu)
                act.activation(stream(row), conv_acc_streams[s], ACT.Silu).then_inc(sem("silu_out"), 1)

            def odd_tile(i, dst, split, weights=True, silus=True):
                if weights:
                    first_high(i + 1, 0)
                if silus:
                    silu(i - 1, 0)
                read_tile(i, dst, split)
                if weights:
                    first_high(i + 1, 1)
                if silus:
                    silu(i - 1, 1)

            pad_flat = arena[:, P0:P0 + 12 * QW]
            odd_tile(0, cols(pad_flat, 1, QW), True, silus=False)
            with act.Fori(1, 6) as i:
                odd_tile(i, cols(pad_flat, 2 * i + 1, QW), True)
            odd_tile(6, h3[:, 1, :], False, weights=NPRE > 14)
            for i in range(7, NPRE // 2):
                odd_tile(i, h3[:, 2 * (i - 6) + 1, :], False, weights=i + 1 < NPRE // 2, silus=False)

            read = [0]

            def read_fills(stage, n):
                while read[0] < NFILL and FILL_END[read[0]] <= ROUND[stage, n]:
                    row = h3[:, NPRE - 12 + read[0], :]
                    read[0] += 1
                    act.wait_ge(sem("fill_mm"), read[0])
                    act.copy(row[:, 0:NP], ps[6][:, :])
                    act.copy(row[:, NP:TOK], ps[7][:, 0:P]).then_inc(sem("fill_out"), 1)

            def lengths(stage, n, to, used):
                if n >= 2:
                    act.wait_ge(sem(used), n - 1)
                for j, c in enumerate((slice(0, NP), slice(NP, TOK))):
                    read_fills(stage, 2 * n + j)
                    act.wait_ge(sem(f"{stage}_mm"), 2 * n + j + 1)
                    b = ps[ROUND[stage, 2 * n + j] % DN_BANKS][:, 0:c.stop - c.start]
                    act.activation(to[n % 2][:, c], b, ACT.Sqrt, bias=eps[:, 0:1]).then_inc(sem(f"{stage}_out"), 1)

            act.wait_ge(sem("silu_out"), 8)
            for n in range(8):
                if n >= 2:
                    act.wait_ge(sem("norm_mm"), 2 * n - 2)
                act.activation(sq[n % 2], qkv3[:, n, :], ACT.Square).then_inc(sem("sq_out"), 1)
                if n >= 1:
                    lengths("norm", n - 1, rn, "qk_norm")
            lengths("norm", 7, rn, "qk_norm")
            read_fills("gcol", 0)
            act.wait_ge(sem("gcol_out"), 1)
            act.activation(kdec, glc, ACT.Exp).then_inc(sem("ecol_out"), 1)
            act.activation(nbeg, gcl[:, :, 0:4], ACT.Exp).then_inc(sem("ecol_out"), 1)
            act.wait_ge(sem("norm_mm"), 16)
            for t in range(TT):
                read_fills("grow", t)
                act.wait_ge(sem("dmin_out"), t + 1)
                if t >= 2:
                    act.wait_ge(sem("qe_out"), t - 1)
                act.activation(eg_sb[t % 2], heads(ps[ROUND["grow", t] % DN_BANKS][:, :]), ACT.Exp
                               ).then_inc(sem("grow_out"), 1)
                act.activation(DEC[:, t], d_sb[t % 2], ACT.Exp).then_inc(sem("dec_out"), 1)

            def keep(stage, t, dst, after=None):
                read_fills(after or stage, t)
                act.wait_ge(sem(f"{after or stage}_mm"), t + 1)
                act.copy(dst, heads(ps[ROUND[stage, t] % DN_BANKS][:, :])).then_inc(sem(f"{stage}_out"), 1)

            for t in range(TT):
                keep("ntr", t, PW[:, t])
            for level in (1, 2, 3):
                for t in range(TT):
                    if level == 1:
                        act.wait_ge(sem("x0_out"), t + 1)
                    keep("p", level_count("p", level, t), PW[:, t], after="pt" if level < 3 else None)
                if level < 3:
                    for t in range(TT):
                        keep("pt", level_count("pt", level, t), PWT[:, t])
            for level in (4, 5, 6):
                for t in range(TT - 1):
                    keep("y", level_count("y", level, t), PW[:, t])
            assert read[0] >= 16 - NPRE
            act.wait_ge(sem("h_out_v"), NPRE // 2)
            act.wait_ge(sem("h_out_a"), NPRE // 2)
            act.wait_ge(sem("fill_out"), max(16 - NPRE, 1))
            act.activation(h3[:, 0:4, :], h3[:, 0:4, :], ACT.Silu).then_inc(sem("z_out"), 1)
            for t in range(TT):
                if t == 4:
                    keep("kst", 0, kst_sb)
                keep("vn", t, vn_sb)
                keep("go", t, oG[:, :, t * P:(t + 1) * P])
            read_fills("on", 0)
            act.wait_ge(sem("ss_mm"), 8)
            for n in range(4):
                if n >= 2:
                    act.wait_ge(sem("on_mm"), 2 * n - 2)
                act.activation(sq[n % 2], oG[:, n, :], ACT.Square).then_inc(sem("osq_out"), 1)
                if n >= 1:
                    lengths("on", n - 1, rn_o, "og_out")
            lengths("on", 3, rn_o, "og_out")

            act.wait_ge(sem("mem_mm"), KT)
            for st in range(2):
                act.copy(mkv[:, st, 512:1024], ps[2 * st + 1][:, :]).then_inc(sem("mkv_out_a"), 1)

            def exponentials(n):
                kind, t, m = UNITS[n]
                i = n % 2
                act.wait_ge(sem("nm_out"), n + 1)
                window = kind in ("wp", "ws")
                if not window and n >= 2:
                    act.wait_ge(sem("pT_mm"), n - 1)
                b = sc_ps[i]
                for u in range(2):
                    ins = act.activation(sm_sb[i][:, u, :], sm_sb[i][:, u, :] if window else b[:, u, :], ACT.Exp,
                                         bias=nm[i][:, u:u + 1], scale=1.0 if window else M_SCALE,
                                         accum_out=den[i][:, u:u + 1])
                if window:
                    ins = act.activation(es[i], es[i], ACT.Exp)
                ins.then_inc(sem("exp_out"), 1)

            def turned(n):
                act.wait_ge(sem("pT_mm"), n + 1)
                if n >= 2:
                    act.wait_ge(sem("pv_mm"), n - 1)
                act.copy(pT_sb[n % 2].rearrange("p u s q -> p (u s q)"), ps[4 + n % 2][:, :]
                         ).then_inc(sem("pT_out"), 1)

            def outputs(n):
                kind, t, m = UNITS[n]
                act.wait_ge(sem("pv_mm"), n + 1)
                b = ps[6 + n % 2]
                c = NP + 32 * m
                if kind == "wp":
                    ins = act.copy(oS[:, m, t * P:(t + 1) * P], b[:, 0:P])
                if kind == "mp":
                    ins = act.copy(oX[:, 2 * m:2 * m + 2, t * P:(t + 1) * P],
                                   b[:, 0:256].rearrange("p (u q) -> p u q", u=2))
                if kind == "ws":
                    ins = act.copy(oS[:, :, c:c + 32].rearrange("p m (e t) -> p m e t", e=2),
                                   b[:, 0:P].rearrange("p (e m t) -> p m e t", e=2, m=4))
                if kind == "ms":
                    ins = act.copy(oX[:, :, c:c + 32], b[:, 0:P].rearrange("p (h x) -> p h x", h=H))
                ins.then_inc(sem("at_out"), 1)

            for n in range(NU + 2):
                if n < NU:
                    exponentials(n)
                if 1 <= n <= NU:
                    turned(n - 1)
                if n >= 2:
                    outputs(n - 2)

            def high_part(n, slot, arrived, width=8 * P, first=False):
                act.wait_ge(sem(f"raw{slot}_in"), 16 * arrived)
                if not first:
                    act.wait_ge(sem("tile_mm"), n - 1)
                act.copy(w_high[slot][:, 0:width], raw[slot][:, 0:width]).then_inc(sem("high_out"), 1)

            act.wait_ge(sem("gdn_end"), 1)
            act.copy(xp[0], x3).then_inc(sem("xh_out"), 1)
            act.wait_ge(sem("pv_mm"), NU)
            act.wait_ge(sem("out_st"), 16 * 6)
            high_part(0, 0, 1, RAWN, first=True)
            act.wait_ge(sem("at_out"), NU)
            for br, o in enumerate((oG, oS, oX)):
                act.copy(op[br][0], o).then_inc(sem("oh_out"), 1)

            act.wait_ge(sem("pm_st"), 16)

            def gates(i, first, last):
                for j in range(6):
                    s, n = j % 2, 6 * i + j
                    high_part(n + 1, 1 - s, 3 * i + ((j + 1) // 2 + 1), 8 * P if last and j == 5 else RAWN,
                              first=first and j == 0)
                    act.wait_ge(sem("tile_mm"), n + 1)
                    if not first or j >= 2:
                        act.wait_ge(sem("gated_out"), n - 1)
                    act.activation(sg[s][:, 0:HALF], ps[4 * s + 2][:, 0:HALF], ACT.Sigmoid)
                    act.activation(sg[s][:, HALF:], ps[4 * s + 3][:, 0:HALF], ACT.Sigmoid
                                   ).then_inc(sem("sg_out"), 1)
                    if j % 3 == 2:
                        act.wait_ge(sem("merged_out"), 2 * i + (j // 3 + 1))
                        act.copy(cols(mp_flat[0], 2 * i + j // 3), merged_sum).then_inc(sem("mh_out"), 1)

            gates(0, True, False)
            with act.Fori(1, 3) as i:
                gates(i, False, False)
            gates(3, False, True)
            with act.Fori(0, 4) as i:
                for s in range(2):
                    high_part(2 * i + (JOBS + 1 + s), 1 - s, i + (JOBS // 2 + 1 + s))

            def deviation(t, n):
                act.wait_ge(sem("var_out"), n + 1)
                act.activation(rstd[t % 2], rstd[t % 2], ACT.Sqrt).then_inc(sem("dev_out"), 1)

            for t in range(TT + 1):
                if t < TT:
                    deviation(t, t)
                if t >= 1:
                    c = slice((t - 1) * P, t * P)
                    act.wait_ge(sem("ln1_back"), t)
                    for k in range(KT):
                        ins = act.activation(y3[:, k, c], ps[4 + 2 * ((t - 1) % 2) + k // 4][:, (k % 4) * P:(k % 4 + 1) * P],
                                             ACT.Identity, bias=ln1c[:, 8 + k:9 + k], scale=ln1c[:, k:k + 1])
                    ins.then_inc(sem("ln1_out"), 1)
                    act.wait_ge(sem("ln1_out"), t)
                    act.copy(x1[0][:, :, c], y3[:, :, c]).then_inc(sem("x1_high"), 1)

            def relus(i, n0, chunk, first=False):
                for s in range(2):
                    n, c = 2 * i + (n0 + s), 2 * i + (8 * chunk + s)
                    high_part(n + 1, 1 - s, i + (n0 // 2 + 1 + s))
                    act.wait_ge(sem("tile_mm"), n + 1)
                    if not first:
                        act.wait_ge(sem("hid_low"), c - 1)
                    act.activation(relu[s][:, 0:HALF], ps[2 * s][:, 0:HALF], ACT.Relu)
                    act.activation(relu[s][:, HALF:], ps[2 * s + 1][:, 0:HALF], ACT.Relu
                                   ).then_inc(sem("up_out"), 1)
                    act.wait_ge(sem("sqr_out"), c + 1)
                    act.copy(cols(hid_flat[chunk % 2][0], 2 * i + s), relu[s]).then_inc(sem("hid_high"), 1)

            for stage, (kind, chunk) in enumerate(FFN_ORDER):
                n0 = JOBS + 8 + 8 * stage
                if kind == "up":
                    relus(0, n0, chunk, first=chunk == 0)
                    with act.Fori(1, 4) as i:
                        relus(i, n0, chunk)
                else:
                    last = chunk == 3
                    with act.Fori(0, 3 if last else 4) as i:
                        for s in range(2):
                            high_part(2 * i + (n0 + s + 1), 1 - s, i + (n0 // 2 + 1 + s))
                    if last:
                        high_part(n0 + 7, 1, n0 // 2 + 4)
            for t in range(TT):
                deviation(t, TT + t)

        @block.gpsimd
        def _(pool):
            with pool.Fori(0, NPRE // 2) as i:
                for s in range(2):
                    pool.wait_ge(sem("wa_high"), 2 * i + (s + 1))
                    pool.tensor_tensor(wa[s][1], ring[:, s * 1024:(s + 1) * 1024], wa[s][0], ALU.subtract
                                       ).then_inc(sem("wa_low"), 1)
            pool.wait_ge(sem("cst_in"), 16)

            def masked(out, src, mask):
                return pool.tensor_tensor(out, src, const(mask).unsqueeze(1).to_broadcast([P, H, P]), ALU.mult)

            for t in range(TT):
                pool.wait_ge(sem("kk_out"), t + 1)
                masked(NT[:, t], NT[:, t], "nstrict_p" if t < 4 else "nstrict_s").then_inc(sem("nt_out"), 1)
                pool.wait_ge(sem("nt_out"), t + 1)
                masked(PWT[:, t], NT[:, t], "bd16").then_inc(sem("nd_out"), 1)
            for t in range(TT):
                pool.wait_ge(sem("ntr_out"), t + 1)
                one = ident.unsqueeze(1).to_broadcast([P, H, P])
                pool.tensor_tensor(X[:, t], PW[:, t], one, ALU.add)
                pool.tensor_tensor(XT[:, t], PWT[:, t], one, ALU.add).then_inc(sem("x0_out"), 1)
            for level, size in ((4, 16), (5, 32), (6, 64)):
                for t in range(TT - 1):
                    if level == 4:
                        pool.wait_ge(sem("p_mm"), level_count("p", 3, t) + 1)
                    else:
                        pool.wait_ge(sem("y_mm"), level_count("y", level - 1, t) + 1)
                    masked(PWT[:, t], NT[:, t], f"off{size}").then_inc(sem("off_out"), 1)
            pool.wait_ge(sem("gdn_end"), 1)
            for m in range(4):
                last = pool.tensor_copy(qs_sb[:, :, m, :], stream(h3[:, W_Q + m, :]))
            last.then_inc(sem("qs_out"), 1)


def kernel(x_prompt, x_sample, state_gdn_s, state_gdn_conv, cache_swa_k, cache_swa_v, cache_mem_k, cache_mem_v,
           mem_prompt, w_in, conv_w, a_log, dt_bias, gdn_norm_w, attn_sinks, w_mem_kv, w_branch, w_o,
           ln1_g, ln1_b, w_up, w_down, ln2_g, ln2_b):
    import concourse.bacc as bacc
    from concourse.bass_utils import run_bass_kernel_spmd

    def ktiles(a):
        return a.reshape(a.shape[0] // P, P, -1).transpose(1, 0, 2)

    def coltiles(a):
        k = a.shape[0] // P
        return a.reshape(k, P, -1, P).transpose(2, 1, 0, 3).reshape(-1, P, k * P)

    w_in, w_branch = np.asarray(w_in)[0], np.asarray(w_branch)[0]
    x = np.concatenate([np.asarray(x_prompt)[0], np.asarray(x_sample).reshape(NB * ST, DM)])
    order = [h * 64 + d for m in range(4) for h in (m, 4 + m) for d in range(64)]
    o = 1536
    w_a, w_z = w_in[:, o:o + 8], w_in[:, o + 8:o + 520]
    o += 520
    w_qs, w_ks, w_vs, w_qx, w_g = (w_in[:, o + a:o + b] for a, b in (
        (0, 512), (512, 640), (640, 768), (768, 1280), (1280, 1280 + 3 * DM)))
    gate = [coltiles(w_g[:, b * DM:(b + 1) * DM]) for b in range(3)]
    branch = [coltiles(w) for w in (w_branch[0], w_branch[1][order], w_branch[2])]
    up, down = np.asarray(w_up)[0], np.asarray(w_down)[0]
    ffn = {"up": [coltiles(up[:, c * DM:(c + 1) * DM]) for c in range(4)],
           "down": [coltiles(down[c * DM:(c + 1) * DM]) for c in range(4)]}
    ck, cv = (np.asarray(c)[0].reshape(NB, P, P) for c in (cache_swa_k, cache_swa_v))
    cmk, cmv = (np.asarray(c)[0].reshape(NB, 256, H, P) for c in (cache_mem_k, cache_mem_v))
    conv_s = np.asarray(state_gdn_conv)[0].reshape(NB, PAD, 12, P)
    arrays = {
        "xT": ktiles(x.T).reshape(P, -1),
        "memT": ktiles(np.asarray(mem_prompt)[0].T).reshape(P, -1),
        "w_h": coltiles(np.concatenate([w_in[:, :1536], w_z, w_qs[:, order], w_ks, w_vs, w_qx], axis=1)),
        "w_ab": ktiles(w_a).reshape(P, -1),
        "w_mem": np.asarray(w_mem_kv)[0].reshape(KT, P, 2 * 512),
        "w_mix": np.stack([np.concatenate([branch[b], gate[b]], axis=2) for b in range(3)], 1).reshape(-1, P, 12 * P),
        "w_tiles": np.concatenate([coltiles(np.asarray(w_o)[0])] + [ffn[kind][chunk] for kind, chunk in FFN_ORDER]),
        "conv_w": np.asarray(conv_w)[0].reshape(4, 12, P).transpose(2, 1, 0).reshape(P, -1),
        "conv_s": conv_s.transpose(3, 2, 0, 1).reshape(P, -1),
        "dt_b": np.asarray(dt_bias), "a_log": np.asarray(a_log),
        "norm_w": np.asarray(gdn_norm_w).reshape(P, 1),
        "sinks": np.repeat(np.asarray(attn_sinks).reshape(8), ST).reshape(P, 1),
        "sinks_row": np.asarray(attn_sinks),
        "ln1": np.concatenate([np.asarray(a).reshape(KT, P).T for a in (ln1_g, ln1_b)], axis=1),
        "ln2": np.concatenate([np.asarray(ln2_g), np.asarray(ln2_b)]),
        "s0": np.asarray(state_gdn_s)[0].transpose(2, 1, 0, 3).reshape(P, -1),
        "ckT": ck.transpose(2, 0, 1), "cvT": cv.transpose(2, 0, 1), "cv": cv.transpose(1, 0, 2),
        "cmkT": cmk.transpose(0, 3, 2, 1).reshape(NB, P, -1),
        "cmv": cmv.reshape(NB, 2, P, 512).transpose(0, 2, 1, 3).reshape(NB, P, -1),
        "consts": shape_constants(),
    }
    outs = {"o_y": (TT, P, DM), "o_ps": (P, 512), "o_pconv": (P, 12, PAD), "o_pk": (P, P), "o_pv": (P, P),
            "o_pm": (P, 2, 1024), "o_ss": (P, H * NB * P), "o_sconv": (P, 12 * NB * PAD),
            "o_skT": (P, NB, P), "o_svT": (P, NB, P)}

    nc = bacc.Bacc("TRN2", target_bir_lowering=False, num_devices=1)
    arrays = {k: np.ascontiguousarray(v) for k, v in arrays.items()}
    args = {k: nc.dram_tensor(k, v.shape, F32, kind="ExternalInput").ap() for k, v in arrays.items()}
    args |= {k: nc.dram_tensor(k, v, F32, kind="ExternalOutput").ap() for k, v in outs.items()}
    build(nc, **args)
    r = run_bass_kernel_spmd(nc, [arrays], core_ids=[0]).results[0]

    y = r["o_y"].reshape(TOK, DM)
    pm = r["o_pm"].transpose(1, 0, 2).reshape(1, 1, 256, 2, H, P)
    s_kv = [r[k].transpose(1, 2, 0).reshape(1, NB, P, 2, 64) for k in ("o_skT", "o_svT")]
    return (y[:NP].reshape(1, NP, DM), y[NP:].reshape(NB, ST, DM),
            r["o_ps"].reshape(P, H, P).transpose(1, 0, 2).reshape(1, 1, H, P, P),
            r["o_pconv"].transpose(2, 1, 0).reshape(1, 1, PAD, 1536),
            r["o_pk"].T.reshape(1, 1, P, 2, 64), r["o_pv"].T.reshape(1, 1, P, 2, 64),
            pm[..., 0, :, :], pm[..., 1, :, :],
            r["o_ss"].reshape(P, H, NB, P).transpose(2, 1, 0, 3).reshape(1, NB, H, P, P),
            r["o_sconv"].reshape(P, 12, NB, PAD).transpose(2, 3, 1, 0).reshape(1, NB, PAD, 1536),
            s_kv[0], s_kv[1])
```

```python
from contextlib import ExitStack

import numpy as np
import concourse.bass as bass
from concourse import mybir

F32 = mybir.dt.float32
F32R = mybir.dt.float32r
ALU = mybir.AluOpType
ACT = mybir.ActivationFunctionType
AX = mybir.AxisListType

P = 128
DM = 1024
KT = DM // P
NP = 512
NB = 8
ST = 16
TOK = NP + NB * ST
HALF = TOK // 2
TT = TOK // P
H = 4
PAD = 3
SPAN = ST + PAD
QW = NP + PAD + NB * SPAN
CW = QW - PAD
HT = 14
DFF = 4096
FT = DFF // P
ALPHA = float(2.0 ** 0.25)
NEG = -1.0e30
BLK = 16

FFN_ORDER = (("up", 0), ("up", 1), ("down", 0), ("up", 2), ("down", 1), ("up", 3), ("down", 2), ("down", 3))

CONST_COLS = {}
_at = 0
for _name, _n in (("ident", P), ("ones", P), ("mean", P), ("cum_p", P), ("cum_s", P), ("neg_p", P), ("neg_s", P),
                  ("nstrict_p", P), ("nstrict_s", P), ("blk_s", P), ("bd16", P), ("off16", P), ("off32", P),
                  ("off64", P), ("win0", 256), ("win", 256), ("snew", 240), ("tokblk", NB)):
    CONST_COLS[_name] = (_at, _n)
    _at += _n
NCONST = _at


def shape_constants():
    c = np.zeros((P, NCONST), np.float32)
    j, i = np.arange(P)[:, None], np.arange(P)[None, :]
    same = (j // ST) == (i // ST)

    def put(name, v):
        a, n = CONST_COLS[name]
        c[:, a:a + n] = v

    put("ident", j == i)
    put("ones", 1.0)
    put("mean", 1.0 / P)
    put("cum_p", j <= i)
    put("cum_s", (j <= i) & same)
    put("neg_p", np.where(j <= i, 0.0, NEG))
    put("neg_s", np.where((j <= i) & same, 0.0, NEG))
    put("nstrict_p", np.where(j < i, -1.0, 0.0))
    put("nstrict_s", np.where((j < i) & same, -1.0, 0.0))
    put("blk_s", same)
    put("bd16", (j // BLK) == (i // BLK))
    for s in (16, 32, 64):
        put(f"off{s}", (j // (2 * s) == i // (2 * s)) & (j // s % 2 == 0) & (i // s % 2 == 1))
    row, key = np.arange(P)[:, None] // 64, np.arange(256)[None, :] // 64
    put("win0", np.where(key <= row, 0.0, NEG))
    put("win", np.where((key <= row + 2) & (key >= row), 0.0, NEG))
    x = np.arange(240)[None, :]
    put("snew", np.where((x >= 112) & (x < 128), 0.0, NEG))
    put("tokblk", np.arange(P)[:, None] // ST == np.arange(NB)[None, :])
    return c



def level_count(stage, level, t):
    if stage in ("y", "off"):
        return (TT - 1) * (level - 4) + t
    return TT * (level - 1) + t if level < 4 else 3 * TT + (TT - 1) * (level - 4) + t


ROUNDS = [("norm", _n) for _n in range(16)] + [("gcol", 0)]
for _t in range(TT):
    ROUNDS += [(_x, _t) for _x in ("qk", "grow", "brow", "ktr", "vtr")] + ([("kk", _t - 1)] if _t else [])
ROUNDS += [("kk", TT - 1)] + [("ntr", _t) for _t in range(TT)]
for _l in range(1, 7):
    for _x in ("p", "pt", "x", "xt") if _l < 4 else ("y", "x", "xt"):
        ROUNDS += [(_x, level_count(_x, _l, _t)) for _t in range(TT if _l < 4 else TT - 1)
                   if (_x, _l) not in (("pt", 3), ("x", 6))]
SCAN = (("ks", 0), ("vn", 0), ("go", 0), ("ds", 0), ("ks", 1), ("kst", 0), ("on", 0), ("vn", 1), ("ks", 4),
        ("go", 1), ("ds", 1), ("vn", 4), ("ks", 2), ("on", 1), ("go", 4), ("vn", 2), ("on", 4), ("go", 2),
        ("ds", 2), ("ks", 3), ("on", 2), ("ss", 0), ("ss", 1), ("vn", 3), ("ss", 2), ("ss", 3), ("go", 3),
        ("vtok", 0), ("ss", 4), ("ss", 5), ("on", 3), ("ds", 3), ("mkT", 0), ("ss", 6), ("ss", 7))


def scan_count(stage, t):
    return [u for x, u in SCAN if x == stage].index(t)


ROUNDS += [(_x, scan_count(_x, _t)) for _x, _t in SCAN if _x not in ("vtok", "mkT")]
ROUND = {r: _n for _n, r in enumerate(ROUNDS)}
DN_BANKS = 6

NPRE = 14
NFILL = 26 - NPRE


def fill_plan():
    steps, ends, done = {}, [], 0
    for r, (stage, n) in enumerate(ROUNDS):
        if stage == "norm":
            k = FILL_NORM
        elif stage in FILL_FIRST and n in FILL_FIRST[stage]:
            k = FILL_FIRST[stage][n]
        else:
            k = FILL_EACH.get(stage, 0)
        steps[r] = min(k, NFILL * KT + 2 * KT - done)
        done += steps[r]
        while len(ends) < done // KT:
            ends.append(r)
    assert done == (NFILL + 2) * KT, done
    return steps, ends


FILL_NORM = 2
FILL_EACH = {"grow": 2, "brow": 1, "ks": 1, "vn": 1, "go": 1, "ds": 1}
FILL_FIRST = {"gcol": {0: 4}, "qk": {0: 4}, "kk": {4: 1}, "ntr": {0: 2}, "p": {0: 3, 5: 2, 10: 2},
              "x": {0: 1, 5: 1, 10: 1}, "pt": {n: 1 for n in (1, 2, 3, 4, 6, 7, 8, 9)},
              "xt": {0: 2, 5: 2, 10: 2, 15: 1, 19: 1}, "y": {0: 5, 4: 5, 8: 2}, "ks": {0: 0}, "vn": {0: 0}}
FILL_STEPS, FILL_END = fill_plan()


def build(nc, xT, memT, w_h, w_ab, w_mem, w_piece, w_mix, w_tiles, conv_w, conv_s, dt_b, a_log, norm_w,
          sinks, sinks_row, ln1, ln2, s0, ckT, cvT, cv, cmkT, cmv, consts,
          o_y, o_ps, o_pconv, o_pk, o_pv, o_pm, o_ss, o_sconv, o_skT, o_svT):
    with ExitStack() as ctx:
        base = -(-nc.sbuf_base // 32) * 32

        def place(name, at, cols, dtype=F32):
            return nc.alloc_sbuf_tensor_at(name, [P, cols], dtype, offset=base + 4 * at)

        CST, SMALL, XSB, ARENA, WORK, RING = 0, 2560, 3680, 8800, 33448, 47784

        semaphores = {}

        def sem(name):
            if name not in semaphores:
                semaphores[name] = ctx.enter_context(nc.semaphore(name))
            return semaphores[name]

        cst = place("cst", CST, NCONST)

        def const(name):
            a, n = CONST_COLS[name]
            return cst[:, a:a + n]

        ident = const("ident")
        x_sb = place("x_sb", XSB, KT * TOK)
        x3 = x_sb[:, :].rearrange("p (k t) -> p k t", k=KT)
        arena = place("arena", ARENA, HT * TOK + 12 * TOK + 12 * QW)
        h_sb = arena[:, 0:HT * TOK]
        h3 = h_sb.rearrange("p (k t) -> p k t", k=HT)
        Q0 = HT * TOK
        qkv3 = arena[:, Q0:Q0 + 12 * TOK].rearrange("p (k t) -> p k t", k=12)
        P0 = Q0 + 12 * TOK
        pad3 = arena[:, P0:P0 + 12 * QW].rearrange("p (k t) -> p k t", k=12)
        work = place("work", WORK, 4 * 2560 + 4096)
        ring = place("ring", RING, 4 * 1024)
        small = place("small", SMALL, 1120)

        def word_parts(name, high, low, words):
            return tuple(place(f"{name}_{x}", at, words, F32R)[:, :] for x, at in (("high", high), ("low", low)))

        xa_flat = word_parts("xa", WORK, WORK + KT * TOK, KT * TOK)
        xa = tuple(x.rearrange("p (k t) -> p k t", k=KT) for x in xa_flat)
        wa = [word_parts(f"wa{i}", WORK + 10240 + 2048 * i, WORK + 11264 + 2048 * i, DM) for i in range(2)]
        fill_w = ([place("fill_w", RING + 4096, DM)[:, :]]
                  + [work[:, 10240 + DM * i:10240 + DM * (i + 1)] for i in range(3)])

        def tiles(ap):
            return ap.rearrange("p (t h x) -> p t h x", h=H, x=P)

        NT = tiles(arena[:, P0:P0 + 2560])
        X = tiles(arena[:, P0 + 2560:P0 + 5120])
        XT = tiles(arena[:, P0 + 5120:P0 + 7680])
        PW = tiles(arena[:, Q0 + 8 * TOK:Q0 + 12 * TOK])
        PWT = tiles(work[:, 0:2560])
        KD = tiles(work[:, 2560:5120])
        VB = tiles(work[:, 5120:7680])
        QKD = tiles(work[:, 7680:10240])
        S0 = work[:, 10240:14336].rearrange("p (h b v) -> p h b v", h=H, b=NB)

        def heads(ap):
            return ap.rearrange("p (h x) -> p h x", h=H)

        conv_acc = [ring[:, 2048:2048 + CW], ring[:, 3072:3072 + CW]]
        conv_acc_streams = [a[:, NP + PAD:NP + PAD + NB * SPAN].rearrange("p (b s) -> p b s", b=NB)[:, :, 0:ST]
                            for a in (ring[:, 2048:3072], ring[:, 3072:4096])]
        rn_o = [ring[:, 512:1024], ring[:, 1024:1536]]
        sq_o = [ring[:, 1536:2048], work[:, 7680:8192]]
        sq = [ring[:, 0:TOK], ring[:, 1024:1024 + TOK]]
        rn = [ring[:, 2048:2048 + TOK], ring[:, 3072:3072 + TOK]]
        d_sb = [heads(ring[:, 0:512]), heads(ring[:, 512:1024])]
        eg_sb = [heads(ring[:, 1024:1536]), heads(ring[:, 1536:2048])]
        KB, DEC = X, XT
        S = heads(ring[:, 3072:3584])
        r_sb = heads(ring[:, 3584:4096])
        r_streams = heads(arena[:, P0 + 2048:P0 + 2560])
        vn_streams, kst_sb = heads(arena[:, P0 + 2560:P0 + 3072]), heads(arena[:, P0 + 3072:P0 + 3584])
        vn_sb = d_sb[0]
        vm_sb = [ring[:, 2048:3072].rearrange("p (b x) -> p b x", b=NB),
                 arena[:, P0 + 3584:P0 + 4608].rearrange("p (b x) -> p b x", b=NB)]

        taken = [0]

        def sm(n, **shape):
            a = taken[0]
            taken[0] += n
            assert taken[0] <= 1120
            ap = small[:, a:a + n]
            return ap.rearrange(f"p ({' '.join(shape)} x) -> p {' '.join(shape)} x", **shape) if shape else ap

        dtb, alog, nea = sm(4), sm(4), sm(4)
        nrm = sm(1)
        sinkb, sinkc, nsinkb, nsinkc = sm(8), sm(1), sm(8), sm(1)
        cw_sb = sm(48)
        ln1c = sm(16)
        cs_in, cs_out = sm(288), sm(288)
        ab = sm(40, t=TT)
        t_a, t_b, t_c, g_tok = (sm(20, t=TT) for _ in range(4))
        beta, e_b, glc, kdec, nbeg = (sm(20, t=TT) for _ in range(5))
        gcl = sm(40, t=TT)
        egl = sm(16, t=4)
        egs = sm(32, h=H)
        wab = sm(64, k=KT)
        eps = sm(1)
        nm, den, es, rden = ([sm(2) for _ in range(3)] for _ in range(4))
        stats, mv, rstd, nmr = (list(x) for x in zip(*[(sm(12), sm(2), sm(1), sm(1)) for _ in range(3)]))

        psum = ctx.enter_context(nc.psum_tensor("psum", [P, 4096], F32))
        ps = [psum[:, 512 * i:512 * i + 512] for i in range(8)]
        sc_ps = [psum[:, 1024 * i:1024 * i + 1024].rearrange("p (u s) -> p u s", u=2)[:, :, 0:256] for i in range(2)]

        W_Q, W_K, W_V, M_Q = 4, 8, 9, 10
        oG = qkv3[:, 0:4, :]
        oS = arena[:, P0 + 2560:P0 + 5120].rearrange("p (m t) -> p m t", m=H)
        oX = arena[:, P0 + 5120:P0 + 7680].rearrange("p (m t) -> p m t", m=H)
        vtok4 = place("vtok4", RING + 5248, P)[:, :]
        vtok = [arena[:, P0 + 2048 + P * t:P0 + 2048 + P * (t + 1)] for t in range(4)] + [vtok4]
        mkv = arena[:, P0:P0 + 2048].rearrange("p (s x) -> p s x", s=2)
        mkT = work[:, 0:1024].rearrange("p (h s) -> p h s", h=H)
        ck_sb = work[:, 1024:2048].rearrange("p (b s) -> p b s", b=NB)
        cv_sb = work[:, 2048:3072].rearrange("p (b s) -> p b s", b=NB)
        sm_sb = [a.rearrange("p (u s) -> p u s", u=2)
                 for a in (work[:, 3072:3584], work[:, 3584:4096], ring[:, 0:512])]
        pT_sb = [work[:, 4096 + 512 * i:4608 + 512 * i].rearrange("p (u s q) -> p u s q", u=2, s=2)
                 for i in range(2)]
        qs_sb = place("qs_sb", RING + 4096, 512)[:, :].rearrange("p (b m t) -> p b m t", b=NB, m=4)
        mem_sb = work[:, 0:2048].rearrange("p (k t) -> p k t", k=KT)
        mem_w = [place("mem_w", RING + 4096, 1024)[:, 512 * i:512 * i + 512] for i in range(2)] + [work[:, 2048:2560]]
        cm = work[:, 10240:14336].rearrange("p (e w x) -> p e w x", e=2, w=2)

        def parts(name, high, low, cols):
            return tuple(place(f"{name}_{x}", at, cols, F32R)[:, :].rearrange("p (k t) -> p k t", t=TOK)
                         for x, at in (("high", high), ("low", low)))

        xp = parts("x", ARENA + Q0 + 2560, XSB, KT * TOK)
        oh = place("o_high", ARENA, 12 * TOK, F32R)[:, :].rearrange("p (b k t) -> p b k t", b=3, t=TOK)
        op = [(oh[:, br], place(f"o{br}_low", at, 4 * TOK, F32R)[:, :].rearrange("p (k t) -> p k t", t=TOK))
              for br, at in enumerate((ARENA + Q0, ARENA + P0 + 2560, ARENA + P0 + 5120))]
        mp_ = parts("merged", WORK, WORK + 5120, KT * TOK)
        RAWN = 12 * P
        JOBS, TILES = 16, 8 + 2 * FT
        SLOTS = (WORK + 10240 + 3 * RAWN, WORK + 10240)
        raw = [place(f"raw{i}", at, RAWN)[:, :] for i, at in enumerate(SLOTS)]
        w_high, w_low = ([place(f"w{i}_{x}", at + d, RAWN, F32R)[:, :] for i, at in enumerate(SLOTS)]
                         for x, d in (("high", RAWN), ("low", 2 * RAWN)))
        PIECE, PIECES = 4 * P, 24
        piece_raw = [ring[:, PIECE * i:PIECE * (i + 1)] for i in (7, 6)]
        piece_parts = [word_parts(f"piece{i}", RING + (2 + 2 * i) * PIECE, RING + (3 + 2 * i) * PIECE, PIECE)
                       for i in range(2)]
        gate0 = place("gate0", RING + 4608, TOK)[:, :]
        first_sum = place("first_sum", WORK + 5120, KT * TOK)[:, :]
        w_parts = list(zip(w_high, w_low))
        sg = [arena[:, P0 + TOK * i:P0 + TOK * (i + 1)] for i in range(2)]
        gated = [arena[:, P0 + TOK * (i + 2):P0 + TOK * (i + 3)] for i in range(2)]
        y_flat = arena[:, 0:KT * TOK]
        y3 = y_flat.rearrange("p (k t) -> p k t", k=KT)
        x1 = parts("x1", XSB, ARENA + Q0 + 2560, KT * TOK)
        hid = [parts("hid0", WORK, WORK + 5120, KT * TOK), parts("hid1", ARENA + 5120, ARENA + P0, KT * TOK)]
        relu = [arena[:, P0 + 5120 + TOK * i:P0 + 5120 + TOK * (i + 1)] for i in range(2)]
        xn = [work[:, 1024 * i:1024 * (i + 1)] for i in range(2)]
        ln2gb = work[:, 2048:4096]
        xn2 = xn + [work[:, 4096 + 1024 * i:5120 + 1024 * i] for i in range(3)]
        merged_sum = place("merged_sum", ARENA + 12 * TOK, TOK)[:, :]

        def flat_parts(p):
            return tuple(x.rearrange("p k t -> p (k t)") for x in p)

        xp_flat, mp_flat, hid_flat = flat_parts(xp), flat_parts(mp_), [flat_parts(x) for x in hid]

        block = ctx.enter_context(nc.Block())

        UNITS = [u for t in range(4) for u in
                 [("wp", t, m) for m in range(4)] + [("ws", 0, p) for p in (2 * t, 2 * t + 1) if p < 4]
                 + [("mp", t, 0), ("mp", t, 1), ("ms", 0, t)]]
        NU = len(UNITS)
        W_SCALE, M_SCALE = 64 ** -0.5, P ** -0.5

        def cols(ap3, c, n=TOK):
            return ap3[:, bass.ds(c * n, n)]

        def stream(ap):
            return ap[:, NP:TOK].rearrange("p (b s) -> p b s", b=NB)

        def padded(row):
            return row[:, PAD:PAD + NP], row[:, PAD + NP:QW].rearrange("p (b s) -> p b s", b=NB)[:, :, PAD:]

        def halves_of(dst, b0, split):
            if not split:
                return [(dst[:, 0:HALF], ps[b0][:, 0:HALF]), (dst[:, HALF:TOK], ps[b0 + 1][:, 0:HALF])]
            prompt, streams = padded(dst)
            return [(prompt[:, 0:HALF], ps[b0][:, 0:HALF]), (prompt[:, HALF:NP], ps[b0 + 1][:, 0:NP - HALF]),
                    (streams, ps[b0 + 1][:, NP - HALF:HALF].rearrange("p (b s) -> p b s", b=NB))]

        def token_bank(t, name):
            return ((6, 0, 2, 0, 2) if name == "ln1" else (4, 6, 0, 2, 4))[t]

        def wtile(w, n):
            return w[bass.ds(n, 1), :, :].rearrange("a p x -> (a p) x")

        @block.sync
        def _(sp):
            def load(dst, src, name):
                sp.dma_start(dst, src).then_inc(sem(name), 16)

            for j in range(4):
                c = slice(2 * j * TOK, 2 * (j + 1) * TOK)
                load(x_sb[:, c], xT[:, c], f"x{j}_in")
                if j < 2:
                    load(ring[:, j * 1024:(j + 1) * 1024], w_h[j], f"wa{j}_in")
            load(wab.rearrange("p k x -> p (k x)"), w_ab, "ab_in")
            for dst, src in ((dtb, dt_b.to_broadcast([P, 4])), (alog, a_log.to_broadcast([P, 4])), (nrm, norm_w),
                             (cw_sb, conv_w), (ln1c, ln1), (sinkb, sinks_row.to_broadcast([P, 8])),
                             (sinkc, sinks), (cs_in, conv_s)):
                load(dst, src, "par_in")
            def first_load(i):
                for s in range(2):
                    sp.wait_ge(sem("wa_high"), 2 * i - 1 + s)
                    sp.wait_ge(sem("wa_low"), 2 * i - 1 + s)
                    load(ring[:, s * 1024:(s + 1) * 1024], wtile(w_h, 2 * i + s), f"wa{s}_in")

            first_load(1)
            load(cst[:, :], consts, "cst_in")
            with sp.Fori(2, NPRE // 2) as i:
                first_load(i)

            def fill_load(f):
                if f == 1:
                    sp.wait_ge(sem("h_mm"), NPRE)
                if f >= 4:
                    sp.wait_ge(sem("fill_mm"), f - 3)
                load(fill_w[f % 4], w_h[NPRE + f], f"quarter{f % 4}_in")

            for f in range(4):
                fill_load(f)
            sp.wait_ge(sem("cs_out"), 1)
            sp.dma_start(o_pconv, pad3[:, :, NP:NP + PAD]).then_inc(sem("conv_st"), 16)
            sp.dma_start(o_sconv, cs_out).then_inc(sem("conv_st"), 16)
            for f in range(4, NFILL):
                fill_load(f)
            sp.wait_ge(sem("fill_mm"), NFILL)
            load(S0[:, 0:2].rearrange("p h b v -> p (h b v)"), s0[:, 0:2048], "s0_in")
            sp.wait_ge(sem("y_mm"), 12)

            def mem_load(m):
                if m >= 3:
                    sp.wait_ge(sem("mem_mm"), m - 2)
                load(mem_w[m % 3], w_mem[m], f"quarter{m % 3}_in")

            load(mem_sb.rearrange("p k t -> p (k t)"), memT, "mem_in")
            for m in range(3):
                mem_load(m)
            load(S0[:, 2:4].rearrange("p h b v -> p (h b v)"), s0[:, 2048:], "s0_in")
            sp.wait_ge(sem("fill_out"), NFILL)
            for out, c in ((o_pk, W_K), (o_pv, W_V)):
                sp.dma_start(out, h3[:, c, NP - P:NP]).then_inc(sem("out_st"), 16)
            for out, old, c in ((o_skT, ckT, W_K), (o_svT, cvT, W_V)):
                sp.dma_start(out[:, :, P - ST:], stream(h3[:, c, :])).then_inc(sem("out_st"), 16)
                sp.dma_start(out[:, :, 0:P - ST], old[:, :, ST:]).then_inc(sem("out_st"), 16)
            for m in range(3, 2 * KT):
                mem_load(m)
            sp.wait_ge(sem("mem_mm"), 2 * KT)
            load(ck_sb, ckT, "ck_in")
            load(cv_sb, cv, "ck_in")
            sp.wait_ge(sem("vn_mm"), TT)
            load(piece_raw[0], w_piece[0], "piece0_in")
            for n in range(8):
                if n == 6:
                    sp.wait_ge(sem("ds_out"), 4)
                    sp.dma_start(o_ps, S.rearrange("p h x -> p (h x)")).then_inc(sem("ps_st"), 16)
                sp.wait_ge(sem("ss_out"), n + 1)
                h, b = n // 2, n % 2 * 4
                sp.dma_start(o_ss[:, (h * NB + b) * P:(h * NB + b + 4) * P],
                             S0[:, h, b:b + 4, :].rearrange("p b v -> p (b v)")).then_inc(sem("ss_st"), 16)
            sp.wait_ge(sem("mkv_out"), 4)
            sp.dma_start(o_pm, mkv).then_inc(sem("out_st"), 16)

            def cache_load(p, e):
                if p == 0:
                    sp.wait_ge(sem("ss_st"), 16 * 8)
                else:
                    sp.wait_ge(sem("pv_mm"), UNITS.index(("ms", 0, p - 1)) + 1)
                load(cm[:, e, 0, :], cmkT[2 * p + e], "cm_in")
                load(cm[:, e, 1, :], cmv[2 * p + e], "cm_in")

            for n in range(1, PIECES):
                if n == 1:
                    sp.wait_ge(sem("ps_st"), 16)
                if n >= 2:
                    sp.wait_ge(sem("piece_high"), n - 1)
                    sp.wait_ge(sem("piece_low"), n - 1)
                load(piece_raw[n % 2], w_piece[n], f"piece{n % 2}_in")
                for p in range(4):
                    for e in range(2):
                        if n == (3 + e if p == 0 else min(UNITS.index(("ms", 0, p - 1)) + 4 + e, PIECES - 1)):
                            cache_load(p, e)

            def stream_in(n, slot, src, first=False):
                if not first:
                    sp.wait_ge(sem("high_out"), n - 1)
                    sp.wait_ge(sem("low_out"), n - 1)
                load(raw[slot][:, 0:src.shape[-1]], src, f"raw{slot}_in")

            sp.wait_ge(sem("piece_mm"), PIECES)
            sp.wait_ge(sem("first_out"), KT)
            sp.wait_ge(sem("pv_mm"), UNITS.index(("ws", 0, 3)) + 1)
            stream_in(0, 0, w_mix[0], first=True)
            sp.wait_ge(sem("pv_mm"), NU)
            stream_in(1, 1, w_mix[1], first=True)
            with sp.Fori(1, JOBS // 2) as i:
                for s in range(2):
                    stream_in(2 * i + s, s, wtile(w_mix, 2 * i + s))
            with sp.Fori(0, TILES // 2) as i:
                for s in range(2):
                    stream_in(2 * i + (JOBS + s), s, wtile(w_tiles, 2 * i + s))
            sp.wait_ge(sem("tile_mm"), JOBS + TILES - 8)
            for j in range(2):
                load(ln2gb[:, j * DM:(j + 1) * DM], ln2[j:j + 1, :].to_broadcast([P, DM]), "ln2_in")
            for t in range(TT):
                if t < TT - 1:
                    sp.wait_ge(sem("final_out"), t + 1)
                else:
                    sp.wait_ge(sem("gain_out"), TT + 1)
                sp.dma_start(o_y[t], xn2[t]).then_inc(sem("y_st"), 16)
            sp.wait_ge(sem("y_st"), 16 * TT)
            sp.wait_ge(sem("out_st"), 16 * 7)
            sp.wait_ge(sem("conv_st"), 32)

        @block.tensor
        def _(pe):
            def product3(b0, ksteps, weights, k0, act, start=True, stop=True, arrived=None, halves=(0, 1)):
                for k in range(ksteps):
                    if arrived:
                        pe.wait_ge(sem(arrived), 2 * k + 2)
                    c = slice((k0 + k) * P, (k0 + k + 1) * P)
                    for n, (weight, part) in enumerate(((0, 0), (0, 1), (1, 0))):
                        for half in halves:
                            mm = pe.matmul(ps[b0 + half][:, 0:HALF], weights[weight][:, c],
                                           act[part][:, k, half * HALF:(half + 1) * HALF],
                                           start=start and k == 0 and n == 0,
                                           stop=stop and k == ksteps - 1 and n == 2)
                return mm

            def h_tiles(i):
                for s in range(2):
                    pe.wait_ge(sem("wa_high"), 2 * i + (s + 1))
                    pe.wait_ge(sem("wa_low"), 2 * i + (s + 1))
                    pe.wait_ge(sem("h_out_v" if s == 0 else "h_out_a"), i)
                    product3(2 * s, KT, wa[s], 0, xa).then_inc(sem("h_mm"), 1)

            for k in range(KT):
                pe.wait_ge(sem("xa_high"), k + 1)
                pe.wait_ge(sem("xa_low"), k + 1)
                for s in range(2):
                    if k == 0:
                        pe.wait_ge(sem("wa_high"), s + 1)
                        pe.wait_ge(sem("wa_low"), s + 1)
                    mm = product3(2 * s, 1, wa[s], k, tuple(x[:, k:k + 1] for x in xa), start=k == 0,
                                  stop=k == KT - 1)
                    if k == KT - 1:
                        mm.then_inc(sem("h_mm"), 1)
            with pe.Fori(1, NPRE // 2) as i:
                h_tiles(i)

            pe.wait_ge(sem("ab_in"), 16)
            for t in range(TT):
                for k in range(KT):
                    mm = pe.matmul(ps[5][:, t * 8:t * 8 + 8], x3[:, k, t * P:(t + 1) * P], wab[:, k, :],
                                   start=k == 0, stop=k == KT - 1)
            mm.then_inc(sem("ab_mm"), 1)

            def memory_step(half, k):
                m = KT * half + k
                if m == 0:
                    pe.wait_ge(sem("mem_in"), 16)
                pe.wait_ge(sem(f"quarter{m % 3}_in"), 16 * (len(range(m % 3, NFILL, 4)) + m // 3 + 1))
                if k == 0:
                    pe.wait_ge(sem("fill_out"), NFILL)
                    if half:
                        pe.wait_ge(sem("mkv_out"), 2)
                for st in range(2):
                    mm = pe.matmul(ps[6 + st][:, :], mem_sb[:, k, st * P:(st + 1) * P], mem_w[m % 3],
                                   start=k == 0, stop=k == KT - 1)
                mm.then_inc(sem("mem_mm"), 1)

            filled = [0, 0]

            def fill_before(stage, n):
                r = ROUND[stage, n]
                while filled[1] <= r:
                    for _ in range(FILL_STEPS[filled[1]]):
                        f, k = divmod(filled[0], KT)
                        filled[0] += 1
                        if f >= NFILL:
                            memory_step(f - NFILL, k)
                            continue
                        if k == 0:
                            pe.wait_ge(sem(f"quarter{f % 4}_in"), 16 * (f // 4 + 1))
                            if f:
                                pe.wait_ge(sem("fill_out"), f)
                        w = fill_w[f % 4][:, k * P:(k + 1) * P]
                        pe.matmul(ps[6][:, :], w, x3[:, k, 0:NP], start=k == 0, stop=k == KT - 1)
                        mm = pe.matmul(ps[7][:, 0:P], w, x3[:, k, NP:TOK], start=k == 0, stop=k == KT - 1)
                        if k == KT - 1:
                            mm.then_inc(sem("fill_mm"), 1)
                    filled[1] += 1

            def bank(stage, n):
                fill_before(stage, n)
                r = ROUND[stage, n]
                if r >= DN_BANKS:
                    old, m = ROUNDS[r - DN_BANKS]
                    pe.wait_ge(sem(f"{old}_out"), m + 1)
                return ps[r % DN_BANKS]

            def per_head(stage, t, lhsT, rhs):
                b = heads(bank(stage, t)[:, :])
                for h in range(H):
                    mm = pe.matmul(b[:, h, :], lhsT(h), rhs(h), start=True, stop=True)
                mm.then_inc(sem(f"{stage}_mm"), 1)

            def per_head_transpose(stage, t, src):
                b = heads(bank(stage, t)[:, :])
                for h in range(H):
                    mm = pe.transpose(b[:, h, :], src(h), ident)
                mm.then_inc(sem(f"{stage}_mm"), 1)

            def tok(t):
                return slice(t * P, (t + 1) * P)

            pe.wait_ge(sem("cst_in"), 16)
            pe.wait_ge(sem("h_out_v"), NPRE // 2)
            pe.wait_ge(sem("h_out_a"), NPRE // 2)
            for n in range(8):
                fill_before("norm", 2 * n)
                if n == 2:
                    pe.wait_ge(sem("ab_out"), 1)
                pe.wait_ge(sem("sq_out"), n + 1)
                for j, c in enumerate((slice(0, NP), slice(NP, TOK))):
                    b = bank("norm", 2 * n + j)
                    pe.matmul(b[:, 0:c.stop - c.start], const("ones"), sq[n % 2][:, c], start=True,
                              stop=True).then_inc(sem("norm_mm"), 1)
            b = bank("gcol", 0)
            pe.wait_ge(sem("g_out"), 1)
            for t in range(TT):
                kind = "p" if t < 4 else "s"
                pe.matmul(b[:, t * 8:t * 8 + 4], const(f"cum_{kind}"), g_tok[:, t, :], start=True, stop=True)
                mm = pe.matmul(b[:, t * 8 + 4:t * 8 + 8], const("ones" if t < 4 else "blk_s"), g_tok[:, t, :],
                               start=True, stop=True)
            mm.then_inc(sem("gcol_mm"), 1)
            fill_before("qk", 0)
            pe.wait_ge(sem("g_out"), 2)
            pe.wait_ge(sem("qk_norm"), 8)
            pe.wait_ge(sem("silu_out"), 12)

            def key_products(t):
                fill_before("kk", t)
                pe.wait_ge(sem("brow_out"), t + 1)
                per_head("kk", t, lambda h: qkv3[:, 4 + h, tok(t)], lambda h: KB[:, t, h, :])

            for t in range(TT):
                cum = const("cum_p" if t < 4 else "cum_s")
                per_head("qk", t, lambda h: qkv3[:, 4 + h, tok(t)], lambda h: qkv3[:, h, tok(t)])
                per_head("grow", t, lambda h: g_tok[:, t, h:h + 1].to_broadcast([P, P]), lambda h: cum)
                per_head("brow", t, lambda h: beta[:, t, h:h + 1].to_broadcast([P, P]), lambda h: ident)
                per_head_transpose("ktr", t, lambda h: qkv3[:, 4 + h, tok(t)])
                per_head_transpose("vtr", t, lambda h: qkv3[:, 8 + h, tok(t)])
                if t:
                    key_products(t - 1)
            key_products(TT - 1)
            for t in range(TT):
                fill_before("ntr", t)
                pe.wait_ge(sem("nd_out"), 2 * t + 2)
                per_head_transpose("ntr", t, lambda h: PWT[:, t, h, :])

            def update(level, t):
                power = "p" if level < 4 else "y"
                if level < 6:
                    fill_before("x", level_count("x", level, t))
                pe.wait_ge(sem(f"{power}_out"), level_count(power, level, t) + 1)
                if level == 1:
                    pe.wait_ge(sem("x0_out"), t + 1)
                else:
                    pe.wait_ge(sem("xt_out"), level_count("xt", level - 1, t) + 1)
                if level < 6:
                    per_head("x", level_count("x", level, t), lambda h: XT[:, t, h, :], lambda h: PW[:, t, h, :])

            def update_t(level, t):
                n = level_count("xt", level, t)
                if level == 6:
                    per_head("xt", n, lambda h: PW[:, t, h, :], lambda h: XT[:, t, h, :])
                    return
                pe.wait_ge(sem("x_out"), level_count("x", level, t) + 1)
                per_head_transpose("xt", n, lambda h: X[:, t, h, :])

            for level in (1, 2, 3):
                for t in range(TT):
                    fill_before("p", level_count("p", level, t))
                    if level == 1:
                        pe.wait_ge(sem("ntr_out"), t + 1)
                    else:
                        pe.wait_ge(sem("p_out"), level_count("p", level - 1, t) + 1)
                        pe.wait_ge(sem("pt_out"), level_count("pt", level - 1, t) + 1)
                    per_head("p", level_count("p", level, t), lambda h: PWT[:, t, h, :], lambda h: PW[:, t, h, :])
                if level < 3:
                    for t in range(TT):
                        n = level_count("pt", level, t)
                        fill_before("pt", n)
                        pe.wait_ge(sem("p_out"), n + 1)
                        per_head_transpose("pt", n, lambda h: PW[:, t, h, :])
                for t in range(TT):
                    update(level, t)
                for t in range(TT):
                    update_t(level, t)
            for level in (4, 5, 6):
                for t in range(TT - 1):
                    fill_before("y", level_count("y", level, t))
                    pe.wait_ge(sem("off_out"), level_count("off", level, t) + 1)
                    pe.wait_ge(sem("x_out"), level_count("x", level - 1, t) + 1)
                    per_head("y", level_count("y", level, t), lambda h: PWT[:, t, h, :], lambda h: X[:, t, h, :])
                for t in range(TT - 1):
                    update(level, t)
                for t in range(TT - 1):
                    update_t(level, t)

            def chunk_product(stage, t):
                n = scan_count(stage, t)
                k = lambda h: qkv3[:, 4 + h, tok(t)]
                if stage == "vtok":
                    pe.wait_ge(sem("mkv_out"), 4)
                    for x in range(TT):
                        mm = pe.transpose(ps[6 + x // 4][:, (x % 4) * P:(x % 4 + 1) * P], h3[:, W_V, tok(x)], ident)
                    mm.then_inc(sem("vtok_mm"), 1)
                    return
                if stage == "mkT":
                    pe.wait_ge(sem("kv_out"), 2)
                    for h in range(H):
                        for st in range(2):
                            b = ps[6 + h // 2][:, (h % 2) * 256 + st * P:(h % 2) * 256 + st * P + P]
                            mm = pe.transpose(b, mkv[:, st, h * P:(h + 1) * P], ident)
                    mm.then_inc(sem("mkT_mm"), 1)
                    return
                fill_before(stage, n)
                if stage == "ks" and t < 4:
                    pe.wait_ge(sem("xt_out"), level_count("xt", 6, t) + 1)
                    pe.wait_ge(sem("s_zero"), 1)
                    if t >= 1:
                        pe.wait_ge(sem("ds_out"), t)
                    per_head("ks", n, k, lambda h: S[:, h, :])
                if stage == "ks" and t == 4:
                    pe.wait_ge(sem("kst_out"), 1)
                    per_head_transpose("ks", n, lambda h: kst_sb[:, h, :])
                if stage == "vn":
                    pe.wait_ge(sem("r_out"), n + 1)
                    if t == 4:
                        pe.wait_ge(sem("xt_out"), level_count("xt", 3, 4) + 1)
                    r = r_streams if t == 4 else r_sb
                    per_head("vn", n, lambda h: XT[:, t, h, :], lambda h: r[:, h, :])
                if stage == "go":
                    pe.wait_ge(sem("qe_out"), t + 1)
                    pe.wait_ge(sem("qk_out"), t + 1)
                    b = heads(bank("go", n)[:, :])
                    pe.wait_ge(sem("vn_out"), n + 1)
                    for h in range(H):
                        if t < 4:
                            pe.matmul(b[:, h, :], S[:, h, :], qkv3[:, h, tok(t)], start=True, stop=False)
                            mm = pe.matmul(b[:, h, :], vn_sb[:, h, :], QKD[:, t, h, :], start=False, stop=True)
                            continue
                        pe.matmul(b[:, h, :], vn_streams[:, h, :], QKD[:, 4, h, :], start=True, stop=False,
                                  skip_group_check=True)
                        for j in range(NB):
                            c = slice(NP + j * ST, NP + (j + 1) * ST)
                            mm = pe.matmul(b[:, h, j * ST:(j + 1) * ST], S0[:, h, j, :], qkv3[:, h, c],
                                           start=False, stop=j == NB - 1, skip_group_check=True)
                    mm.then_inc(sem("go_mm"), 1)
                if stage == "ds":
                    pe.wait_ge(sem("ktr_out"), t + 1)
                    per_head("ds", n, lambda h: KD[:, t, h, :], lambda h: vn_sb[:, h, :])
                if stage == "kst":
                    pe.wait_ge(sem("s0_in"), 32)
                    b = heads(bank("kst", 0)[:, :])
                    for h in range(H):
                        for j in range(NB):
                            c = slice(NP + j * ST, NP + (j + 1) * ST)
                            mm = pe.matmul(b[:, h, j * ST:(j + 1) * ST], S0[:, h, j, :], qkv3[:, 4 + h, c],
                                           start=True, stop=True)
                    mm.then_inc(sem("kst_mm"), 1)
                if stage == "ss":
                    h, j = n // 2, n % 2 * 4
                    b = bank("ss", n)
                    pe.wait_ge(sem("vm_out"), h + 1)
                    pe.matmul(b[:, :], KD[:, 4, h, :], vm_sb[h % 2][:, j:j + 4, :].rearrange("p b x -> p (b x)"),
                              start=True, stop=True).then_inc(sem("ss_mm"), 1)
                if stage == "on":
                    pe.wait_ge(sem("osq_out"), n + 1)
                    b = bank("on", n)
                    pe.matmul(b[:, :], const("mean"), sq_o[n % 2], start=True, stop=True
                              ).then_inc(sem("on_mm"), 1)

            for stage, t in SCAN:
                chunk_product(stage, t)

            def bank_read(*banks):
                for b in banks:
                    stage, n = [x for r, x in enumerate(ROUNDS) if r % DN_BANKS == b][-1]
                    pe.wait_ge(sem(f"{stage}_out"), n + 1)

            def scores(n):
                kind, t, m = UNITS[n]
                if n < 2:
                    bank_read(2 * n, 2 * n + 1)
                else:
                    pe.wait_ge(sem("exp_out"), n - 1)
                b = sc_ps[n % 2]
                if kind == "wp":
                    k0 = max(t - 1, 0) * P
                    for g in range(2):
                        r = slice(64 * g, 64 * g + 64)
                        mm = pe.matmul(b[:, g, :], h3[r, W_Q + m, tok(t)],
                                       h3[r, W_K, k0:k0 + 256], start=True, stop=True)
                if kind == "ws":
                    pe.wait_ge(sem("ck_in"), 32)
                    pe.wait_ge(sem("qs_out"), 1)
                    for e in range(2):
                        j = 2 * m + e
                        for g in range(2):
                            r = slice(64 * g, 64 * g + 64)
                            q = qs_sb[r, j, :, :].rearrange("p m t -> p (m t)")
                            pe.matmul(b[r, e, 0:P], q, ck_sb[r, j, :], start=True, stop=True)
                            mm = pe.matmul(b[r, e, P:], q, h3[r, W_K, NP:TOK],
                                           start=True, stop=True)
                if kind == "mp":
                    for u in range(2):
                        mm = pe.matmul(b[:, u, :], h3[:, M_Q + 2 * m + u, tok(t)],
                                       mkT[:, 2 * m + u, :], start=True, stop=True)
                if kind == "ms":
                    pe.wait_ge(sem("cm_in"), 64 * (m + 1))
                    for e in range(2):
                        for h in range(H):
                            mm = pe.matmul(b[32 * h:32 * h + 32, e, :],
                                           h3[:, M_Q + h, NP + 32 * m:NP + 32 * m + 32],
                                           cm[:, e, 0, h * 256:h * 256 + 256], start=True, stop=True,
                                           tile_position=(0, 32 * h))
                mm.then_inc(sem("sc_mm"), 1)

            def probs_turned(n):
                pe.wait_ge(sem("prob_out"), n + 1)
                if n == 0:
                    bank_read(4)
                else:
                    pe.wait_ge(sem("pT_out"), n)
                b = ps[4]
                for u in range(2):
                    for st in range(2):
                        mm = pe.transpose(b[:, (2 * u + st) * P:(2 * u + st + 1) * P],
                                          sm_sb[n % 3][:, u, st * P:(st + 1) * P], ident)
                mm.then_inc(sem("pT_mm"), 1)

            def values(n):
                kind, t, m = UNITS[n]
                pe.wait_ge(sem("pT_out"), n + 1)
                if n == 0:
                    bank_read(5)
                else:
                    pe.wait_ge(sem("at_out"), n)
                b, pT = ps[5], pT_sb[n % 2]
                for u in range(2):
                    for st in range(2):
                        go = dict(start=st == 0, stop=st == 1)
                        if kind == "wp":
                            mm = pe.matmul(b[64 * u:64 * u + 64, 0:P], vtok[max(t - 1, 0) + st][:, 64 * u:64 * u + 64],
                                           pT[:, u, st, :], **go)
                        if kind == "mp":
                            c = 512 + (2 * m + u) * P
                            mm = pe.matmul(b[:, u * P:(u + 1) * P], mkv[:, st, c:c + P], pT[:, u, st, :], **go)
                    if kind == "ws":
                        for g in range(2):
                            r = slice(64 * g, 64 * g + 64)
                            pe.matmul(b[r, u * 64:u * 64 + 64], cv_sb[:, 2 * m + u, r], pT[:, u, 0, r],
                                      start=True, stop=False)
                            mm = pe.matmul(b[r, u * 64:u * 64 + 64], vtok[4][:, r], pT[:, u, 1, r],
                                           start=False, stop=True)
                    if kind == "ms":
                        for h in range(H):
                            for st in range(2):
                                c = 512 * st + h * P
                                mm = pe.matmul(b[:, h * 32 + 16 * u:h * 32 + 16 * u + 16],
                                               cm[:, u, 1, c:c + P],
                                               pT[:, u, st, 32 * h + 16 * u:32 * h + 16 * u + 16],
                                               start=st == 0, stop=st == 1)
                mm.then_inc(sem("pv_mm"), 1)

            def piece(n):
                c, part = divmod(n, 3)
                pe.wait_ge(sem("piece_high"), n + 1)
                pe.wait_ge(sem("piece_low"), n + 1)
                if n == 0:
                    pe.wait_ge(sem("kv_out"), 4)
                    pe.wait_ge(sem("xo_out"), 4)
                if n == 1:
                    pe.wait_ge(sem("xo_out"), 8)
                if n == 2:
                    pe.wait_ge(sem("op_out"), 1)
                if part == 0 and c:
                    pe.wait_ge(sem("first_out"), c)
                if part == 2:
                    pe.wait_ge(sem("gate0_out"), c + 1)
                act = op[0] if part == 2 else tuple(x[:, 4 - 4 * part:8 - 4 * part] for x in xp)
                product3(6, 4, piece_parts[n % 2], 0, act, start=part != 1, stop=part != 0
                         ).then_inc(sem("piece_mm"), 1)

            pe.wait_ge(sem("kv_out"), 4)
            for n in range(NU + 3):
                if n < NU:
                    scores(n)
                if n < PIECES:
                    piece(n)
                if 2 <= n <= NU + 1:
                    probs_turned(n - 2)
                if n >= 3:
                    values(n - 3)

            def mix_jobs(i, first):
                for s in range(2):
                    n = 2 * i + s
                    pe.wait_ge(sem("high_out"), n + 1)
                    pe.wait_ge(sem("low_out"), n + 1)
                    if not first:
                        pe.wait_ge(sem("gated_out"), n - 1)
                    elif s == 1:
                        pe.wait_ge(sem("at_out"), NU)
                        pe.wait_ge(sem("first_out"), KT)
                    product3(4 * s + 2, KT, w_parts[s], 4, xp)
                    if first and s == 0:
                        pe.wait_ge(sem("xo_out"), 9)
                    if first and s == 1:
                        pe.wait_ge(sem("op_out"), 2)
                    product3(4 * s, 4, w_parts[s], 0, op[1 + s]).then_inc(sem("tile_mm"), 1)

            mix_jobs(0, True)
            with pe.Fori(1, JOBS // 2) as i:
                mix_jobs(i, False)

            def column_tiles(i, n0, act, free, freed, arrived=None):
                for s in range(2):
                    n = 2 * i + (n0 + s)
                    pe.wait_ge(sem("high_out"), n + 1)
                    pe.wait_ge(sem("low_out"), n + 1)
                    pe.wait_ge(sem(free), freed + s)
                    product3(2 * s, KT, w_parts[s], 0, act, arrived=arrived if s == 0 else None
                             ).then_inc(sem("tile_mm"), 1)

            column_tiles(0, JOBS, mp_, "gated_out", JOBS - 1, arrived="merged_parts")
            with pe.Fori(1, 4) as i:
                column_tiles(i, JOBS, mp_, "o_out", 2 * i - 1)

            def to_tokens(t, done):
                b = token_bank(t, done)
                if t >= (2 if done == "ln1" else 4):
                    pe.wait_ge(sem(f"{done}_norm"), t - (1 if done == "ln1" else 3))
                for k in range(KT):
                    if t == 0:
                        if done == "ln1":
                            pe.wait_ge(sem("residual_out"), k + 1)
                        else:
                            pe.wait_ge(sem("down_out"), 3 * KT + k + 1)
                    mm = pe.transpose(ps[b + k // 4][:, (k % 4) * P:(k % 4 + 1) * P], y3[:, k, tok(t)],
                                      ident)
                mm.then_inc(sem(f"{done}_turn"), 1)

            def to_channels(t):
                pe.wait_ge(sem("ln1_norm"), t + 1)
                if t >= 2:
                    pe.wait_ge(sem("ln1_out"), t - 1)
                for k in range(KT):
                    mm = pe.transpose(ps[4 + 2 * (t % 2) + k // 4][:, (k % 4) * P:(k % 4 + 1) * P],
                                      xn[t % 2][:, k * P:(k + 1) * P], ident)
                mm.then_inc(sem("ln1_back"), 1)

            for t in range(TT + 1):
                if t < TT:
                    to_tokens(t, "ln1")
                if t >= 1:
                    to_channels(t - 1)

            def first_up(n0):
                for half in range(2):
                    pe.wait_ge(sem("x1_low"), 3 if half == 0 else TT)
                    for s in range(2):
                        if half == 0:
                            pe.wait_ge(sem("high_out"), n0 + s + 1)
                            pe.wait_ge(sem("low_out"), n0 + s + 1)
                        mm = product3(2 * s, KT, w_parts[s], 0, x1, halves=(half,))
                        if half:
                            mm.then_inc(sem("tile_mm"), 1)

            pe.wait_ge(sem("ln1_norm"), TT)
            before = ("ln1_norm", TT - 1)
            for stage, (kind, chunk) in enumerate(FFN_ORDER):
                n0 = JOBS + 8 + 8 * stage
                act = x1 if kind == "up" else hid[chunk % 2]
                if kind == "down":
                    pe.wait_ge(sem("hid_low"), 8 * (chunk + 1))
                if stage == 0:
                    first_up(n0)
                else:
                    column_tiles(0, n0, act, before[0], before[1])
                with pe.Fori(1, 4) as i:
                    column_tiles(i, n0, act, kind + "_out", 2 * i + (8 * chunk - 1))
                before = (kind + "_out", 8 * chunk + 7)
            for t in range(TT):
                to_tokens(t, "ln2")

        @block.vector
        def _(dve):
            steps = [0]

            def then_wait(ins):
                steps[0] += 1
                ins.then_inc(sem("dve_step"), 1)
                dve.wait_ge(sem("dve_step"), steps[0])

            def bc(ap, n):
                return ap.unsqueeze(2).to_broadcast([P, ap.shape[1], n])

            def flat(ap):
                return ap.rearrange("p h x -> p (h x)")

            dve.memset(pad3[:, :, 0:PAD], 0.0)
            dve.memset(eps, 1e-6)
            for k in range(KT):
                dve.wait_ge(sem("xa_high"), k + 1)
                dve.tensor_tensor(xa[1][:, k], x3[:, k], xa[0][:, k], ALU.subtract).then_inc(sem("xa_low"), 1)
            def read_tile(i, dst, split):
                dve.wait_ge(sem("h_mm"), 2 * i + 1)
                for d, b in halves_of(dst, 0, split):
                    last = dve.tensor_copy(d, b)
                last.then_inc(sem("h_out_v"), 1)

            pad_flat = arena[:, P0:P0 + 12 * QW]

            def convolve(i, s, first):
                n = 2 * i + s
                if s == 0:
                    dve.wait_ge(sem("h_out_v"), i + 1)
                    dve.wait_ge(sem("h_out_a"), i + 1)
                if not first:
                    dve.wait_ge(sem("silu_out"), n - 1)
                acc = conv_acc[s]

                def tap(w):
                    return arena[:, bass.ds(n * QW + (P0 + w), CW)], cw_sb[:, bass.ds(4 * n + w, 1)]

                x0, w0 = tap(0)
                dve.tensor_scalar(acc, x0, w0, None, ALU.mult).then_inc(sem("conv_step"), 1)
                for w in range(1, 4):
                    dve.wait_ge(sem("conv_step"), 3 * n + w)
                    xw, ww = tap(w)
                    ins = dve.scalar_tensor_tensor(acc, xw, ww, acc, ALU.mult, ALU.add)
                    ins.then_inc(sem("conv_step" if w < 3 else "conv_out"), 1)

            def tile_and_conv(i, dst, split, first=False):
                read_tile(i, dst, split)
                for s in range(2):
                    convolve(i - 1, s, first)

            read_tile(0, cols(pad_flat, 0, QW), True)
            dve.wait_ge(sem("par_in"), 16 * 8)
            dve.tensor_copy(pad3[:, :, NP + PAD:].rearrange("p k (b s) -> p k b s", b=NB)[:, :, :, 0:PAD],
                            cs_in.rearrange("p (k b s) -> p k b s", k=12, b=NB))
            dve.tensor_scalar(nsinkb, sinkb, -1.0, None, ALU.mult)
            then_wait(dve.tensor_scalar(nsinkc, sinkc, -1.0, None, ALU.mult))
            tile_and_conv(1, cols(pad_flat, 2, QW), True, first=True)
            with dve.Fori(2, 6) as i:
                tile_and_conv(i, cols(pad_flat, 2 * i, QW), True)
            tile_and_conv(6, h3[:, 0, :], False)
            for i in range(7, NPRE // 2):
                read_tile(i, h3[:, 2 * (i - 6), :], False)
            dve.tensor_copy(cs_out.rearrange("p (k b s) -> p k b s", k=12, b=NB),
                            pad3[:, :, NP + PAD:].rearrange("p k (b s) -> p k b s", b=NB)[:, :, :, ST:]
                            ).then_inc(sem("cs_out"), 1)

            dve.wait_ge(sem("ab_mm"), 1)
            then_wait(dve.tensor_copy(ab.rearrange("p t x -> p (t x)"), ps[5][:, 0:40]))
            then_wait(dve.tensor_tensor(t_a, ab[:, :, 0:4], dtb.unsqueeze(1).to_broadcast([P, TT, 4]), ALU.add))
            dve.scalar_tensor_tensor(t_b, t_a, -1.0, t_a, ALU.mult, ALU.max).then_inc(sem("ab_out"), 1)
            then_wait(dve.tensor_scalar(t_a, t_a, 0.0, None, ALU.max))
            dve.wait_ge(sem("ln_out"), 1)
            then_wait(dve.tensor_tensor(t_a, t_a, t_c, ALU.add))
            dve.scalar_tensor_tensor(g_tok, t_a, -1.0, nea.unsqueeze(1).to_broadcast([P, TT, 4]), ALU.mult,
                                     ALU.mult).then_inc(sem("g_out"), 1)
            then_wait(dve.tensor_scalar(e_b, e_b, 1.0, None, ALU.add))
            dve.reciprocal(beta, e_b).then_inc(sem("g_out"), 1)

            for n in range(8):
                dve.wait_ge(sem("norm_out"), 2 * n + 2)
                then_wait(dve.reciprocal(rn[n % 2], rn[n % 2]))
                dve.scalar_tensor_tensor(qkv3[:, n, :], qkv3[:, n, :], P ** -0.5 if n < H else 1.0, rn[n % 2],
                                         ALU.mult, ALU.mult).then_inc(sem("qk_norm"), 1)

            def result(stage, n):
                dve.wait_ge(sem(f"{stage}_mm"), n + 1)
                return ps[ROUND[stage, n] % DN_BANKS]

            then_wait(dve.tensor_copy(gcl.rearrange("p t x -> p (t x)"), result("gcol", 0)[:, 0:40]))
            dve.tensor_tensor(glc, gcl[:, :, 4:8], gcl[:, :, 0:4], ALU.subtract).then_inc(sem("gcol_out"), 1)
            dve.wait_ge(sem("ecol_out"), 2)
            then_wait(dve.scalar_tensor_tensor(nbeg, beta, -1.0, nbeg, ALU.mult, ALU.mult))

            dve.wait_ge(sem("conv_st"), 32)

            def lower_part(t):
                dve.tensor_tensor(NT[:, t], heads(result("kk", t)[:, :]), DEC[:, t], ALU.mult
                                  ).then_inc(sem("kk_out"), 1)

            for t in range(TT):
                b = heads(result("grow", t)[:, :])
                mask = const("neg_p" if t < 4 else "neg_s")
                if t >= 2:
                    dve.wait_ge(sem("dec_out"), t - 1)
                then_wait(dve.tensor_tensor(d_sb[t % 2], b, bc(gcl[:, t, 0:4], P), ALU.subtract))
                dve.tensor_tensor(d_sb[t % 2], d_sb[t % 2], mask.unsqueeze(1).to_broadcast([P, H, P]),
                                  ALU.min).then_inc(sem("dmin_out"), 1)
                dve.tensor_tensor(KB[:, t], qkv3[:, 4:8, t * P:(t + 1) * P], heads(result("brow", t)[:, :]),
                                  ALU.mult).then_inc(sem("brow_out"), 1)
                dve.tensor_tensor(KD[:, t], heads(result("ktr", t)[:, :]), bc(kdec[:, t, :], P),
                                  ALU.mult).then_inc(sem("ktr_out"), 1)
                dve.tensor_tensor(VB[:, t], heads(result("vtr", t)[:, :]), bc(beta[:, t, :], P),
                                  ALU.mult).then_inc(sem("vtr_out"), 1)
                e = eg_sb[t % 2]
                dve.wait_ge(sem("grow_out"), t + 1)
                if t < 4:
                    dve.tensor_copy(egl[:, t, :].unsqueeze(2), e[:, :, P - 1:P])
                else:
                    dve.tensor_copy(egs, e[:, :, ST - 1::ST])
                q = qkv3[:, 0:4, t * P:(t + 1) * P]
                b = heads(result("qk", t)[:, :])
                dve.tensor_tensor(q, q, e, ALU.mult).then_inc(sem("qe_out"), 1)
                dve.wait_ge(sem("dec_out"), t + 1)
                dve.tensor_tensor(QKD[:, t], b, DEC[:, t], ALU.mult).then_inc(sem("qk_out"), 1)
                if t:
                    lower_part(t - 1)
            lower_part(TT - 1)
            for t in range(TT):
                dve.wait_ge(sem("ntr_out"), t + 1)
                one = ident.unsqueeze(1).to_broadcast([P, H, P])
                dve.tensor_tensor(X[:, t], PW[:, t], one, ALU.add)
                dve.tensor_tensor(XT[:, t], PWT[:, t], one, ALU.add).then_inc(sem("x0_out"), 1)

            for level in range(1, 7):
                tt = TT if level < 4 else TT - 1
                if level < 6:
                    for t in range(tt):
                        if level == 1:
                            dve.wait_ge(sem("x0_out"), t + 1)
                        b = result("x", level_count("x", level, t))
                        dve.tensor_tensor(X[:, t], X[:, t], heads(b[:, :]), ALU.add).then_inc(sem("x_out"), 1)
                for t in range(tt):
                    b = result("xt", level_count("xt", level, t))
                    if level < 6:
                        dve.tensor_copy(XT[:, t], heads(b[:, :])).then_inc(sem("xt_out"), 1)
                    else:
                        dve.tensor_tensor(XT[:, t], XT[:, t], heads(b[:, :]), ALU.add).then_inc(sem("xt_out"), 1)
                if level == 1:
                    then_wait(dve.memset(S, 0.0))
                    dve.sem_inc(sem("s_zero"), 1)

            def chunk_step(stage, t):
                n = scan_count(stage, t)
                if stage == "vtok":
                    dve.wait_ge(sem("vtok_mm"), 1)
                    dve.tensor_copy(arena[:, P0 + 2048:P0 + 2560], ps[6][:, :]).then_inc(sem("kv_out"), 1)
                    dve.tensor_copy(vtok4, ps[7][:, 0:P]).then_inc(sem("kv_out"), 1)
                if stage == "mkT":
                    dve.wait_ge(sem("mkT_mm"), 1)
                    for j in range(2):
                        dve.tensor_copy(mkT[:, 2 * j:2 * j + 2, :].rearrange("p h s -> p (h s)"), ps[6 + j][:, :]
                                        ).then_inc(sem("kv_out"), 1)
                if stage == "ks":
                    b = heads(result("ks", n)[:, :])
                    r = r_streams if t == 4 else r_sb
                    dve.tensor_tensor(r, b, bc(nbeg[:, t, :], P), ALU.mult).then_inc(sem("ks_out"), 1)
                    dve.wait_ge(sem("ks_out"), n + 1)
                    dve.tensor_tensor(r, r, VB[:, t], ALU.add).then_inc(sem("r_out"), 1)
                if stage == "ds":
                    b = heads(result("ds", n)[:, :])
                    then_wait(dve.tensor_tensor(S, S, bc(egl[:, t, :], P), ALU.mult))
                    dve.tensor_tensor(S, S, b, ALU.add).then_inc(sem("ds_out"), 1)
                if stage == "vn" and t == 4:
                    dve.wait_ge(sem("vn_out"), n + 1)
                    for h in range(2):
                        stream_values(h)
                if stage == "ss":
                    h, j = n // 2, n % 2 * 4
                    state = S0[:, h, j:j + 4, :]
                    b = result("ss", n)[:, :].rearrange("p (b v) -> p b v", b=4)
                    dve.wait_ge(sem("sdec_out"), n + 1)
                    dve.tensor_tensor(state, state, b, ALU.add).then_inc(sem("ss_out"), 1)
                    if n in (1, 3):
                        stream_values(h + 2)
                if stage == "on":
                    c = slice(t * P, (t + 1) * P)
                    o = oG[:, :, c]
                    dve.wait_ge(sem("on_out"), n + 1)
                    then_wait(dve.reciprocal(rn_o[n % 2], rn_o[n % 2]))
                    then_wait(dve.scalar_tensor_tensor(o, o, nrm[:, 0:1], heads(rn_o[n % 2]), ALU.mult, ALU.mult))
                    if n == 0:
                        dve.wait_ge(sem("z_out"), 1)
                    dve.tensor_tensor(o, o, h3[:, 0:4, c], ALU.mult).then_inc(sem("og_out"), 1)

            def stream_values(h):
                dve.tensor_tensor(vm_sb[h % 2], vn_streams[:, h, :].unsqueeze(1).to_broadcast([P, NB, P]),
                                  const("tokblk").unsqueeze(2).to_broadcast([P, NB, P]), ALU.mult
                                  ).then_inc(sem("vm_out"), 1)

            for stage, t in SCAN:
                chunk_step(stage, t)
            dve.wait_ge(sem("og_out"), TT)
            dve.sem_inc(sem("gdn_end"), 1)

            def low_part(n, slot, width=8 * P):
                dve.wait_ge(sem("high_out"), n + 1)
                dve.tensor_tensor(w_low[slot][:, 0:width], raw[slot][:, 0:width], w_high[slot][:, 0:width],
                                  ALU.subtract).then_inc(sem("low_out"), 1)

            def front(n):
                kind, t, m = UNITS[n]
                dve.wait_ge(sem("sc_mm"), n + 1)
                b = sc_ps[n % 2]
                s, neg = sm_sb[n % 3], nm[n % 3]
                if kind in ("mp", "ms"):
                    then_wait(dve.tensor_reduce(neg, b, AX.X, ALU.max, negate=True))
                    dve.tensor_scalar(neg, neg, M_SCALE, None, ALU.mult).then_inc(sem("nm_out"), 1)
                    return
                if n >= 3:
                    dve.wait_ge(sem("pT_mm"), n - 2)
                if kind == "wp":
                    mask = const("win0" if t == 0 else "win")
                    then_wait(dve.scalar_tensor_tensor(s, b, W_SCALE, mask.unsqueeze(1).to_broadcast([P, 2, 256]),
                                                       ALU.mult, ALU.add))
                    sink, nsink = sinkb[:, m::4], nsinkb[:, m::4]
                else:
                    dve.tensor_scalar(s[:, :, 0:P], b[:, :, 0:P], W_SCALE, None, ALU.mult)
                    for e in range(2):
                        x = 112 - ST * (2 * m + e)
                        last = dve.scalar_tensor_tensor(s[:, e, P:], b[:, e, P:], W_SCALE,
                                                        const("snew")[:, x:x + P], ALU.mult, ALU.add)
                    then_wait(last)
                    sink, nsink = sinkc.to_broadcast([P, 2]), nsinkc.to_broadcast([P, 2])
                then_wait(dve.tensor_reduce(neg, s, AX.X, ALU.max, negate=True))
                then_wait(dve.tensor_tensor(neg, neg, nsink, ALU.min))
                dve.tensor_tensor(es[n % 3], neg, sink, ALU.add).then_inc(sem("nm_out"), 1)

            def back(n):
                i = n % 3
                dve.wait_ge(sem("exp_out"), n + 1)
                if UNITS[n][0] in ("wp", "ws"):
                    then_wait(dve.tensor_tensor(den[i], den[i], es[i], ALU.add))
                then_wait(dve.reciprocal(rden[i], den[i]))
                dve.tensor_tensor(sm_sb[i], sm_sb[i], rden[i].unsqueeze(2).to_broadcast([P, 2, 256]), ALU.mult
                                  ).then_inc(sem("prob_out"), 1)

            def first_gated(c):
                dve.wait_ge(sem("piece_mm"), 3 * c + 3)
                for h in range(2):
                    x = slice(h * HALF, (h + 1) * HALF)
                    last = dve.tensor_tensor(cols(first_sum, c)[:, x], ps[6 + h][:, 0:HALF], gate0[:, x],
                                             ALU.mult)
                last.then_inc(sem("first_out"), 1)

            for n in range(NU + 1):
                if n < NU:
                    front(n)
                if n == 0:
                    dve.wait_ge(sem("xo_high"), 9)
                    dve.tensor_tensor(op[0][1], oG, op[0][0], ALU.subtract).then_inc(sem("op_out"), 1)
                if n == NU:
                    low_part(0, 0, RAWN)
                if n >= 1:
                    back(n - 1)
                if n % 3 == 2 and n < PIECES:
                    first_gated(n // 3)

            dve.wait_ge(sem("oh_out"), 2)
            dve.tensor_tensor(op[2][1], oX, op[2][0], ALU.subtract).then_inc(sem("op_out"), 1)
            low_part(1, 1, RAWN)

            def merge(i, first, width=RAWN):
                total = merged_sum
                for s in range(2):
                    n = 2 * i + s
                    if not (first and s == 0):
                        low_part(n + 1, 1 - s, width if s else RAWN)
                    dve.wait_ge(sem("sg_out"), n + 1)
                    if s == 0 and not first:
                        dve.wait_ge(sem("merged_out"), i)
                    for h in range(2):
                        x = slice(h * HALF, (h + 1) * HALF)
                        last = dve.tensor_tensor(gated[s][:, x], ps[4 * s + h][:, 0:HALF], sg[s][:, x], ALU.mult)
                    last.then_inc(sem("gated_out"), 1)
                    dve.wait_ge(sem("gated_out"), n + 1)
                    if s == 0:
                        if not first:
                            dve.wait_ge(sem("merged_parts"), 2 * i)
                        dve.tensor_tensor(total, cols(first_sum, i), gated[s], ALU.add
                                          ).then_inc(sem("merged_two"), 1)
                    else:
                        dve.wait_ge(sem("merged_two"), i + 1)
                        dve.tensor_tensor(total, total, gated[s], ALU.add).then_inc(sem("merged_out"), 1)
                dve.wait_ge(sem("mh_out"), i + 1)
                dve.tensor_tensor(cols(mp_flat[1], i), total, cols(mp_flat[0], i), ALU.subtract
                                  ).then_inc(sem("merged_parts"), 2)

            merge(0, True)
            with dve.Fori(1, 7) as i:
                merge(i, False)
            merge(7, False, 8 * P)

            def residuals(i, n0, name, done, skip_last=False):
                for s in range(2):
                    n = 2 * i + (n0 + s)
                    if not (skip_last and s == 1):
                        low_part(n + 1, 1 - s)
                    dve.wait_ge(sem("tile_mm"), n + 1)
                    y = cols(y_flat, 2 * i + s)
                    for h, c in ((0, slice(0, HALF)), (1, slice(HALF, TOK))):
                        b = ps[2 * s + h][:, 0:HALF]
                        if name == "o":
                            src = cols(xp_flat[0], 2 * i + s)
                            last = dve.scalar_tensor_tensor(y[:, c], src[:, c], ALPHA, b, ALU.mult, ALU.add)
                        else:
                            last = dve.scalar_tensor_tensor(y[:, c], y[:, c], ALPHA if name == "first" else 1.0, b,
                                                            ALU.mult, ALU.add)
                    last.then_inc(sem(done), 1)
                    if name == "o":
                        dve.wait_ge(sem(done), 2 * i + s + 1)
                        dve.scalar_tensor_tensor(y, cols(xp_flat[1], 2 * i + s), ALPHA, y, ALU.mult, ALU.add
                                                 ).then_inc(sem("residual_out"), 1)

            dve.wait_ge(sem("gated_out"), JOBS)
            with dve.Fori(0, 4) as i:
                residuals(i, JOBS, "o", "o_out")
            def token_variance(t, name):
                i = t % 3
                dve.wait_ge(sem(f"{name}_turn"), t + 1)
                b = token_bank(t, name)
                for j in range(2):
                    last = dve.bn_stats(stats[i][:, 6 * j:6 * j + 6], ps[b + j][:, :])
                then_wait(last)
                then_wait(dve.bn_aggr(mv[i], stats[i]))
                then_wait(dve.tensor_scalar(rstd[i], mv[i][:, 1:2], 1e-5, None, ALU.add))
                dve.sem_inc(sem("var_out"), 1)

            def token_scale(t, name):
                i, b = t % 3, token_bank(t, name)
                dve.wait_ge(sem("dev_out"), t + 1 + (TT if name == "ln2" else 0))
                then_wait(dve.reciprocal(rstd[i], rstd[i]))
                if name == "ln2":
                    dve.scalar_tensor_tensor(nmr[i], mv[i][:, 0:1], -1.0, rstd[i], ALU.mult, ALU.mult
                                             ).then_inc(sem("nmr_out"), 1)
                    return
                if t >= 2:
                    dve.wait_ge(sem("ln1_back"), t - 1)
                for j in range(2):
                    last = dve.tensor_scalar(xn[t % 2][:, 512 * j:512 * j + 512], ps[b + j][:, :], mv[i][:, 0:1],
                                             rstd[i], ALU.subtract, ALU.mult)
                last.then_inc(sem(f"{name}_norm"), 1)

            for t in range(TT):
                token_variance(t, "ln1")
                token_scale(t, "ln1")

            def squares(i, n0, chunk):
                for s in range(2):
                    n, c = 2 * i + (n0 + s), 2 * i + (8 * chunk + s)
                    low_part(n + 1, 1 - s)
                    dve.wait_ge(sem("up_out"), c + 1)
                    dve.tensor_tensor(relu[s], relu[s], relu[s], ALU.mult).then_inc(sem("sqr_out"), 1)
                    dve.wait_ge(sem("hid_high"), c + 1)
                    dve.tensor_tensor(cols(hid_flat[chunk % 2][1], 2 * i + s), relu[s],
                                      cols(hid_flat[chunk % 2][0], 2 * i + s), ALU.subtract
                                      ).then_inc(sem("hid_low"), 1)

            for stage, (kind, chunk) in enumerate(FFN_ORDER):
                n0 = JOBS + 8 + 8 * stage
                if kind == "up":
                    with dve.Fori(0, 4) as i:
                        squares(i, n0, chunk)
                elif chunk < 3:
                    with dve.Fori(0, 4) as i:
                        residuals(i, n0, "first" if chunk == 0 else "more", "down_out")
                else:
                    with dve.Fori(0, 3) as i:
                        residuals(i, n0, "more", "down_out")
                    residuals(3, n0, "more", "down_out", skip_last=True)
            dve.wait_ge(sem("ln2_in"), 32)
            for t in range(TT + 2):
                if t < TT:
                    if t >= 3:
                        dve.wait_ge(sem("ln2_norm"), t - 2)
                    token_variance(t, "ln2")
                if 1 <= t <= TT:
                    token_scale(t - 1, "ln2")
                if t >= 2:
                    dve.wait_ge(sem("ln2_norm"), t - 1)
                    dve.tensor_tensor(xn2[t - 2], xn2[t - 2], ln2gb[:, 0:DM], ALU.mult).then_inc(sem("gain_out"), 1)
            dve.wait_ge(sem("gain_out"), TT)
            dve.tensor_tensor(xn2[TT - 1], xn2[TT - 1], ln2gb[:, DM:], ALU.add).then_inc(sem("gain_out"), 1)

        @block.scalar
        def _(act):
            steps = [0]

            def then_wait(ins):
                steps[0] += 1
                ins.then_inc(sem("act_step"), 1)
                act.wait_ge(sem("act_step"), steps[0])

            def first_high(i, s, first=False):
                act.wait_ge(sem(f"wa{s}_in"), 16 * (i + 1))
                if not first:
                    act.wait_ge(sem("h_mm"), 2 * i + (s - 1))
                act.copy(wa[s][0], ring[:, s * 1024:(s + 1) * 1024]).then_inc(sem("wa_high"), 1)

            for k in range(KT):
                if k % 2 == 0:
                    act.wait_ge(sem(f"x{k // 2}_in"), 16)
                act.copy(xa[0][:, k], x3[:, k]).then_inc(sem("xa_high"), 1)
                if k in (1, 3):
                    first_high(0, k // 2, first=True)
            def read_tile(i, dst, split):
                act.wait_ge(sem("h_mm"), 2 * i + 2)
                for d, b in halves_of(dst, 2, split):
                    last = act.copy(d, b)
                last.then_inc(sem("h_out_a"), 1)

            def silu(i, s):
                act.wait_ge(sem("conv_out"), 2 * i + (s + 1))
                row = cols(arena[:, Q0:Q0 + 12 * TOK], 2 * i + s)
                act.activation(row[:, 0:NP], conv_acc[s][:, 0:NP], ACT.Silu)
                act.activation(stream(row), conv_acc_streams[s], ACT.Silu).then_inc(sem("silu_out"), 1)

            def odd_tile(i, dst, split, weights=True, silus=True):
                if weights:
                    first_high(i + 1, 0)
                if silus:
                    silu(i - 1, 0)
                read_tile(i, dst, split)
                if weights:
                    first_high(i + 1, 1)
                if silus:
                    silu(i - 1, 1)

            pad_flat = arena[:, P0:P0 + 12 * QW]
            odd_tile(0, cols(pad_flat, 1, QW), True, silus=False)
            with act.Fori(1, 6) as i:
                odd_tile(i, cols(pad_flat, 2 * i + 1, QW), True)
            odd_tile(6, h3[:, 1, :], False, weights=NPRE > 14)
            for i in range(7, NPRE // 2):
                odd_tile(i, h3[:, 2 * (i - 6) + 1, :], False, weights=i + 1 < NPRE // 2, silus=False)

            read = [0]

            def read_fills(stage, n):
                while read[0] < NFILL + 2 and FILL_END[read[0]] <= ROUND[stage, n]:
                    if read[0] >= NFILL:
                        half = read[0] - NFILL
                        read[0] += 1
                        act.wait_ge(sem("mem_mm"), KT * (half + 1))
                        for st in range(2):
                            act.copy(mkv[:, st, 512 * half:512 * half + 512], ps[6 + st][:, :]
                                     ).then_inc(sem("mkv_out"), 1)
                        continue
                    row = h3[:, NPRE - 12 + read[0], :]
                    read[0] += 1
                    act.wait_ge(sem("fill_mm"), read[0])
                    act.copy(row[:, 0:NP], ps[6][:, :])
                    act.copy(row[:, NP:TOK], ps[7][:, 0:P]).then_inc(sem("fill_out"), 1)

            def lengths(stage, n, to, used):
                if n >= 2:
                    act.wait_ge(sem(used), n - 1)
                for j, c in enumerate((slice(0, NP), slice(NP, TOK))):
                    read_fills(stage, 2 * n + j)
                    act.wait_ge(sem(f"{stage}_mm"), 2 * n + j + 1)
                    b = ps[ROUND[stage, 2 * n + j] % DN_BANKS][:, 0:c.stop - c.start]
                    act.activation(to[n % 2][:, c], b, ACT.Sqrt, bias=eps[:, 0:1]).then_inc(sem(f"{stage}_out"), 1)

            act.wait_ge(sem("par_in"), 16 * 8)
            act.activation(nea, alog, ACT.Exp)
            act.wait_ge(sem("ab_out"), 1)
            act.activation(e_b, ab[:, :, 4:8], ACT.Exp, scale=-1.0)
            then_wait(act.activation(t_b, t_b, ACT.Exp, scale=-1.0))
            act.activation(t_c, t_b, ACT.Ln, bias=1.0).then_inc(sem("ln_out"), 1)

            act.wait_ge(sem("silu_out"), 8)
            for n in range(8):
                if n >= 2:
                    act.wait_ge(sem("norm_mm"), 2 * n - 2)
                act.activation(sq[n % 2], qkv3[:, n, :], ACT.Square).then_inc(sem("sq_out"), 1)
                if n >= 1:
                    lengths("norm", n - 1, rn, "qk_norm")
            lengths("norm", 7, rn, "qk_norm")
            read_fills("gcol", 0)
            act.wait_ge(sem("gcol_out"), 1)
            act.activation(kdec, glc, ACT.Exp).then_inc(sem("ecol_out"), 1)
            act.activation(nbeg, gcl[:, :, 0:4], ACT.Exp).then_inc(sem("ecol_out"), 1)
            act.wait_ge(sem("norm_mm"), 16)
            for t in range(TT):
                read_fills("grow", t)
                act.wait_ge(sem("dmin_out"), t + 1)
                if t >= 2:
                    act.wait_ge(sem("qe_out"), t - 1)
                act.activation(eg_sb[t % 2], heads(ps[ROUND["grow", t] % DN_BANKS][:, :]), ACT.Exp
                               ).then_inc(sem("grow_out"), 1)
                act.activation(DEC[:, t], d_sb[t % 2], ACT.Exp).then_inc(sem("dec_out"), 1)

            def keep(stage, t, dst):
                read_fills(stage, t)
                act.wait_ge(sem(f"{stage}_mm"), t + 1)
                act.copy(dst, heads(ps[ROUND[stage, t] % DN_BANKS][:, :])).then_inc(sem(f"{stage}_out"), 1)

            for t in range(TT):
                keep("ntr", t, PW[:, t])
            for level in (1, 2, 3):
                for t in range(TT):
                    if level == 1:
                        act.wait_ge(sem("x0_out"), t + 1)
                    keep("p", level_count("p", level, t), PW[:, t])
                if level < 3:
                    for t in range(TT):
                        keep("pt", level_count("pt", level, t), PWT[:, t])
            for level in (4, 5, 6):
                for t in range(TT - 1):
                    keep("y", level_count("y", level, t), PW[:, t])
            assert read[0] >= 16 - NPRE
            act.wait_ge(sem("h_out_v"), NPRE // 2)
            act.wait_ge(sem("h_out_a"), NPRE // 2)
            act.wait_ge(sem("fill_out"), max(16 - NPRE, 1))
            act.activation(h3[:, 0:4, :], h3[:, 0:4, :], ACT.Silu).then_inc(sem("z_out"), 1)
            def piece_high(n):
                act.wait_ge(sem(f"piece{n % 2}_in"), 16 * (n // 2 + 1))
                if n >= 2:
                    act.wait_ge(sem("piece_mm"), n - 1)
                act.copy(piece_parts[n % 2][0], piece_raw[n % 2]).then_inc(sem("piece_high"), 1)

            def x_high(k):
                act.copy(xp[0][:, k], x3[:, k]).then_inc(sem("xo_high"), 1)

            for stage, t in SCAN:
                n = scan_count(stage, t)
                if stage == "kst":
                    keep("kst", 0, kst_sb)
                if stage == "vn":
                    keep("vn", n, vn_streams if t == 4 else vn_sb)
                    if t == 3:
                        x_high(0)
                        x_high(1)
                if stage == "go":
                    read_fills("go", n)
                    act.wait_ge(sem("go_mm"), n + 1)
                    b = ps[ROUND["go", n] % DN_BANKS]
                    if n >= 2:
                        act.wait_ge(sem("on_mm"), n - 1)
                    act.activation(sq_o[n % 2], b[:, :], ACT.Square).then_inc(sem("osq_out"), 1)
                    act.copy(oG[:, :, t * P:(t + 1) * P], heads(b[:, :])).then_inc(sem("go_out"), 1)
                    if n < 4:
                        x_high(4 + n)
                    else:
                        x_high(2)
                        x_high(3)
                if stage == "on":
                    read_fills("on", n)
                    act.wait_ge(sem("on_mm"), n + 1)
                    if n >= 2:
                        act.wait_ge(sem("og_out"), n - 1)
                    act.activation(rn_o[n % 2], ps[ROUND["on", n] % DN_BANKS][:, :], ACT.Sqrt, bias=eps[:, 0:1]
                                   ).then_inc(sem("on_out"), 1)
            act.wait_ge(sem("og_out"), 4)
            piece_high(0)
            act.wait_ge(sem("gdn_end"), 1)
            act.copy(op[0][0], oG).then_inc(sem("xo_high"), 1)

            def high_part(n, slot, arrived, width=8 * P, first=False):
                act.wait_ge(sem(f"raw{slot}_in"), 16 * arrived)
                if not first:
                    act.wait_ge(sem("tile_mm"), n - 1)
                act.copy(w_high[slot][:, 0:width], raw[slot][:, 0:width]).then_inc(sem("high_out"), 1)

            def exponentials(n):
                kind, t, m = UNITS[n]
                i = n % 3
                act.wait_ge(sem("nm_out"), n + 1)
                window = kind in ("wp", "ws")
                if not window and n >= 3:
                    act.wait_ge(sem("pT_mm"), n - 2)
                b = sc_ps[n % 2]
                for u in range(2):
                    ins = act.activation(sm_sb[i][:, u, :], sm_sb[i][:, u, :] if window else b[:, u, :], ACT.Exp,
                                         bias=nm[i][:, u:u + 1], scale=1.0 if window else M_SCALE,
                                         accum_out=den[i][:, u:u + 1])
                if window:
                    ins = act.activation(es[i], es[i], ACT.Exp)
                ins.then_inc(sem("exp_out"), 1)

            def turned(n):
                act.wait_ge(sem("pT_mm"), n + 1)
                if n >= 2:
                    act.wait_ge(sem("pv_mm"), n - 1)
                act.copy(pT_sb[n % 2].rearrange("p u s q -> p (u s q)"), ps[4][:, :]
                         ).then_inc(sem("pT_out"), 1)

            def outputs(n):
                kind, t, m = UNITS[n]
                act.wait_ge(sem("pv_mm"), n + 1)
                b = ps[5]
                c = NP + 32 * m
                if kind == "wp":
                    ins = act.copy(oS[:, m, t * P:(t + 1) * P], b[:, 0:P])
                if kind == "mp":
                    ins = act.copy(oX[:, 2 * m:2 * m + 2, t * P:(t + 1) * P],
                                   b[:, 0:256].rearrange("p (u q) -> p u q", u=2))
                if kind == "ws":
                    ins = act.copy(oS[:, :, c:c + 32].rearrange("p m (e t) -> p m e t", e=2),
                                   b[:, 0:P].rearrange("p (e m t) -> p m e t", e=2, m=4))
                if kind == "ms":
                    ins = act.copy(oX[:, :, c:c + 32], b[:, 0:P].rearrange("p (h x) -> p h x", h=H))
                ins.then_inc(sem("at_out"), 1)

            def first_gate(c):
                act.wait_ge(sem("piece_mm"), 3 * c + 2)
                if c:
                    act.wait_ge(sem("first_out"), c)
                act.activation(gate0[:, 0:HALF], ps[6][:, 0:HALF], ACT.Sigmoid)
                act.activation(gate0[:, HALF:], ps[7][:, 0:HALF], ACT.Sigmoid).then_inc(sem("gate0_out"), 1)

            last_window = max(n for n in range(NU) if UNITS[n][0] in ("wp", "ws"))
            for n in range(NU + 3):
                if n + 1 < PIECES:
                    piece_high(n + 1)
                if n == NU - 1:
                    high_part(0, 0, 1, RAWN, first=True)
                if n < NU:
                    exponentials(n)
                if n % 3 == 1 and n < PIECES:
                    first_gate(n // 3)
                if 2 <= n <= NU + 1:
                    turned(n - 2)
                if n >= 3:
                    outputs(n - 3)
                if n == last_window + 3:
                    act.wait_ge(sem("at_out"), last_window + 1)
                    act.copy(op[1][0], oS).then_inc(sem("oh_out"), 1)

            act.wait_ge(sem("out_st"), 16 * 7)
            act.wait_ge(sem("at_out"), NU)
            act.copy(op[2][0], oX).then_inc(sem("oh_out"), 1)
            high_part(1, 1, 1, RAWN, first=True)


            def gates(i, first, width=RAWN):
                for s in range(2):
                    n = 2 * i + s
                    if not (first and s == 0):
                        high_part(n + 1, 1 - s, i + (1 + s), width if s else RAWN)
                    act.wait_ge(sem("tile_mm"), n + 1)
                    if not first:
                        act.wait_ge(sem("gated_out"), n - 1)
                    for h in range(2):
                        last = act.activation(sg[s][:, h * HALF:(h + 1) * HALF], ps[4 * s + 2 + h][:, 0:HALF],
                                              ACT.Sigmoid)
                    last.then_inc(sem("sg_out"), 1)
                act.wait_ge(sem("merged_out"), i + 1)
                act.copy(cols(mp_flat[0], i), merged_sum).then_inc(sem("mh_out"), 1)

            gates(0, True)
            with act.Fori(1, 7) as i:
                gates(i, False)
            gates(7, False, 8 * P)
            with act.Fori(0, 4) as i:
                for s in range(2):
                    high_part(2 * i + (JOBS + 1 + s), 1 - s, i + (JOBS // 2 + 1 + s))

            def deviation(t, n):
                act.wait_ge(sem("var_out"), n + 1)
                act.activation(rstd[t % 3], rstd[t % 3], ACT.Sqrt).then_inc(sem("dev_out"), 1)

            for t in range(TT + 1):
                if t < TT:
                    deviation(t, t)
                if t >= 1:
                    c = slice((t - 1) * P, t * P)
                    act.wait_ge(sem("ln1_back"), t)
                    for k in range(KT):
                        ins = act.activation(y3[:, k, c], ps[4 + 2 * ((t - 1) % 2) + k // 4][:, (k % 4) * P:(k % 4 + 1) * P],
                                             ACT.Identity, bias=ln1c[:, 8 + k:9 + k], scale=ln1c[:, k:k + 1])
                    ins.then_inc(sem("ln1_out"), 1)
                    act.wait_ge(sem("ln1_out"), t)
                    act.copy(x1[0][:, :, c], y3[:, :, c]).then_inc(sem("x1_high"), 1)

            def relus(i, n0, chunk, first=False):
                for s in range(2):
                    n, c = 2 * i + (n0 + s), 2 * i + (8 * chunk + s)
                    high_part(n + 1, 1 - s, i + (n0 // 2 + 1 + s))
                    act.wait_ge(sem("tile_mm"), n + 1)
                    if not first:
                        act.wait_ge(sem("hid_low"), c - 1)
                    act.activation(relu[s][:, 0:HALF], ps[2 * s][:, 0:HALF], ACT.Relu)
                    act.activation(relu[s][:, HALF:], ps[2 * s + 1][:, 0:HALF], ACT.Relu
                                   ).then_inc(sem("up_out"), 1)
                    act.wait_ge(sem("sqr_out"), c + 1)
                    act.copy(cols(hid_flat[chunk % 2][0], 2 * i + s), relu[s]).then_inc(sem("hid_high"), 1)

            for stage, (kind, chunk) in enumerate(FFN_ORDER):
                n0 = JOBS + 8 + 8 * stage
                if kind == "up":
                    relus(0, n0, chunk, first=chunk == 0)
                    with act.Fori(1, 4) as i:
                        relus(i, n0, chunk)
                else:
                    last = chunk == 3
                    with act.Fori(0, 3 if last else 4) as i:
                        for s in range(2):
                            high_part(2 * i + (n0 + s + 1), 1 - s, i + (n0 // 2 + 1 + s))
                    if last:
                        high_part(n0 + 7, 1, n0 // 2 + 4)
            for t in range(TT + 1):
                if t < TT:
                    deviation(t, TT + t)
                if t >= 1:
                    act.wait_ge(sem("nmr_out"), t)
                    i = (t - 1) % 3
                    for j in range(2):
                        last = act.activation(xn2[t - 1][:, 512 * j:512 * j + 512],
                                              ps[token_bank(t - 1, "ln2") + j][:, :], ACT.Identity,
                                              bias=nmr[i], scale=rstd[i])
                    last.then_inc(sem("ln2_norm"), 1)

        @block.gpsimd
        def _(pool):
            with pool.Fori(0, NPRE // 2) as i:
                for s in range(2):
                    pool.wait_ge(sem("wa_high"), 2 * i + (s + 1))
                    pool.tensor_tensor(wa[s][1], ring[:, s * 1024:(s + 1) * 1024], wa[s][0], ALU.subtract
                                       ).then_inc(sem("wa_low"), 1)
            pool.wait_ge(sem("cst_in"), 16)

            def masked(out, src, mask):
                return pool.tensor_tensor(out, src, const(mask).unsqueeze(1).to_broadcast([P, H, P]), ALU.mult)

            for t in range(TT):
                pool.wait_ge(sem("kk_out"), t + 1)
                masked(NT[:, t], NT[:, t], "nstrict_p" if t < 4 else "nstrict_s").then_inc(sem("nd_out"), 1)
                pool.wait_ge(sem("nd_out"), 2 * t + 1)
                masked(PWT[:, t], NT[:, t], "bd16").then_inc(sem("nd_out"), 1)
            for level, size in ((4, 16), (5, 32), (6, 64)):
                for t in range(TT - 1):
                    if level == 4:
                        pool.wait_ge(sem("p_mm"), level_count("p", 3, t) + 1)
                    else:
                        pool.wait_ge(sem("y_mm"), level_count("y", level - 1, t) + 1)
                    masked(PWT[:, t], NT[:, t], f"off{size}").then_inc(sem("off_out"), 1)
            def x_low(n, k):
                pool.wait_ge(sem("xo_high"), n + 1)
                pool.tensor_tensor(xp[1][:, k], x3[:, k], xp[0][:, k], ALU.subtract).then_inc(sem("xo_out"), 1)

            for n in range(2):
                x_low(n, 4 + n)
            pool.wait_ge(sem("go_mm"), scan_count("go", 4) + 1)
            for n in range(8):
                state = S0[:, n // 2, n % 2 * 4:n % 2 * 4 + 4, :]
                pool.tensor_tensor(state, state, egs[:, n // 2, n % 2 * 4:n % 2 * 4 + 4].unsqueeze(2
                                   ).to_broadcast([P, 4, P]), ALU.mult).then_inc(sem("sdec_out"), 1)
            for n in range(2, 4):
                x_low(n, 4 + n)
            pool.wait_ge(sem("fill_out"), NFILL)
            pool.wait_ge(sem("mem_mm"), 2 * KT)
            for m in range(4):
                last = pool.tensor_copy(qs_sb[:, :, m, :], stream(h3[:, W_Q + m, :]))
            last.then_inc(sem("qs_out"), 1)
            for k in range(4):
                x_low(4 + k, k)
            for n in range(PIECES):
                pool.wait_ge(sem("piece_high"), n + 1)
                pool.tensor_tensor(piece_parts[n % 2][1], piece_raw[n % 2], piece_parts[n % 2][0], ALU.subtract
                                   ).then_inc(sem("piece_low"), 1)
            pool.wait_ge(sem("oh_out"), 1)
            pool.tensor_tensor(op[1][1], oS, op[1][0], ALU.subtract).then_inc(sem("xo_out"), 1)
            for t in range(TT):
                c = slice(t * P, (t + 1) * P)
                pool.wait_ge(sem("x1_high"), t + 1)
                pool.tensor_tensor(x1[1][:, :, c], y3[:, :, c], x1[0][:, :, c], ALU.subtract
                                   ).then_inc(sem("x1_low"), 1)
            for t in range(TT - 1):
                pool.wait_ge(sem("gain_out"), t + 1)
                pool.tensor_tensor(xn2[t], xn2[t], ln2gb[:, DM:], ALU.add).then_inc(sem("final_out"), 1)


def kernel(x_prompt, x_sample, state_gdn_s, state_gdn_conv, cache_swa_k, cache_swa_v, cache_mem_k, cache_mem_v,
           mem_prompt, w_in, conv_w, a_log, dt_bias, gdn_norm_w, attn_sinks, w_mem_kv, w_branch, w_o,
           ln1_g, ln1_b, w_up, w_down, ln2_g, ln2_b):
    import concourse.bacc as bacc
    from concourse.bass_utils import run_bass_kernel_spmd

    def ktiles(a):
        return a.reshape(a.shape[0] // P, P, -1).transpose(1, 0, 2)

    def coltiles(a):
        k = a.shape[0] // P
        return a.reshape(k, P, -1, P).transpose(2, 1, 0, 3).reshape(-1, P, k * P)

    w_in, w_branch = np.asarray(w_in)[0], np.asarray(w_branch)[0]
    x = np.concatenate([np.asarray(x_prompt)[0], np.asarray(x_sample).reshape(NB * ST, DM)])
    order = [h * 64 + d for m in range(4) for h in (m, 4 + m) for d in range(64)]
    o = 1536
    w_a, w_z = w_in[:, o:o + 8], w_in[:, o + 8:o + 520]
    o += 520
    w_qs, w_ks, w_vs, w_qx, w_g = (w_in[:, o + a:o + b] for a, b in (
        (0, 512), (512, 640), (640, 768), (768, 1280), (1280, 1280 + 3 * DM)))
    gate = [coltiles(w_g[:, b * DM:(b + 1) * DM]) for b in range(3)]
    branch = [coltiles(w) for w in (w_branch[0], w_branch[1][order], w_branch[2])]
    up, down = np.asarray(w_up)[0], np.asarray(w_down)[0]
    ffn = {"up": [coltiles(up[:, c * DM:(c + 1) * DM]) for c in range(4)],
           "down": [coltiles(down[c * DM:(c + 1) * DM]) for c in range(4)]}
    ck, cv = (np.asarray(c)[0].reshape(NB, P, P) for c in (cache_swa_k, cache_swa_v))
    cmk, cmv = (np.asarray(c)[0].reshape(NB, 256, H, P) for c in (cache_mem_k, cache_mem_v))
    conv_s = np.asarray(state_gdn_conv)[0].reshape(NB, PAD, 12, P)
    arrays = {
        "xT": ktiles(x.T).reshape(P, -1),
        "memT": ktiles(np.asarray(mem_prompt)[0].T).reshape(P, -1),
        "w_h": coltiles(np.concatenate([w_in[:, :1536], w_z, w_qs[:, order], w_ks, w_vs, w_qx], axis=1)),
        "w_ab": ktiles(w_a).reshape(P, -1),
        "w_mem": np.asarray(w_mem_kv)[0].reshape(KT, P, 2, 512).transpose(2, 0, 1, 3).reshape(2 * KT, P, 512),
        "w_piece": np.concatenate([gate[0][:, :, 4 * P:], gate[0][:, :, :4 * P], branch[0]], axis=2).reshape(KT, P, 3, 4 * P
                                                                        ).transpose(0, 2, 1, 3).reshape(-1, P, 4 * P),
        "w_mix": np.stack([np.concatenate([branch[b], gate[b]], axis=2) for b in (1, 2)], 1).reshape(-1, P, 12 * P),
        "w_tiles": np.concatenate([coltiles(np.asarray(w_o)[0])] + [ffn[kind][chunk] for kind, chunk in FFN_ORDER]),
        "conv_w": np.asarray(conv_w)[0].reshape(4, 12, P).transpose(2, 1, 0).reshape(P, -1),
        "conv_s": conv_s.transpose(3, 2, 0, 1).reshape(P, -1),
        "dt_b": np.asarray(dt_bias), "a_log": np.asarray(a_log),
        "norm_w": np.asarray(gdn_norm_w).reshape(P, 1),
        "sinks": np.repeat(np.asarray(attn_sinks).reshape(8), ST).reshape(P, 1),
        "sinks_row": np.asarray(attn_sinks),
        "ln1": np.concatenate([np.asarray(a).reshape(KT, P).T for a in (ln1_g, ln1_b)], axis=1),
        "ln2": np.concatenate([np.asarray(ln2_g), np.asarray(ln2_b)]),
        "s0": np.asarray(state_gdn_s)[0].transpose(2, 1, 0, 3).reshape(P, -1),
        "ckT": ck.transpose(2, 0, 1), "cvT": cv.transpose(2, 0, 1), "cv": cv.transpose(1, 0, 2),
        "cmkT": cmk.transpose(0, 3, 2, 1).reshape(NB, P, -1),
        "cmv": cmv.reshape(NB, 2, P, 512).transpose(0, 2, 1, 3).reshape(NB, P, -1),
        "consts": shape_constants(),
    }
    outs = {"o_y": (TT, P, DM), "o_ps": (P, 512), "o_pconv": (P, 12, PAD), "o_pk": (P, P), "o_pv": (P, P),
            "o_pm": (P, 2, 1024), "o_ss": (P, H * NB * P), "o_sconv": (P, 12 * NB * PAD),
            "o_skT": (P, NB, P), "o_svT": (P, NB, P)}

    nc = bacc.Bacc("TRN2", target_bir_lowering=False, num_devices=1)
    arrays = {k: np.ascontiguousarray(v) for k, v in arrays.items()}
    args = {k: nc.dram_tensor(k, v.shape, F32, kind="ExternalInput").ap() for k, v in arrays.items()}
    args |= {k: nc.dram_tensor(k, v, F32, kind="ExternalOutput").ap() for k, v in outs.items()}
    build(nc, **args)
    r = run_bass_kernel_spmd(nc, [arrays], core_ids=[0]).results[0]

    y = r["o_y"].reshape(TOK, DM)
    pm = r["o_pm"].transpose(1, 0, 2).reshape(1, 1, 256, 2, H, P)
    s_kv = [r[k].transpose(1, 2, 0).reshape(1, NB, P, 2, 64) for k in ("o_skT", "o_svT")]
    return (y[:NP].reshape(1, NP, DM), y[NP:].reshape(NB, ST, DM),
            r["o_ps"].reshape(P, H, P).transpose(1, 0, 2).reshape(1, 1, H, P, P),
            r["o_pconv"].transpose(2, 1, 0).reshape(1, 1, PAD, 1536),
            r["o_pk"].T.reshape(1, 1, P, 2, 64), r["o_pv"].T.reshape(1, 1, P, 2, 64),
            pm[..., 0, :, :], pm[..., 1, :, :],
            r["o_ss"].reshape(P, H, NB, P).transpose(2, 1, 0, 3).reshape(1, NB, H, P, P),
            r["o_sconv"].reshape(P, 12, NB, PAD).transpose(2, 3, 1, 0).reshape(1, NB, PAD, 1536),
            s_kv[0], s_kv[1])
```
